# Optimizing a Trainium2 kernel written in Bass

```python
import math
import jax
import jax.numpy as jnp
from jax import lax
import numpy as np

D_MODEL = 1024
BATCH = 1
SEQ = 512
DEPTH = 1
DEC_BATCH = 8
DEC_SEQ = 1
PAST_LEN = 512
PAGE_SIZE = 128

EPS = 1e-6
DN_HEADS = 8
DN_DK = 128
DN_DV = 128
CONV_W = 4
CONV_DIM = 2 * DN_HEADS * DN_DK + DN_HEADS * DN_DV
DN_CHUNK = 64
NSA_HEADS = 8
NSA_KV = 2
NSA_G = NSA_HEADS // NSA_KV
NSA_DH = 128
NSA_SCALE = NSA_DH ** -0.5
NSA_BLK = 64
NSA_TOPN = 16
NSA_WINDOW = 512
NSA_CMP_HID = 128
SEL_QBLK = 32
WIN_QBLK = 128
FORCE_SCORE = 1e4
NEG_INF = -1e30
NUM_BUCKETS = 32
MAX_DISTANCE = 128
D_FF = 256 * (-(-8 * D_MODEL // (3 * 256)))
IN_SIZES = (CONV_DIM, DN_HEADS * DN_DV, DN_HEADS, DN_HEADS, NSA_HEADS * NSA_DH,
            6 * NSA_KV * NSA_DH, 3 * NSA_HEADS, 2 * D_MODEL)
IN_DIM = sum(IN_SIZES)
POOL_NUM = 5
POOL_DEN = 4

kernel_name = 'hybrid_gdn_nsa_decode_step'

def _rms(x, g):
    xf = x.astype(jnp.float32)
    y = xf * lax.rsqrt(jnp.mean(xf * xf, axis=-1, keepdims=True) + EPS)
    return (y * g.astype(jnp.float32)).astype(x.dtype)

def _l2n(x):
    xf = x.astype(jnp.float32)
    return xf * lax.rsqrt(jnp.sum(xf * xf, axis=-1, keepdims=True) + EPS)

def _split(t, sizes):
    return jnp.split(t, [int(i) for i in np.cumsum(sizes)[:-1]], axis=-1)

def _t5_bucket(dist):
    n = jnp.maximum(dist, 0)
    exact = NUM_BUCKETS // 2
    big = exact + (jnp.log(jnp.maximum(n, 1).astype(jnp.float32) / exact)
                   / math.log(MAX_DISTANCE / exact) * (NUM_BUCKETS - exact)).astype(jnp.int32)
    return jnp.where(n < exact, n, jnp.minimum(big, NUM_BUCKETS - 1))

def _gather_pages(pool, page_table):
    g = pool[page_table]
    return g.reshape((g.shape[0], g.shape[1] * g.shape[2]) + g.shape[3:])

def _gated_delta(q, k, v, g, beta, s0):
    B, T, H, _ = q.shape
    Dv = v.shape[-1]
    C = min(DN_CHUNK, T)
    n = -(-T // C)
    pad = n * C - T

    def chunks(t):
        t = jnp.pad(t, ((0, 0), (0, pad)) + ((0, 0),) * (t.ndim - 2))
        t = t.reshape((B, n, C) + t.shape[2:])
        return jnp.transpose(t, (1, 0, 3, 2) + tuple(range(4, t.ndim)))

    qc, kc, vc, bc = chunks(q), chunks(k), chunks(v), chunks(beta)
    gc = jnp.cumsum(chunks(g), axis=-1)
    idx = jnp.arange(C)
    incl = idx[:, None] >= idx[None, :]
    decay = jnp.exp(jnp.where(incl, gc[..., :, None] - gc[..., None, :], -jnp.inf))
    kb = kc * bc[..., None]
    lower = jnp.where(idx[:, None] > idx[None, :],
                      jnp.einsum('nbhcd,nbhsd->nbhcs', kb, kc) * decay, 0.0)
    rhs = jnp.concatenate([vc * bc[..., None], kb * jnp.exp(gc)[..., None]], axis=-1)
    sol = lax.linalg.triangular_solve(lower, rhs, left_side=True, lower=True, unit_diagonal=True)
    u, w = sol[..., :Dv], sol[..., Dv:]
    qk = jnp.einsum('nbhcd,nbhsd->nbhcs', qc, kc) * decay

    def step(S, xs):
        q_i, k_i, u_i, w_i, g_i, qk_i = xs
        v_new = u_i - jnp.einsum('bhcd,bhde->bhce', w_i, S)
        o_i = (jnp.einsum('bhcd,bhde->bhce', q_i * jnp.exp(g_i)[..., None], S)
               + jnp.einsum('bhcs,bhse->bhce', qk_i, v_new))
        g_last = g_i[..., -1:]
        S = S * jnp.exp(g_last)[..., None] + jnp.einsum(
            'bhcd,bhce->bhde', k_i * jnp.exp(g_last - g_i)[..., None], v_new)
        return S, o_i

    S, o = lax.scan(step, s0, (qc, kc, u, w, gc, qk))
    o = jnp.transpose(o, (1, 0, 3, 2, 4)).reshape(B, n * C, H, Dv)[:, :T]
    return o, S

def _deltanet(qkv_pre, z, b, a, conv_buf, s0, conv_w, a_log, dt_bias, onorm_g):
    B, T, _ = qkv_pre.shape
    xp = jnp.concatenate([conv_buf.astype(qkv_pre.dtype), qkv_pre], axis=1)
    conv = xp[:, 0:T] * conv_w[0]
    for i in range(1, CONV_W):
        conv = conv + xp[:, i:i + T] * conv_w[i]
    q, k, v = jnp.split(jax.nn.silu(conv), [DN_HEADS * DN_DK, 2 * DN_HEADS * DN_DK], axis=-1)
    q = _l2n(q.reshape(B, T, DN_HEADS, DN_DK)) * (DN_DK ** -0.5)
    k = _l2n(k.reshape(B, T, DN_HEADS, DN_DK))
    v = v.reshape(B, T, DN_HEADS, DN_DV).astype(jnp.float32)
    beta = jax.nn.sigmoid(b.astype(jnp.float32))
    g = -jnp.exp(a_log.astype(jnp.float32)) * jax.nn.softplus(a.astype(jnp.float32) + dt_bias.astype(jnp.float32))
    o, s = _gated_delta(q, k, v, g, beta, s0.astype(jnp.float32))
    zr = z.reshape(B, T, DN_HEADS, DN_DV).astype(jnp.float32)
    o = o * lax.rsqrt(jnp.mean(o * o, axis=-1, keepdims=True) + EPS) * onorm_g.astype(jnp.float32) * jax.nn.silu(zr)
    return o.reshape(B, T, DN_HEADS * DN_DV).astype(qkv_pre.dtype), xp[:, T:], s.astype(qkv_pre.dtype)

def _cmp_branch(q, q_pos, cmp_full, pe, w1, w2, rel):
    B, L = cmp_full.shape[:2]
    n = L // NSA_BLK
    blocks = cmp_full[:, :n * NSA_BLK].reshape(B, n, NSA_BLK, 2, NSA_KV, NSA_DH) + pe[:, :, None, :].astype(q.dtype)
    hid = jax.nn.silu(jnp.einsum('bnlckd,cldf->bnckf', blocks, w1))
    kvc = jnp.einsum('bnckf,cfd->bnckd', hid, w2)
    end = jnp.arange(n) * NSA_BLK + (NSA_BLK - 1)
    dist = q_pos[:, None] - end[None, :]
    valid = dist >= 0
    bias = jnp.transpose(rel[_t5_bucket(dist)].astype(jnp.float32).reshape(dist.shape + (NSA_KV, NSA_G)), (2, 3, 0, 1))
    logits = jnp.einsum('btkgd,bnkd->bkgtn', q, kvc[:, :, 0], preferred_element_type=jnp.float32) * NSA_SCALE + bias
    p = jax.nn.softmax(jnp.where(valid, logits, NEG_INF), axis=-1) * valid
    o = jnp.einsum('bkgtn,bnkd->btkgd', p.astype(q.dtype), kvc[:, :, 1])
    return o, p.sum(axis=2)

def _select(imp, q_pos, n_blocks):
    imp = jnp.pad(imp, ((0, 0), (0, 0), (0, 0), (0, n_blocks - imp.shape[-1])))
    j = jnp.arange(n_blocks)[None, :]
    cur = (q_pos // NSA_BLK)[:, None]
    forced = (j == 0) | (j == cur) | (j == cur - 1)
    score = jnp.where(j <= cur, jnp.where(forced, FORCE_SCORE, imp), -1.0)
    return lax.top_k(score, min(NSA_TOPN, n_blocks))[1]

def _sel_branch(q, q_pos, sel_idx, sel_full, rel):
    B, Tq = q.shape[:2]
    n_top = sel_idx.shape[-1]
    nblk = sel_full.shape[1] // NSA_BLK
    kvr = jnp.transpose(sel_full.reshape(B, nblk, NSA_BLK, 2, NSA_KV, NSA_DH), (0, 4, 1, 2, 3, 5))
    qb = min(SEL_QBLK, Tq)
    nq = -(-Tq // qb)
    pad = nq * qb - Tq
    qp = jnp.transpose(jnp.pad(q, ((0, 0), (0, pad), (0, 0), (0, 0), (0, 0))).reshape(
        B, nq, qb, NSA_KV, NSA_G, NSA_DH), (1, 0, 2, 3, 4, 5))
    ip = jnp.transpose(jnp.pad(sel_idx, ((0, 0), (0, 0), (0, pad), (0, 0)), mode='edge').reshape(
        B, NSA_KV, nq, qb, n_top), (2, 0, 1, 3, 4))
    pp = jnp.pad(q_pos, (0, pad), mode='edge').reshape(nq, qb)
    rel_kv = jnp.transpose(rel.reshape(NUM_BUCKETS, NSA_KV, NSA_G), (1, 0, 2)).astype(jnp.float32)
    kv_ix = jnp.arange(NSA_KV)[None, :, None, None]

    def one(args):
        qi, ii, pi = args
        gath = jnp.take_along_axis(kvr, ii.reshape(B, NSA_KV, qb * n_top)[..., None, None, None], axis=2)
        gath = gath.reshape(B, NSA_KV, qb, n_top * NSA_BLK, 2, NSA_DH)
        tok = (ii[..., None] * NSA_BLK + jnp.arange(NSA_BLK)).reshape(B, NSA_KV, qb, n_top * NSA_BLK)
        dist = pi[None, None, :, None] - tok
        bias = rel_kv[kv_ix, _t5_bucket(dist)]
        logits = jnp.einsum('bqkgd,bkqsd->bkgqs', qi, gath[..., 0, :],
                            preferred_element_type=jnp.float32) * NSA_SCALE + jnp.moveaxis(bias, -1, 2)
        p = jax.nn.softmax(jnp.where((dist >= 0)[:, :, None], logits, NEG_INF), axis=-1)
        return jnp.einsum('bkgqs,bkqsd->bqkgd', p.astype(qi.dtype), gath[..., 1, :])

    o = lax.map(one, (qp, ip, pp))
    return jnp.transpose(o, (1, 0, 2, 3, 4, 5)).reshape(B, nq * qb, NSA_KV, NSA_G, NSA_DH)[:, :Tq]

def _win_branch(qw, kvw, qpos, kpos, rel):
    dist = qpos[:, :, None] - kpos[:, None, :]
    valid = (dist >= 0) & (dist < NSA_WINDOW) & (kpos[:, None, :] >= 0)
    bias = rel[_t5_bucket(dist)].astype(jnp.float32).reshape(dist.shape + (NSA_KV, NSA_G))
    bias = jnp.transpose(bias, (0, 3, 4, 1, 2))
    logits = jnp.einsum('bnqkgd,bnskd->bnkgqs', qw, kvw[:, :, :, 0],
                        preferred_element_type=jnp.float32) * NSA_SCALE + bias
    p = jax.nn.softmax(jnp.where(valid[:, None, None], logits, NEG_INF), axis=-1)
    return jnp.einsum('bnkgqs,bnskd->bnqkgd', p.astype(qw.dtype), kvw[:, :, :, 1])

def _nsa(q, gates, kv_new, q_pos, past, pe, w1, w2, rel):
    B, T = q.shape[:2]
    cmp_new, sel_new, win_new = kv_new[:, :, 0:2], kv_new[:, :, 2:4], kv_new[:, :, 4:6]
    if past is None:
        cmp_full, sel_full = cmp_new, sel_new
        n = T // WIN_QBLK
        kvp = jnp.pad(win_new, ((0, 0), (NSA_WINDOW, 0), (0, 0), (0, 0), (0, 0)))
        kidx = (jnp.arange(n) * WIN_QBLK)[:, None] + jnp.arange(NSA_WINDOW + WIN_QBLK)[None, :]
        kvw = kvp[:, kidx]
        kpos = kidx - NSA_WINDOW
        qw = q.reshape(B, n, WIN_QBLK, NSA_KV, NSA_G, NSA_DH)
        qpos_w = q_pos.reshape(n, WIN_QBLK)
        win_state = win_new[:, T - min(NSA_WINDOW, T):]
    else:
        cmp_past, sel_past, win_buf = past
        cmp_full = jnp.concatenate([cmp_past.astype(q.dtype), cmp_new], axis=1)
        sel_full = jnp.concatenate([sel_past.astype(q.dtype), sel_new], axis=1)
        wb = win_buf.shape[1]
        win_cat = jnp.concatenate([win_buf.astype(q.dtype), win_new], axis=1)
        kvw = win_cat[:, None]
        kpos = (q_pos[0] - wb + jnp.arange(wb + T))[None]
        qw = q[:, None]
        qpos_w = q_pos[None]
        win_state = win_cat[:, T:]
    L = sel_full.shape[1]
    n_blocks = -(-L // NSA_BLK)
    sel_full = jnp.pad(sel_full, ((0, 0), (0, n_blocks * NSA_BLK - L), (0, 0), (0, 0), (0, 0)))
    o_cmp, imp = _cmp_branch(q, q_pos, cmp_full, pe, w1, w2, rel)
    o_sel = _sel_branch(q, q_pos, _select(imp, q_pos, n_blocks), sel_full, rel)
    o_win = _win_branch(qw, kvw, qpos_w, kpos, rel).reshape(B, T, NSA_KV, NSA_G, NSA_DH)
    gt = jax.nn.sigmoid(gates).reshape(B, T, 3, NSA_KV, NSA_G, 1)
    o = gt[:, :, 0] * o_cmp + gt[:, :, 1] * o_sel + gt[:, :, 2] * o_win
    return o.reshape(B, T, NSA_HEADS * NSA_DH), win_state

def _layer(x, c, q_pos, past, P, rel):
    B, T, _ = x.shape
    mod = jnp.einsum('bd,de->be', jax.nn.silu(c), P['w_ada']) + P['b_ada']
    sh1, sc1, gt1, sh2, sc2, gt2 = [m[:, None, :] for m in jnp.split(mod, 6, axis=-1)]
    h = _rms(x, P['norm_g'][0]) * (1.0 + sc1) + sh1
    qkv_pre, z, b, a, q_nsa, kv_nsa, g_nsa, g_merge = _split(h @ P['w_in'], IN_SIZES)
    if past is None:
        conv_buf = jnp.zeros((B, CONV_W - 1, CONV_DIM), x.dtype)
        s0 = jnp.zeros((B, DN_HEADS, DN_DK, DN_DV), x.dtype)
        nsa_past = None
    else:
        conv_buf, s0, nsa_past = past[0], past[1], past[2:]
    o_a, conv_new, s_new = _deltanet(qkv_pre, z, b, a, conv_buf, s0, P['conv_w'], P['a_log'],
                                     P['dt_bias'], P['onorm_g'])
    kv_nsa = kv_nsa.reshape(B, T, 6, NSA_KV, NSA_DH)
    o_b, win_new = _nsa(q_nsa.reshape(B, T, NSA_KV, NSA_G, NSA_DH), g_nsa, kv_nsa, q_pos, nsa_past,
                        P['cmp_pe'], P['cmp_w1'], P['cmp_w2'], rel)
    gate_a, gate_b = jnp.split(jax.nn.sigmoid(g_merge), 2, axis=-1)
    mixed = (gate_a * (o_a @ P['w_oa']) + gate_b * (o_b @ P['w_ob'])) @ P['w_out']
    x = x + gt1 * _rms(mixed, P['norm_g'][1])
    h = _rms(x, P['norm_g'][2]) * (1.0 + sc2) + sh2
    gate, up = jnp.split(h @ P['w_gu'], 2, axis=-1)
    x = x + gt2 * _rms((jax.nn.silu(gate) * up) @ P['w_down'], P['norm_g'][3])
    return x, (kv_nsa[:, :, 0:2], kv_nsa[:, :, 2:4], win_new, s_new, conv_new)

def setup_inputs(seed: int = 0) -> dict:
    key = jax.random.key(seed)
    ks = jax.random.split(key, 28)
    f32 = jnp.float32

    def nrm(k, shape, scale):
        return jax.random.normal(k, shape, f32) * scale

    n_pages = PAST_LEN // PAGE_SIZE
    n_pool = (DEC_BATCH * n_pages * POOL_NUM) // POOL_DEN
    w_buf = min(NSA_WINDOW, PAST_LEN)
    page_table = jax.random.permutation(ks[0], n_pool)[:DEC_BATCH * n_pages].reshape(
        DEC_BATCH, n_pages).astype(jnp.int32)
    return {
        'x_prompt': nrm(ks[1], (BATCH, SEQ, D_MODEL), 1.0),
        'x_sample': nrm(ks[2], (DEC_BATCH, DEC_SEQ, D_MODEL), 1.0),
        'cache_cmp_kv': nrm(ks[3], (DEPTH, n_pool, PAGE_SIZE, 2, NSA_KV, NSA_DH), 1.0),
        'cache_sel_kv': nrm(ks[4], (DEPTH, n_pool, PAGE_SIZE, 2, NSA_KV, NSA_DH), 1.0),
        'cache_win_kv': nrm(ks[5], (DEPTH, DEC_BATCH, w_buf, 2, NSA_KV, NSA_DH), 1.0),
        'state_delta': nrm(ks[6], (DEPTH, DEC_BATCH, DN_HEADS, DN_DK, DN_DV), 0.5),
        'state_conv': nrm(ks[7], (DEPTH, DEC_BATCH, CONV_W - 1, CONV_DIM), 1.0),
        'page_table': page_table,
        'c_prompt': nrm(ks[8], (BATCH, D_MODEL), 1.0),
        'c_sample': nrm(ks[9], (DEC_BATCH, D_MODEL), 1.0),
        'w_ada': nrm(ks[10], (DEPTH, D_MODEL, 6 * D_MODEL), 0.5 * D_MODEL ** -0.5),
        'b_ada': nrm(ks[11], (DEPTH, 6 * D_MODEL), 0.02),
        'norm_g': 1.0 + nrm(ks[12], (DEPTH, 4, D_MODEL), 0.05),
        'w_in': nrm(ks[13], (DEPTH, D_MODEL, IN_DIM), D_MODEL ** -0.5),
        'conv_w': nrm(ks[14], (DEPTH, CONV_W, CONV_DIM), CONV_W ** -0.5),
        'a_log': jnp.log(jax.random.uniform(ks[15], (DEPTH, DN_HEADS), f32, 1.0, 16.0)),
        'dt_bias': nrm(ks[16], (DEPTH, DN_HEADS), 0.1),
        'onorm_g': 1.0 + nrm(ks[17], (DEPTH, DN_DV), 0.05),
        'w_oa': nrm(ks[18], (DEPTH, DN_HEADS * DN_DV, D_MODEL), (DN_HEADS * DN_DV) ** -0.5),
        'w_ob': nrm(ks[19], (DEPTH, NSA_HEADS * NSA_DH, D_MODEL), (NSA_HEADS * NSA_DH) ** -0.5),
        'w_out': nrm(ks[20], (DEPTH, D_MODEL, D_MODEL), D_MODEL ** -0.5),
        'cmp_pe': nrm(ks[21], (DEPTH, NSA_BLK, 2, NSA_DH), 0.1),
        'cmp_w1': nrm(ks[22], (DEPTH, 2, NSA_BLK, NSA_DH, NSA_CMP_HID), (NSA_BLK * NSA_DH) ** -0.5),
        'cmp_w2': nrm(ks[23], (DEPTH, 2, NSA_CMP_HID, NSA_DH), NSA_CMP_HID ** -0.5),
        'rel_bias': nrm(ks[24], (NUM_BUCKETS, NSA_HEADS), 0.3),
        'w_gu': nrm(ks[25], (DEPTH, D_MODEL, 2 * D_FF), D_MODEL ** -0.5),
        'w_down': nrm(ks[26], (DEPTH, D_FF, D_MODEL), D_FF ** -0.5),
    }

def reference(x_prompt, x_sample, cache_cmp_kv, cache_sel_kv, cache_win_kv, state_delta, state_conv,
              page_table, c_prompt, c_sample, w_ada, b_ada, norm_g, w_in, conv_w, a_log, dt_bias,
              onorm_g, w_oa, w_ob, w_out, cmp_pe, cmp_w1, cmp_w2, rel_bias, w_gu, w_down):
    past_len = page_table.shape[1] * cache_cmp_kv.shape[2]
    pos_p = jnp.arange(x_prompt.shape[1])
    pos_s = past_len + jnp.arange(x_sample.shape[1])
    yp, ys = x_prompt, x_sample
    p_st, s_st = [], []
    for l in range(DEPTH):
        P = {'w_ada': w_ada[l], 'b_ada': b_ada[l], 'norm_g': norm_g[l], 'w_in': w_in[l],
             'conv_w': conv_w[l], 'a_log': a_log[l], 'dt_bias': dt_bias[l], 'onorm_g': onorm_g[l],
             'w_oa': w_oa[l], 'w_ob': w_ob[l], 'w_out': w_out[l], 'cmp_pe': cmp_pe[l],
             'cmp_w1': cmp_w1[l], 'cmp_w2': cmp_w2[l], 'w_gu': w_gu[l], 'w_down': w_down[l]}
        yp, st = _layer(yp, c_prompt, pos_p, None, P, rel_bias)
        p_st.append(st)
        past = (state_conv[l], state_delta[l], _gather_pages(cache_cmp_kv[l], page_table),
                _gather_pages(cache_sel_kv[l], page_table), cache_win_kv[l])
        ys, st = _layer(ys, c_sample, pos_s, past, P, rel_bias)
        s_st.append(st)

    def stk(states, i):
        return jnp.stack([s[i] for s in states])

    return (yp, ys, stk(p_st, 0), stk(p_st, 1), stk(p_st, 2), stk(p_st, 3), stk(p_st, 4),
            stk(s_st, 0), stk(s_st, 1), stk(s_st, 2), stk(s_st, 3), stk(s_st, 4))


_drawn_inputs = setup_inputs


def setup_inputs(seed=0):
    import zlib

    import numpy as np

    out = dict(_drawn_inputs(seed))
    spreads = {}
    factors = {'onorm_g': 19.833,
     'cmp_pe': 16.607,
     'rel_bias': 10.445,
     'cache_cmp_kv': 3.113,
     'cache_sel_kv': 8.0}
    for name, (base, spread) in spreads.items():
        noise = np.random.default_rng([zlib.crc32(name.encode()), seed]).standard_normal(out[name].shape)
        drawn = base * np.exp(spread * noise) if base else spread * noise
        out[name] = jnp.asarray(drawn.astype(out[name].dtype))
    for name, factor in factors.items():
        out[name] = (out[name] * factor).astype(out[name].dtype)
    return out
```

```python
from contextlib import ExitStack

import concourse.bass as bass
from concourse import mybir

F32 = mybir.dt.float32
I32 = mybir.dt.int32
ALU = mybir.AluOpType
ACT = mybir.ActivationFunctionType
AX = mybir.AxisListType

P = 128
D = 1024
KD = D // P
TP = 512
NB = 8
T = TP + NB
HALF = T // 2
NCH = TP // P
H = 8
KV = 2
G = H // KV
NR = NB * H
CONV_W = 4
CONV_T = 24
BLK = 64
NBLK = TP // BLK
PAGE = 128
NPAGE = 4
FF = 2816
KF = FF // P
EPS = 1e-6
SCALE = P ** -0.5
MASKED = -1e30
NMOD = 1 + NB
ROWS = NB * KV * NBLK + KV * NBLK
LEVELS = (2, 4, 8, 16, 32, 64)

C_Z = 3072
C_B = 4096
C_Q = C_B + 2 * H
C_KV = C_Q + H * P
C_G = C_KV + 6 * KV * P
C_M = C_G + 3 * H

K_ID, K_LE, K_GT, K_LT, K_NEG1 = 0, P, 2 * P, 3 * P, 4 * P
K_LEV = 5 * P
K_ONE = K_LEV + len(LEVELS) * P
K_E8 = K_ONE + P
K_HM = K_E8 + NR
K_KVM = K_HM + H
K_X = K_KVM + KV
K_RV = K_X + P
K_MH = K_RV + 1
K_J = K_MH + 1
K_COLS = K_J + P
B_R, B_S = 0, 384
B_CP = B_S + TP + 2
B_CS = B_CP + NCH * NBLK * P
B_COLS = B_CS + P
NBK = 33


def split_halves(ap):
    return ap.rearrange("p (a n) -> p a n", a=2)


def over(ap, n):
    if len(ap.shape) == 2:
        ap = ap.unsqueeze(2)
    return ap.broadcast_to([ap.shape[0], ap.shape[1], n])


def each(ap, n):
    return ap.unsqueeze(1).broadcast_to([ap.shape[0], n, ap.shape[1]])


class Phase:

    def __init__(self, nc, name):
        self.nc, self.name, self.ctx, self.sems = nc, name, ExitStack(), []

    def __enter__(self):
        return self

    def __exit__(self, *e):
        done = self.ctx.__exit__(*e)
        for s in self.sems:
            self.nc.sync.sem_clear(s)
        return done

    def sb(self, name, shape, dt=F32):
        return self.ctx.enter_context(self.nc.sbuf_tensor(f"{self.name}_{name}", shape, dt))

    def ps(self, name, shape, dt=F32):
        return self.ctx.enter_context(self.nc.psum_tensor(f"{self.name}_{name}", shape, dt))

    def sem(self, name):
        self.sems.append(self.ctx.enter_context(self.nc.semaphore(f"{self.name}_{name}")))
        return self.sems[-1]

    def block(self):
        return self.ctx.enter_context(self.nc.Block())


def gemm(nc, name, ring, src, rhs, iters, act=None, dve=None, cols=((0, HALF), (HALF, HALF)), per=1):
    with Phase(nc, name) as ph:
        ps = ph.ps("ps", [P, 2, 2, 512])
        loaded = [ph.sem(f"loaded{b}") for b in range(2)]
        done = [ph.sem(f"done{j}") for j in range(2)]
        free = [ph.sem(f"free{j}") for j in range(2)]
        block = ph.block()

        @block.sync
        def _(sp):
            for b in range(2):
                for dst, s in src(ring[:, b], 0, b):
                    sp.dma_start(dst, s).then_inc(loaded[b], 16)
            with sp.Fori(1, iters) as t:
                for b in range(2):
                    sp.wait_ge(done[1], 2 * t + b - 1)
                    for dst, s in src(ring[:, b], t, b):
                        sp.dma_start(dst, s).then_inc(loaded[b], 16)

        @block.tensor
        def _(pe):
            with pe.Fori(0, iters) as t:
                for b in range(2):
                    pe.wait_ge(loaded[b], 16 * per * t + 16 * per)
                    for j in range(2):
                        pe.wait_ge(free[j], 2 * t + b)
                        for k in range(KD):
                            for c, (c0, n) in enumerate(cols):
                                last = pe.matmul(ps[:, j, c, 0:n], ring[:, b, k, j * P:(j + 1) * P],
                                                 rhs[:, k, c0:c0 + n], start=(k == 0), stop=(k == KD - 1))
                        last.then_inc(done[j], 1)

        def view(j):
            return ps[:, j, :, 0:HALF] if len(cols) == 2 else ps[:, j, 0, 0:cols[0][1]]

        if act:
            @block.scalar
            def _(eng):
                with eng.Fori(0, iters) as t:
                    for b in range(2):
                        act(eng, t, b, done, free, view)
        if dve:
            @block.vector
            def _(eng):
                with eng.Fori(0, iters) as t:
                    for b in range(2):
                        dve(eng, t, b, done, free, view)


def columns(w, base, step=4 * P):
    def src(slot, t, b):
        c = base + t * 512 + b * 256
        return [(slot[:, 0:KD, :], w[:, bass.ds(c, 256)].rearrange("(k p) m -> p k m", p=P))]
    return src


def rms_modulate(nc, name, src, dst, s, sh, consts, extra=None):
    with Phase(nc, name) as ph:
        sq = ph.sb("sq", [P, KD, T])
        rbc = ph.sb("rbc", [P, T])
        ps = ph.ps("ps", [P, 2, 512])
        squared, summed, rooted, normed, scaled, part = (
            ph.sem(n) for n in ("squared", "summed", "rooted", "normed", "scaled", "part"))
        block = ph.block()

        @block.scalar
        def _(act):
            for k in range(KD):
                act.activation(sq[:, k, :], src[:, k, :], ACT.Square).then_inc(squared, 1)
            act.wait_ge(part, 1)
            act.activation(rbc[:], rbc[:], ACT.Sqrt).then_inc(rooted, 1)

        @block.tensor
        def _(pe):
            for k in range(KD):
                pe.wait_ge(squared, k + 1)
                for c in range(2):
                    last = pe.matmul(ps[:, c, 0:HALF], consts[:, K_ONE:K_ONE + P],
                                     sq[:, k, c * HALF:(c + 1) * HALF], start=(k == 0), stop=(k == KD - 1))
            last.then_inc(summed, 1)

        @block.vector
        def _(v):
            v.wait_ge(summed, 1)
            v.tensor_scalar(split_halves(rbc[:]), ps[:, :, 0:HALF], 1.0 / D, EPS, ALU.mult, ALU.add).then_inc(part, 1)
            v.wait_ge(rooted, 1)
            v.reciprocal(rbc[:], rbc[:]).then_inc(part, 1)
            v.wait_ge(part, 2)
            for k in range(KD):
                v.tensor_tensor(dst[:, k, :], src[:, k, :], rbc[:], ALU.mult).then_inc(normed, 1)
            for k in range(KD):
                v.wait_ge(normed, k + 1)
                v.tensor_scalar(dst[:, k, 0:TP], dst[:, k, 0:TP], s[:, k, 0:1],
                                sh[:, k, 0:1] if sh is not None else None, ALU.mult,
                                *([ALU.add] if sh is not None else [])).then_inc(scaled, 1)
            v.wait_ge(normed, KD)
            v.tensor_tensor(dst[:, :, TP:T], dst[:, :, TP:T], s[:, :, 1:NMOD], ALU.mult).then_inc(part, 1)
            if sh is not None:
                v.wait_ge(part, 3)
                v.tensor_tensor(dst[:, :, TP:T], dst[:, :, TP:T], sh[:, :, 1:NMOD], ALU.add).then_inc(scaled, 1)
            if extra is not None:
                v.wait_ge(scaled, KD)
                v.wait_ge(part, 3)
                extra(v)


def prepare(nc, io, st):
    consts, xT, cT, par, taps = st["consts"], st["xT"], st["cT"], st["par"], st["taps"]
    with Phase(nc, "prep") as ph:
        par_rows = ph.sb("par_rows", [81, P])
        tap_rows = ph.sb("tap_rows", [CONV_W * CONV_T, P])
        x_rows = ph.sb("x_rows", [P, NCH, D])
        s_rows = ph.sb("s_rows", [NB, D])
        c_rows = ph.sb("c_rows", [NMOD, D])
        st_rows = ph.sb("st_rows", [NB * 3, CONV_T * P])
        ps = ph.ps("ps", [P, 8, 512])
        const_in, rows_in, c_in, x_in, conv_in, c_silu, turned, copied = (
            ph.sem(n) for n in ("const_in", "rows_in", "c_in", "x_in", "conv_in", "c_silu", "turned", "copied"))
        block = ph.block()
        ident = consts[:, K_ID:K_ID + P]

        @block.sync
        def _(sp):
            sp.dma_start(consts[:], io["consts"]).then_inc(const_in, 16)
            sp.dma_start(c_rows[0:1, :], io["c_prompt"]).then_inc(c_in, 16)
            sp.dma_start(c_rows[1:NMOD, :], io["c_sample"]).then_inc(c_in, 16)
            sp.dma_start(par_rows[0:48, :], io["b_ada"].rearrange("a (m p) -> (a m) p", p=P)).then_inc(rows_in, 16)
            sp.dma_start(par_rows[48:80, :], io["norm_g"].rearrange("a i (m p) -> (a i m) p", p=P)).then_inc(rows_in, 16)
            sp.dma_start(par_rows[80:81, :], io["onorm_g"]).then_inc(rows_in, 16)
            sp.dma_start(tap_rows[:], io["conv_w"].rearrange("a i (m p) -> (a i m) p", p=P)).then_inc(rows_in, 16)
            for i in range(NCH):
                sp.dma_start(x_rows[:, i, :], io["x_prompt"][0, i * P:(i + 1) * P, :]).then_inc(x_in, 16)
            sp.dma_start(s_rows[:], io["x_sample"].rearrange("b t d -> (b t) d")).then_inc(x_in, 16)
            sp.dma_start(st_rows[:], io["state_conv"].rearrange("a b j n -> (a b j) n")).then_inc(conv_in, 16)
            sp.dma_start(st["scal"][:, 0:H], io["a_log"].broadcast_to([P, H])).then_inc(rows_in, 16)
            sp.dma_start(st["scal"][:, H:2 * H], io["dt_bias"].broadcast_to([P, H])).then_inc(rows_in, 16)

        @block.scalar
        def _(act):
            act.wait_ge(c_in, 32)
            act.activation(c_rows[:], c_rows[:], ACT.Silu).then_inc(c_silu, 1)

        @block.tensor
        def _(pe):
            pe.wait_ge(const_in, 16)
            pe.wait_ge(c_silu, 1)
            for k in range(KD):
                last = pe.transpose(ps[:, 0, k * NMOD:(k + 1) * NMOD], c_rows[:, k * P:(k + 1) * P],
                                    consts[0:NMOD, K_ID:K_ID + NMOD])
            last.then_inc(turned, 1)
            pe.wait_ge(rows_in, 96)
            pe.transpose(ps[:, 1, 0:81], par_rows[:], consts[0:81, K_ID:K_ID + 81])
            pe.transpose(ps[:, 1, 128:224], tap_rows[:], consts[0:96, K_ID:K_ID + 96]).then_inc(turned, 1)
            pe.wait_ge(x_in, 80)
            for k in range(KD):
                if k >= 6:
                    pe.wait_ge(copied, k - 3)
                for i in range(NCH):
                    last = pe.transpose(ps[:, 2 + k % 6, i * P:(i + 1) * P], x_rows[:, i, k * P:(k + 1) * P], ident)
                last.then_inc(turned, 1)
            pe.wait_ge(copied, 2)
            for k in range(KD):
                last = pe.transpose(ps[:, 0, k * NB:(k + 1) * NB], s_rows[:, k * P:(k + 1) * P],
                                    consts[0:NB, K_ID:K_ID + NB])
            last.then_inc(turned, 1)
            pe.wait_ge(conv_in, 16)
            pe.wait_ge(copied, 9)
            for c in range(CONV_T):
                bank, at = (1, c * 24) if c < 12 else (2, (c - 12) * 24)
                last = pe.transpose(ps[:, bank, at:at + 24], st_rows[:, c * P:(c + 1) * P],
                                    consts[0:24, K_ID:K_ID + 24])
            last.then_inc(turned, 1)

        @block.vector
        def _(v):
            v.wait_ge(turned, 1)
            v.tensor_copy(cT[:], ps[:, 0, 0:KD * NMOD].rearrange("p (k n) -> p k n", n=NMOD)).then_inc(copied, 1)
            v.wait_ge(turned, 2)
            v.tensor_copy(par[:], ps[:, 1, 0:81])
            v.tensor_copy(taps[:], ps[:, 1, 128:224]).then_inc(copied, 1)
            for k in range(KD):
                v.wait_ge(turned, 3 + k)
                v.tensor_copy(xT[:, k, 0:TP], ps[:, 2 + k % 6, :]).then_inc(copied, 1)
            v.wait_ge(turned, 3 + KD)
            v.tensor_copy(xT[:, :, TP:T], ps[:, 0, 0:KD * NB].rearrange("p (k n) -> p k n", n=NB)).then_inc(copied, 1)
            v.wait_ge(turned, 4 + KD)
            for g in range(2):
                v.tensor_copy(st["stT"][:, g * 12:(g + 1) * 12], ps[:, 1 + g, 0:288].rearrange(
                    "p (c n) -> p c n", n=24)).then_inc(copied, 1)


def modulation(nc, io, st):
    mod, par = st["mod"], st["par"]

    def dve(v, t, b, done, free, view):
        for j in range(2):
            m = t * 4 + b * 2 + j
            v.wait_ge(done[j], 2 * t + b + 1)
            v.tensor_scalar(mod[:, bass.ds(m, 1), :].rearrange("p a n -> p (a n)"), view(j),
                            par[:, bass.ds(m, 1)], None, ALU.add).then_inc(free[j], 1)

    gemm(nc, "ada", st["ring"], columns(io["w_ada"], 0), st["cT"], 12, dve=dve, cols=((0, NMOD),))
    with Phase(nc, "fac") as ph:
        step = ph.sem("step")
        block = ph.block()

        @block.vector
        def _(v):
            for n, (row, norm) in enumerate(((1, 0), (4, 2), (2, 1), (5, 3))):
                m = mod[:, row * KD:(row + 1) * KD, :]
                if row in (1, 4):
                    v.tensor_scalar(m, m, 1.0, None, ALU.add).then_inc(step, 1)
                    v.wait_ge(step, n + 1)
                v.tensor_tensor(m, m, over(par[:, 48 + norm * KD:48 + (norm + 1) * KD], NMOD), ALU.mult)


def token_scalars(nc, io, st):
    hT, consts, scal = st["hT"], st["consts"], st["scal"]
    with Phase(nc, "tok") as ph:
        w = ph.sb("w", [P, KD, 40])
        raw = ph.sb("raw", [P, NCH + 1, 40])
        sp_a = ph.sb("sp_a", [P, NCH + 1, H])
        sp_b = ph.sb("sp_b", [P, NCH + 1, H])
        ea = ph.sb("ea", [P, H])
        ps = ph.ps("ps", [P, NCH + 1, 40])
        pc = ph.ps("pc", [P, 3, NCH, H])
        w_in, projected, step, a_step, summed = (ph.sem(n) for n in ("w_in", "projected", "step", "a_step", "summed"))
        block = ph.block()
        sizes = [P] * NCH + [NB]

        @block.sync
        def _(sp):
            wv = io["w_in"].rearrange("(k p) m -> p k m", p=P)
            sp.dma_start(w[:, :, 0:16], wv[:, :, C_B:C_B + 16]).then_inc(w_in, 16)
            sp.dma_start(w[:, :, 16:40], wv[:, :, C_G:C_G + 24]).then_inc(w_in, 16)

        @block.tensor
        def _(pe):
            pe.wait_ge(w_in, 32)
            for i, n in enumerate(sizes):
                for k in range(KD):
                    last = pe.matmul(ps[0:n, i, :], hT[:, k, i * P:i * P + n], w[:, k, :],
                                     start=(k == 0), stop=(k == KD - 1))
            last.then_inc(projected, 1)
            pe.wait_ge(step, 7)
            for c in range(NCH):
                for n, m in enumerate((K_LE, K_GT, K_ONE)):
                    last = pe.matmul(pc[:, n, c, :], consts[:, m:m + P], st["g"][:, c, :], start=True, stop=True)
            last.then_inc(summed, 1)

        @block.vector
        def _(v):
            v.memset(raw[:], 0.0).then_inc(step, 1)
            v.wait_ge(step, 1)
            v.wait_ge(projected, 1)
            v.tensor_copy(raw[:, 0:NCH, :], ps[:, 0:NCH, :])
            v.tensor_copy(raw[0:NB, NCH, :], ps[0:NB, NCH, :]).then_inc(step, 1)
            v.wait_ge(step, 2)
            v.tensor_tensor(sp_a[:], raw[:, :, H:2 * H], each(scal[:, H:2 * H], NCH + 1), ALU.add).then_inc(step, 1)
            v.wait_ge(a_step, 5)
            v.wait_ge(step, 3)
            v.tensor_scalar(sp_a[:], sp_a[:], 0.0, None, ALU.max).then_inc(step, 1)
            v.wait_ge(step, 4)
            v.tensor_tensor(sp_a[:], sp_a[:], sp_b[:], ALU.add).then_inc(step, 1)
            v.tensor_scalar(ea[:], ea[:], -1.0, None, ALU.mult).then_inc(step, 1)
            v.wait_ge(step, 6)
            v.tensor_tensor(st["g"][:], sp_a[:], each(ea[:], NCH + 1), ALU.mult).then_inc(step, 1)

        @block.scalar
        def _(a):
            a.wait_ge(step, 3)
            a.activation(sp_b[:], sp_a[:], ACT.Abs).then_inc(a_step, 1)
            a.wait_ge(a_step, 1)
            a.activation(sp_b[:], sp_b[:], ACT.Exp, scale=-1.0).then_inc(a_step, 1)
            a.activation(ea[:], scal[:, 0:H], ACT.Exp).then_inc(a_step, 1)
            a.wait_ge(a_step, 2)
            a.activation(sp_b[:], sp_b[:], ACT.Ln, bias=1.0).then_inc(a_step, 1)
            a.activation(st["beta"][:], raw[:, :, 0:H], ACT.Sigmoid)
            a.activation(st["gates"][:], raw[:, :, 16:40], ACT.Sigmoid).then_inc(a_step, 1)
            a.wait_ge(summed, 1)
            a.activation(st["egc"][:], pc[:, 0], ACT.Exp)
            a.activation(st["egl"][:], pc[:, 1], ACT.Exp)
            a.activation(st["eall"][:], pc[:, 2], ACT.Exp)
            a.activation(st["es"][:], st["g"][:, NCH, :], ACT.Exp)


def deltanet(nc, io, st):
    hT, consts, ring, taps, par = st["hT"], st["consts"], st["ring"], st["taps"], st["par"]
    oaT = st["oaT"]
    ident = consts[:, K_ID:K_ID + P]
    NL = len(LEVELS)
    with Phase(nc, "dn") as ph:
        xin = [ph.sb(f"xin{j}", [P, 3 + T]) for j in range(3)]
        cv = [ph.sb(f"cv{j}", [P, T]) for j in range(3)]
        zs = ph.sb("zs", [P, T])
        kn, kb, kbg, kp, qn, qg, vb = (ph.sb(n, [P, NCH, P]) for n in ("kn", "kb", "kbg", "kp", "qn", "qg", "vb"))
        knT, kbT, qnT, qgT = (ph.sb(n, [P, NCH, P]) for n in ("knT", "kbT", "qnT", "qgT"))
        gm, e, em, es, LT, QKT, mk = (ph.sb(n, [P, NCH, P]) for n in ("gm", "e", "em", "es", "LT", "QKT", "mk"))
        Lm = [ph.sb(f"Lm{i}", [P, NCH, P]) for i in range(2)]
        M, MT, nwT, sq, sk = (ph.sb(n, [P, NCH, P]) for n in ("M", "MT", "nwT", "sq", "sk"))
        X = ph.sb("X", [P, NCH, BLK])
        on = ph.sb("on", [P, NCH, P])
        vn = ph.sb("vn", [P, P])
        S = ph.sb("S", [P, P])
        S_out = ph.sb("S_out", [P, H, P])
        ss = ph.sb("ss", [P, 3, NCH])
        fac = ph.sb("fac", [P, 6, NCH])
        pg = ph.ps("pg", [P, 2, 2, 512])
        A, B, C, Dp = (ph.ps(n, [P, NCH, P]) for n in "ABCD")

        def sems(*names):
            return [ph.sem(n) for n in names]

        loaded = sems("loaded0", "loaded1")
        done = sems("done_q", "done_k", "done_v", "done_z")
        free = sems("free_q", "free_k", "free_v", "free_z")
        conv, silu, z_silu, z_ready, tails_kept, samples_kept = sems(
            "conv", "silu", "z_silu", "z_ready", "tails_kept", "samples_kept")
        tok_q, tok_k, tok_v, sq_ready, ss_ready, factors, scaled = sems(
            "tok_q", "tok_k", "tok_v", "sq_ready", "ss_ready", "factors", "scaled")
        turned, ch_ready = sems("turned", "ch_ready")
        gm_ready, dt_done, e_ready, em_ready, es_ready = sems("gm_ready", "dt_done", "e_ready", "em_ready", "es_ready")
        kk_done, qk_done, LT_ready, QKT_ready, m1_ready, MT0_ready, M0_turned, M_ready = sems(
            "kk_done", "qk_done", "LT_ready", "QKT_ready", "m1_ready", "MT0_ready", "M0_turned", "M_ready")
        Lm_ready, X_done, X_ready, Y_done, M_turned, MT_ready = sems(
            "Lm_ready", "X_done", "X_ready", "Y_done", "M_turned", "MT_ready")
        w_done, w_ready, v_done, v_ready, s_done, S_ready, o_done, o_sq, o_sum, o_ready, o_turned, out_ready = sems(
            "w_done", "w_ready", "v_done", "v_ready", "s_done", "S_ready", "o_done", "o_sq", "o_sum", "o_ready",
            "o_turned", "out_ready")
        padded, stored, eps_added = sems("padded", "stored", "eps_added")
        mh = consts[:, K_MH:K_MH + 1].unsqueeze(1)
        block = ph.block()
        wv = io["w_in"]

        def load(sp, h, b):
            for j in range(2):
                sp.dma_start(ring[:, b, 0:KD, j * P:(j + 1) * P],
                             wv[:, bass.ds(h * P + (2 * b + j) * 1024, P)].rearrange("(k p) m -> p k m", p=P))\
                    .then_inc(loaded[b], 16)

        @block.sync
        def _(sp):
            for b in range(2):
                load(sp, 0, b)
            with sp.Fori(1, H) as h:
                for b in range(2):
                    sp.wait_ge(done[2 * b + 1], h)
                    load(sp, h, b)
            sp.wait_ge(S_ready, H * NCH)
            sp.dma_start(io["p_delta"].rearrange("a b h k v -> k (a b h) v"), S_out[:]).then_inc(stored, 16)
            sp.wait_ge(stored, 16)

        @block.tensor
        def _(pe):
            with pe.Fori(0, H) as h:
                h1 = h + 1
                for n in range(4):
                    b, j = n // 2, n % 2
                    if j == 0:
                        pe.wait_ge(loaded[b], 32 * h + 32)
                    pe.wait_ge(free[(n + 2) % 4], h if n < 2 else h1)
                    for k in range(KD):
                        for c in range(2):
                            last = pe.matmul(pg[:, j, c, 0:HALF], ring[:, b, k, j * P:(j + 1) * P],
                                             hT[:, k, c * HALF:(c + 1) * HALF], start=(k == 0), stop=(k == KD - 1))
                    last.then_inc(done[n], 1)
                pe.wait_ge(out_ready, h)
                for n, (bank, sem) in enumerate(((A, tok_q), (B, tok_k), (C, tok_v))):
                    pe.wait_ge(silu, 3 * h + n + 1)
                    for c in range(NCH):
                        last = pe.transpose(bank[:, c, :], cv[n][:, c * P:(c + 1) * P], ident)
                    last.then_inc(sem, 1)
                pe.wait_ge(scaled, 7 * h + 7)
                for bank, src in ((Dp, kn), (B, kb), (A, qn), (C, qg)):
                    for c in range(NCH):
                        last = pe.transpose(bank[:, c, :], src[:, c, :], ident)
                    last.then_inc(turned, 1)
                pe.wait_ge(gm_ready, h1)
                pe.wait_ge(ch_ready, 4 * h + 4)
                for c in range(NCH):
                    last = pe.matmul(Dp[:, c, :], consts[:, K_GT:K_GT + P], gm[:, c, :], start=True, stop=True)
                last.then_inc(dt_done, 1)
                for bank, rhs, sem in ((A, kbT, kk_done), (B, qnT, qk_done)):
                    for c in range(NCH):
                        last = pe.matmul(bank[:, c, :], knT[:, c, :], rhs[:, c, :], start=True, stop=True)
                    last.then_inc(sem, 1)
                pe.wait_ge(MT0_ready, h1)
                for c in range(NCH):
                    last = pe.transpose(C[:, c, :], MT[:, c, :], ident)
                last.then_inc(M0_turned, 1)
                pe.wait_ge(e_ready, h1)
                for i, s in enumerate(LEVELS):
                    pe.wait_ge(Lm_ready, NL * h + i + 1)
                    pe.wait_ge(M_ready, (NL + 1) * h + i + 1)
                    for c in range(NCH):
                        even = M[:, c, :].rearrange("p (n two s) -> p n two s", two=2, s=s)[:, :, 0, :]
                        last = pe.matmul(Dp[:, c, 0:BLK], Lm[i % 2][:, c, :], even, start=True, stop=True)
                    last.then_inc(X_done, 1)
                    pe.wait_ge(X_ready, NL * h + i + 1)
                    if i:
                        pe.wait_ge(MT_ready, NL * h + i)
                    for c in range(NCH):
                        last = pe.matmul(A[:, c, 0:BLK], MT[:, c, :], X[:, c, :], start=True, stop=True)
                    last.then_inc(Y_done, 1)
                    pe.wait_ge(M_ready, (NL + 1) * h + i + 2)
                    for c in range(NCH):
                        last = pe.transpose(C[:, c, :], M[:, c, :], ident)
                    last.then_inc(M_turned, 1)
                pe.wait_ge(MT_ready, NL * h + NL)
                pe.wait_ge(QKT_ready, h1)
                for c in range(NCH):
                    last = pe.matmul(B[:, c, :], kbg[:, c, :], MT[:, c, :], start=True, stop=True)
                last.then_inc(w_done, 1)
                pe.wait_ge(w_ready, h1)
                for c in range(NCH):
                    last = pe.matmul(Dp[:, c, :], MT[:, c, :], vb[:, c, :], start=True, stop=(c == 0))
                    if c:
                        pe.wait_ge(S_ready, NCH * h + c)
                        last = pe.matmul(Dp[:, c, :], nwT[:, c, :], S[:], start=False, stop=True)
                    last.then_inc(v_done, 1)
                    if c:
                        pe.matmul(A[:, c, :], qgT[:, c, :], S[:], start=True, stop=False)
                    pe.wait_ge(v_ready, NCH * h + c + 1)
                    last = pe.matmul(A[:, c, :], QKT[:, c, :], vn[:], start=(c == 0), stop=True)
                    if c == NCH - 1:
                        last.then_inc(o_done, 1)
                    pe.matmul(C[:, c, :], kp[:, c, :], vn[:], start=True, stop=True).then_inc(s_done, 1)
                pe.wait_ge(o_ready, h1)
                for c in range(NCH):
                    last = pe.transpose(B[:, c, :], on[:, c, :], ident)
                last.then_inc(o_turned, 1)

        @block.scalar
        def _(a):
            with a.Fori(0, H) as h:
                h1 = h + 1
                for n in range(3):
                    a.wait_ge(done[n], h1)
                    a.wait_ge(tails_kept, 3 * h)
                    a.activation(split_halves(xin[n][:, 3:3 + T]), pg[:, n % 2, :, 0:HALF], ACT.Copy).then_inc(free[n], 1)
                a.wait_ge(done[3], h1)
                a.wait_ge(out_ready, h)
                a.activation(split_halves(zs[:]), pg[:, 1, :, 0:HALF], ACT.Silu).then_inc(free[3], 1)
                for n in range(3):
                    a.wait_ge(conv, 3 * CONV_W * h + CONV_W * (n + 1))
                    a.activation(cv[n][:], cv[n][:], ACT.Silu).then_inc(silu, 1)
                a.wait_ge(tok_q, h1)
                a.wait_ge(ss_ready, 3 * h)
                a.activation(sq[:], A[:], ACT.Square).then_inc(sq_ready, 1)
                a.wait_ge(tok_k, h1)
                a.activation(sk[:], B[:], ACT.Square).then_inc(sq_ready, 1)
                for n, (bank, dst) in enumerate(((Dp, knT), (B, kbT), (A, qnT), (C, qgT))):
                    a.wait_ge(turned, 4 * h + n + 1)
                    a.activation(dst[:], bank[:], ACT.Copy).then_inc(ch_ready, 1)
                a.wait_ge(dt_done, h1)
                a.wait_ge(em_ready, h)
                a.wait_ge(es_ready, h)
                a.activation(e[:], Dp[:], ACT.Exp).then_inc(e_ready, 1)
                for i in range(NL):
                    a.wait_ge(X_done, NL * h + i + 1)
                    a.activation(X[:], Dp[:, :, 0:BLK], ACT.Copy).then_inc(X_ready, 1)
                    a.wait_ge(M_turned, NL * h + i + 1)
                    a.activation(MT[:], C[:], ACT.Copy).then_inc(MT_ready, 1)
                a.wait_ge(w_done, h1)
                a.activation(nwT[:], B[:], ACT.Copy).then_inc(w_ready, 1)
                a.wait_ge(o_done, h1)
                a.activation(sq[:], A[:], ACT.Square).then_inc(o_sq, 1)

        @block.gpsimd
        def _(g):
            for n in range(3):
                g.memset(xin[n][:, 0:3], 0.0).then_inc(padded, 1)
            with g.Fori(0, H) as h:
                h1 = h + 1
                g.wait_ge(dt_done, h)
                g.tensor_tensor(gm[:], each(consts[:, K_LE:K_LE + P], NCH), over(st["g"][:, 0:NCH, bass.ds(h, 1)], P),
                                ALU.mult).then_inc(gm_ready, 1)
                for n in range(3):
                    g.wait_ge(free[n], h1)
                    g.tensor_copy(st["tails"][:, bass.ds(h + H * n, 1), :],
                                  xin[n][:, TP:3 + T].unsqueeze(1)).then_inc(tails_kept, 1)
                g.wait_ge(eps_added, h1)
                g.tensor_tensor(ss[:, 0:2, :], ss[:, 0:2, :], mh.broadcast_to([P, 2, NCH]), ALU.pow).then_inc(factors, 1)
                for n in range(3):
                    g.wait_ge(silu, 3 * h + n + 1)
                    g.tensor_copy(st["qkv_s"][:, n, :, bass.ds(h, 1)], cv[n][:, TP:T].unsqueeze(2)).then_inc(samples_kept, 1)
                g.wait_ge(z_ready, h1)
                g.tensor_copy(st["z_s"][:, :, bass.ds(h, 1)], zs[:, TP:T].unsqueeze(2)).then_inc(samples_kept, 1)
                g.wait_ge(e_ready, h1)
                g.wait_ge(LT_ready, h)
                g.tensor_tensor(es[:], e[:], each(consts[:, K_LT:K_LT + P], NCH), ALU.mult).then_inc(es_ready, 1)
                g.wait_ge(QKT_ready, h)
                g.tensor_tensor(em[:], e[:], each(consts[:, K_LE:K_LE + P], NCH), ALU.mult).then_inc(em_ready, 1)
                g.wait_ge(LT_ready, h1)
                g.tensor_tensor(mk[:], LT[:], each(consts[:, K_NEG1:K_NEG1 + P], NCH), ALU.mult).then_inc(m1_ready, 1)
                for i in range(NL):
                    if i >= 2:
                        g.wait_ge(X_done, NL * h + i - 1)
                    g.tensor_tensor(Lm[i % 2][:], LT[:], each(consts[:, K_LEV + i * P:K_LEV + (i + 1) * P], NCH),
                                    ALU.mult).then_inc(Lm_ready, 1)
                g.wait_ge(o_sum, 2 * h + 1)
                g.tensor_tensor(ss[:, 2, :], ss[:, 2, :], mh[:, 0, :].broadcast_to([P, NCH]), ALU.pow).then_inc(o_sum, 1)

        @block.vector
        def _(v):
            v.wait_ge(padded, 3)
            with v.Fori(0, H) as h:
                h1 = h + 1
                for n in range(3):
                    tap = [taps[:, bass.ds(h + CONV_T * i + H * n, 1)] for i in range(CONV_W)]
                    state = st["stT"][:, bass.ds(h + H * n, 1), :].rearrange("p a (b j) -> p (a b) j", j=3)
                    v.wait_ge(free[n], h1)
                    v.wait_ge((tok_q, tok_k, tok_v)[n], h)
                    v.wait_ge(samples_kept, 4 * h)
                    base = 3 * CONV_W * h + CONV_W * n
                    for i in range(CONV_W):
                        if i == 0:
                            v.tensor_scalar(cv[n][:, 0:TP], xin[n][:, 0:TP], tap[0], None, ALU.mult)
                            ins = v.tensor_scalar(cv[n][:, TP:T], state[:, :, 0], tap[0], None, ALU.mult)
                        else:
                            v.wait_ge(conv, base + i)
                            v.scalar_tensor_tensor(cv[n][:, 0:TP], xin[n][:, i:i + TP], tap[i], cv[n][:, 0:TP],
                                                   ALU.mult, ALU.add)
                            new = state[:, :, i] if i < 3 else xin[n][:, 3 + TP:3 + T]
                            ins = v.scalar_tensor_tensor(cv[n][:, TP:T], new, tap[i], cv[n][:, TP:T], ALU.mult, ALU.add)
                        ins.then_inc(conv, 1)
                v.wait_ge(free[3], h1)
                v.tensor_scalar(zs[:], zs[:], par[:, 80:81], None, ALU.mult).then_inc(z_ready, 1)
                v.wait_ge(sq_ready, 2 * h + 1)
                v.tensor_reduce(ss[:, 0, :], sq[:], AX.X, ALU.add).then_inc(ss_ready, 1)
                v.wait_ge(sq_ready, 2 * h + 2)
                v.tensor_reduce(ss[:, 1, :], sk[:], AX.X, ALU.add).then_inc(ss_ready, 1)
                v.wait_ge(ss_ready, 3 * h + 2)
                v.tensor_scalar(ss[:, 0:2, :], ss[:, 0:2, :], EPS, None, ALU.add).then_inc(eps_added, 1)
                egc, egl, beta = (st[n][:, 0:NCH, bass.ds(h, 1)].rearrange("p c a -> p (c a)") for n in ("egc", "egl", "beta"))
                v.wait_ge(factors, 4 * h + 1)
                v.tensor_scalar(fac[:, 0, :], ss[:, 0, :], SCALE, None, ALU.mult)
                v.scalar_tensor_tensor(fac[:, 1, :], ss[:, 0, :], SCALE, egc, ALU.mult, ALU.mult)
                v.tensor_tensor(fac[:, 3, :], ss[:, 1, :], beta, ALU.mult).then_inc(factors, 1)
                v.tensor_tensor(fac[:, 5, :], ss[:, 1, :], egl, ALU.mult).then_inc(factors, 1)
                v.wait_ge(factors, 4 * h + 2)
                v.scalar_tensor_tensor(fac[:, 4, :], fac[:, 3, :], -1.0, egc, ALU.mult, ALU.mult).then_inc(factors, 1)
                v.wait_ge(factors, 4 * h + 4)
                for dst, bank, f in ((qn, A, fac[:, 0, :]), (qg, A, fac[:, 1, :]), (kn, B, ss[:, 1, :]), (kb, B, fac[:, 3, :]),
                                     (kbg, B, fac[:, 4, :]), (kp, B, fac[:, 5, :])):
                    v.tensor_tensor(dst[:], bank[:], over(f, P), ALU.mult).then_inc(scaled, 1)
                v.wait_ge(tok_v, h1)
                v.tensor_tensor(vb[:], C[:], over(beta, P), ALU.mult).then_inc(scaled, 1)
                v.wait_ge(kk_done, h1)
                v.wait_ge(es_ready, h1)
                v.tensor_tensor(LT[:], A[:], es[:], ALU.mult).then_inc(LT_ready, 1)
                v.wait_ge(qk_done, h1)
                v.wait_ge(em_ready, h1)
                v.tensor_tensor(QKT[:], B[:], em[:], ALU.mult).then_inc(QKT_ready, 1)
                v.wait_ge(m1_ready, h1)
                v.tensor_tensor(MT[:], mk[:], each(ident, NCH), ALU.add).then_inc(MT0_ready, 1)
                v.wait_ge(M0_turned, h1)
                v.tensor_copy(M[:], C[:]).then_inc(M_ready, 1)
                for i, s in enumerate(LEVELS):
                    v.wait_ge(Y_done, NL * h + i + 1)
                    v.wait_ge(M_ready, (NL + 1) * h + i + 1)
                    even = M[:].rearrange("p c (n two s) -> p (c n) two s", two=2, s=s)[:, :, 0, :]
                    y = A[:, :, 0:BLK]
                    v.tensor_tensor(even.rearrange("p (c n) s -> p c n s", c=NCH), even.rearrange("p (c n) s -> p c n s", c=NCH),
                                    y.rearrange("p c (n s) -> p c n s", s=s), ALU.subtract).then_inc(M_ready, 1)
                for c in range(NCH):
                    v.wait_ge(v_done, NCH * h + c + 1)
                    v.wait_ge(s_done, NCH * h + c)
                    v.tensor_copy(vn[:], Dp[:, c, :]).then_inc(v_ready, 1)
                    v.wait_ge(s_done, NCH * h + c + 1)
                    to = S_out[:, bass.ds(h, 1), :].rearrange("p a n -> p (a n)") if c == NCH - 1 else S[:]
                    if c == 0:
                        v.tensor_copy(to, C[:, c, :]).then_inc(S_ready, 1)
                    else:
                        v.wait_ge(S_ready, NCH * h + c)
                        v.scalar_tensor_tensor(to, S[:], st["eall"][:, c, bass.ds(h, 1)], C[:, c, :],
                                               ALU.mult, ALU.add).then_inc(S_ready, 1)
                v.wait_ge(o_sq, h1)
                v.tensor_reduce(ss[:, 2, :], sq[:], AX.X, ALU.add).then_inc(ss_ready, 1)
                v.wait_ge(ss_ready, 3 * h + 3)
                v.tensor_scalar(ss[:, 2, :], ss[:, 2, :], 1.0 / P, EPS, ALU.mult, ALU.add).then_inc(o_sum, 1)
                v.wait_ge(o_sum, 2 * h + 2)
                v.tensor_tensor(on[:], A[:], over(ss[:, 2, :], P), ALU.mult).then_inc(o_ready, 1)
                v.wait_ge(o_turned, h1)
                v.wait_ge(z_ready, h1)
                v.tensor_tensor(oaT[:, bass.ds(h, 1), 0:TP].rearrange("p a n -> p (a n)"),
                                B[:].rearrange("p c n -> p (c n)"), zs[:, 0:TP], ALU.mult).then_inc(out_ready, 1)


def sparse_projections(nc, io, st):
    consts, ring = st["consts"], st["ring"]
    ident = consts[:, K_ID:K_ID + P]

    def copy_to(dst):
        def act(a, t, b, done, free, view):
            a.wait_ge(done[0], 2 * t + b + 1)
            a.activation(split_halves(dst[:, bass.ds(4 * t + 2 * b, 1), :].rearrange("p a n -> p (a n)")),
                         view(0), ACT.Copy).then_inc(free[0], 1)

        def dve(v, t, b, done, free, view):
            v.wait_ge(done[1], 2 * t + b + 1)
            v.tensor_copy(split_halves(dst[:, bass.ds(4 * t + 2 * b + 1, 1), :].rearrange("p a n -> p (a n)")),
                          view(1)).then_inc(free[1], 1)
        return dict(act=act, dve=dve)

    gemm(nc, "gq", ring, columns(io["w_in"], C_Q), st["hT"], 2, **copy_to(st["qT"]))
    gemm(nc, "gkv", ring, columns(io["w_in"], C_KV), st["hT"], 3, **copy_to(st["kvT"]))

    with Phase(nc, "kvr") as ph:
        rows = ph.sb("rows", [P, NCH, 12 * P])
        tail_rows = ph.sb("tail_rows", [11, CONV_T * P])
        slanted = ring[:].rearrange("p a k m -> p (a k m)")[:, 0:H * 2 * P]
        oh = ring[0:NBK].rearrange("p a k m -> p (a k m)")
        rel = ph.sb("rel", [NBK, H])
        rel64 = ph.sb("rel64", [NBK, NB, H])
        vec = st["bias"][0:H, 0:2, :].rearrange("p a n -> p (a n)")[:, 0:B_S]
        vec_dram = nc.dram_tensor("bias_by_distance", [H, B_S], F32, kind="Internal")
        pt = ph.ps("pt", [P, 2, 4, 512])
        turned, emptied, tab_in, rel_in, masked, stored, vec_ready, vec_out, bias_in, biased, repeated, kept = (ph.sem(n) for n in (
            "turned", "emptied", "tab_in", "rel_in", "masked", "stored", "vec_ready", "vec_out", "bias_in", "biased",
            "repeated", "kept"))
        block = ph.block()
        NSTEP = 8

        @block.sync
        def _(sp):
            sp.dma_start(oh[:, 0:B_COLS], io["buckets"]).then_inc(tab_in, 16)
            sp.dma_start(rel[0:32, :], io["rel_bias"]).then_inc(rel_in, 16)
            sp.dma_start(io["s_conv"][0, :, 0:2, :], io["state_conv"][0, :, 1:3, :]).then_inc(stored, 16)
            for i in range(NCH):
                sp.wait_ge(emptied, i + 1)
                for n, name in enumerate(("p_cmp", "p_sel", "p_win")):
                    sp.dma_start(io[name][0, 0, i * P:(i + 1) * P].rearrange("t c k d -> t (c k d)"),
                                 rows[:, i, n * 512:(n + 1) * 512]).then_inc(stored, 16)
            sp.wait_ge(emptied, 5)
            for n, (name, at) in enumerate((("s_cmp", 0), ("s_sel", 0), ("s_win", TP - 1))):
                sp.dma_start(io[name][0, :, at].rearrange("b c k d -> b (c k d)"),
                             st["rows_s"][:, n * 512:(n + 1) * 512]).then_inc(stored, 16)
            sp.wait_ge(emptied, 7)
            sp.dma_start(io["p_conv"].rearrange("a b j n -> (a b j) n"), tail_rows[0:3, :]).then_inc(stored, 16)
            sp.dma_start(io["s_conv"][0, :, 2, :], tail_rows[3:11, :]).then_inc(stored, 16)
            sp.wait_ge(vec_ready, 1)
            sp.dma_start(vec_dram.ap(), vec).then_inc(vec_out, 16)
            sp.wait_ge(vec_out, 16)
            sp.dma_start(slanted.rearrange("p (h k) -> p h k", h=H),
                         bass.AP(vec_dram, 0, [[1, P], [B_S, H], [1, 2 * P]])).then_inc(bias_in, 16)
            sp.wait_ge(stored, 16 * 18)

        @block.scalar
        def _(a):
            a.dma_start(io["s_win"][0, :, 0:TP - 1], io["cache_win_kv"][0, :, 1:TP]).then_inc(kept, 16)
            a.wait_ge(kept, 16)

        @block.tensor
        def _(pe):
            for s in range(7):
                bank = pt[:, s % 2].rearrange("p a n -> p (a n)")
                if s >= 2:
                    pe.wait_ge(emptied, s - 1)
                if s < NCH:
                    for m in range(12):
                        last = pe.transpose(bank[:, m * P:(m + 1) * P], st["kvT"][:, m, s * P:(s + 1) * P], ident)
                elif s == NCH:
                    for m in range(12):
                        last = pe.transpose(bank[0:NB, m * P:(m + 1) * P], st["kvT"][:, m, TP:T], ident)
                else:
                    for m in range(12):
                        last = pe.transpose(bank[0:11, m * P:(m + 1) * P], st["tails"][:, (s - 5) * 12 + m, :], ident)
                last.then_inc(turned, 1)
            pe.wait_ge(tab_in, 16)
            pe.wait_ge(rel_in, 16)
            pe.wait_ge(masked, 1)
            pe.wait_ge(repeated, 1)
            pe.wait_ge(emptied, 6)
            bank = pt[:, 1]
            pe.matmul(bank[0:H, 0, 0:B_S], rel[:], oh[:, B_R:B_R + B_S], start=True, stop=True)
            r64 = rel64[:].rearrange("p b h -> p (b h)")
            pe.matmul(bank[0:NR, 1, :], r64, oh[:, B_S:B_S + TP], start=True, stop=True)
            pe.matmul(bank[0:NR, 2, 0:2], r64, oh[:, B_S + TP:B_S + TP + 2], start=True, stop=True)
            pe.matmul(bank[0:NR, 2, 128:256], r64, oh[:, B_CS:B_CS + P], start=True, stop=True)
            for m in range(NCH * NBLK):
                last = pe.matmul(bank[:, 3, m * H:(m + 1) * H], oh[:, B_CP + m * P:B_CP + (m + 1) * P], rel[:],
                                 start=True, stop=True)
            last.then_inc(turned, 1)
            pe.wait_ge(bias_in, 16)
            pe.wait_ge(emptied, 7)
            for n in range(4):
                last = pe.matmul(pt[:, 0, n, :], consts[:, K_J:K_J + P], slanted[:, n * 512:(n + 1) * 512], start=True, stop=True)
            last.then_inc(turned, 1)

        @block.vector
        def _(v):
            v.memset(rel[32:33, :], MASKED).then_inc(masked, 1)
            for s in range(7):
                bank = pt[:, s % 2].rearrange("p a n -> p (a n)")
                v.wait_ge(turned, s + 1)
                if s < NCH:
                    v.tensor_copy(rows[:, s, :], bank[:, 0:12 * P]).then_inc(emptied, 1)
                    v.wait_ge(emptied, s + 1)
                    for n in range(2):
                        v.tensor_copy(st["vtok"][:, s, n, :], rows[:, s, 768 + 512 * n:1024 + 512 * n])
                elif s == NCH:
                    v.tensor_copy(st["rows_s"][:], bank[0:NB, 0:12 * P]).then_inc(emptied, 1)
                else:
                    v.tensor_copy(tail_rows[:, (s - 5) * 12 * P:(s - 4) * 12 * P], bank[0:11, 0:12 * P]).then_inc(emptied, 1)
            v.wait_ge(rel_in, 16)
            v.wait_ge(masked, 1)
            v.tensor_copy(rel64[:], each(rel[:], NB)).then_inc(repeated, 1)
            v.wait_ge(turned, 8)
            bank = pt[:, 1]
            v.tensor_copy(vec, bank[0:H, 0, 0:B_S]).then_inc(vec_ready, 1)
            v.tensor_copy(st["bias_s"][:, 0:TP], bank[0:NR, 1, :])
            v.tensor_copy(st["bias_s"][:, TP:TP + 1], bank[0:NR, 2, 0:1])
            v.tensor_tensor(st["bias_cs"][:], bank[0:NR, 2, 128:256], consts[0:NR, K_X:K_X + P], ALU.add)
            v.tensor_copy(st["bias_c"][:], bank[:, 3, 0:256].rearrange("p (m h) -> p h m", h=H)).then_inc(biased, 1)
            v.wait_ge(turned, 9)
            v.tensor_copy(st["bias"][:].rearrange("p h k -> p (h k)"), pt[:, 0].rearrange("p a n -> p (a n)")).then_inc(biased, 1)


def compress(nc, io, st):
    consts, kvT = st["consts"], st["kvT"]
    ident = consts[:, K_ID:K_ID + P]
    LC = 8
    with Phase(nc, "cmp") as ph:
        table = ph.sb("table", [1, NB * NPAGE], I32)
        spare = st["obT"][:].rearrange("p h t -> p (h t)")
        pages = spare[:, 0:2048].rearrange("p (s n m) -> p s n m", s=2, n=NPAGE)
        w2 = spare[:, 2048:2304].rearrange("p (c m) -> p c m", c=2)
        pe_rows = spare[0:BLK, 2304:2560].rearrange("p (c m) -> p c m", c=2)
        cT = ph.sb("cT", [P, BLK, ROWS + 1])
        w1 = st["ring"][:, :, 0:LC // 2, :].rearrange("p s k (m f) -> p s (k m) f", f=P)
        hidden = ph.sb("hidden", [P, ROWS])
        pe_term = ph.sb("pe_term", [P, 1])
        ptr = ph.ps("ptr", [P, 2, 2, 512])
        pm = ph.ps("pm", [P, 512])
        pk = ph.ps("pk", [P, 512])
        pp = ph.ps("pp", [P, 512])
        table_in, small_in, turned, spread, pe_turned, pe_ready, mixed, term, hid, outp, outc = (ph.sem(n) for n in (
            "table_in", "small_in", "turned", "spread", "pe_turned", "pe_ready", "mixed", "term", "hid", "outp", "outc"))
        page_in = [ph.sem(f"page_in{i}") for i in range(2)]
        w_in = [ph.sem(f"w_in{i}") for i in range(2)]
        used = ph.sem("used")
        block = ph.block()

        @block.sync
        def _(sp):
            sp.dma_start(table[:], io["page_table"].rearrange("b n -> (b n)").unsqueeze(0)).then_inc(table_in, 16)
            sp.dma_start(w2, io["cmp_w2"][0].rearrange("c f d -> f c d")).then_inc(small_in, 16)
            sp.dma_start(pe_rows, io["cmp_pe"][0]).then_inc(small_in, 16)
            sp.wait_ge(table_in, 16)
            for c in range(2):
                with sp.Fori(0, NB // 2) as r:
                    for s in range(2):
                        sp.wait_ge(turned, NB * c + 2 * r)
                        for n in range(NPAGE):
                            page = sp.value_load(table[0:1, bass.ds((2 * r + s) * NPAGE + n, 1)], min_val=0, max_val=39)
                            sp.dma_start(pages[:, s, n, :], io["cache_cmp_kv"][0, bass.ds(page, 1), :, c].rearrange(
                                "a t k d -> t (a k d)")).then_inc(page_in[s], 16)

        @block.scalar
        def _(a):
            def load(c, i):
                n = c * 8 + i
                if n >= 2:
                    a.wait_ge(used, n - 1)
                a.dma_start(w1[:, n % 2], io["cmp_w1"][0, c, i * LC:(i + 1) * LC].rearrange("l d f -> d l f"))\
                    .then_inc(w_in[n % 2], 16)

            for c in range(2):
                load(c, 0)
                load(c, 1)
                for i in range(2, 8):
                    load(c, i)
                a.wait_ge(term, c + 1)
                a.activation(hidden[:], pm[:, 0:ROWS], ACT.Silu, bias=pe_term[:]).then_inc(hid, 1)

        @block.tensor
        def _(pe):
            pe.wait_ge(small_in, 32)
            for c in range(2):
                pe.transpose(pp[:, 64 * c:64 * c + 64], pe_rows[:, c, :], consts[0:BLK, K_ID:K_ID + BLK]).then_inc(pe_turned, 1)
            for c in range(2):
                with pe.Fori(0, NB // 2) as r:
                    for s in range(2):
                        pe.wait_ge(page_in[s], 64 * (NB // 2 * c + r) + 64)
                        pe.wait_ge(spread, NB * c + 2 * r)
                        for k in range(KV):
                            for n in range(NPAGE):
                                last = pe.transpose(ptr[:, s, k, n * P:(n + 1) * P], pages[:, s, n, k * P:(k + 1) * P], ident)
                        last.then_inc(turned, 1)
                pe.wait_ge(spread, NB * (c + 1))
                pe.wait_ge(pe_ready, c + 1)
                for i in range(8):
                    n = c * 8 + i
                    pe.wait_ge(w_in[n % 2], 16 * (n // 2) + 16)
                    for j in range(LC):
                        l = i * LC + j
                        last = pe.matmul(pm[:, 0:ROWS + 1], w1[:, n % 2, j, :], cT[:, l, :], start=(l == 0), stop=(l == BLK - 1))
                    last.then_inc(used, 1)
                last = None
                pe.wait_ge(hid, c + 1)
                if c == 0:
                    pe.matmul(pk[:, 0:ROWS], w2[:, 0, :], hidden[:], start=True, stop=True).then_inc(outp, 1)
                else:
                    pe.wait_ge(outc, 1)
                    pe.matmul(pk[:, 0:P], hidden[:, 0:P], w2[:, 1, :], start=True, stop=True)
                    pe.matmul(pk[0:16, P:2 * P], hidden[:, P:ROWS], w2[:, 1, :], start=True, stop=True).then_inc(outp, 1)

        @block.vector
        def _(v):
            for c in range(2):
                if c:
                    v.wait_ge(used, 8)
                v.wait_ge(pe_turned, 2)
                v.tensor_copy(cT[:, :, ROWS:ROWS + 1], pp[:, 64 * c:64 * c + 64].unsqueeze(2))
                for k in range(KV):
                    at = NB * KV * NBLK + k * NBLK
                    last = v.tensor_copy(cT[:, :, at:at + NBLK], kvT[:, 2 * c + k, 0:TP].rearrange("p (n l) -> p l n", l=BLK))
                last.then_inc(pe_ready, 1)
                with v.Fori(0, NB // 2) as r:
                    for s in range(2):
                        v.wait_ge(turned, NB * c + 2 * r + s + 1)
                        for k in range(KV):
                            ins = v.tensor_copy(cT[:, :, bass.ds((2 * r + s) * 16 + k * NBLK, NBLK)],
                                                ptr[:, s, k, :].rearrange("p (n l) -> p l n", l=BLK))
                        ins.then_inc(spread, 1)
                v.wait_ge(used, 8 * (c + 1))
                if c:
                    v.wait_ge(hid, 1)
                v.tensor_copy(pe_term[:], pm[:, ROWS:ROWS + 1]).then_inc(term, 1)
                v.wait_ge(outp, c + 1)
                if c == 0:
                    v.tensor_copy(st["kcT"][:], pk[:, 0:ROWS]).then_inc(outc, 1)
                else:
                    v.tensor_copy(st["vc_s"][:], pk[:, 0:P])
                    v.tensor_copy(st["vc_p"][:], pk[0:16, P:2 * P]).then_inc(outc, 1)


def prompt_attention(nc, io, st):
    consts, qT, kvT, obT = st["consts"], st["qT"], st["kvT"], st["obT"]
    ident = consts[:, K_ID:K_ID + P]
    NU = KV * 2 * NCH
    RING = 4
    with Phase(nc, "att") as ph:
        qs = ph.sb("qs", [P, KV, TP])
        lg = ph.sb("lg", [P, RING, TP])
        PT = ph.sb("PT", [P, 2, NCH, TP])
        nm, sm, rc = (ph.sb(n, [P, RING]) for n in ("nm", "sm", "rc"))
        lc = ph.sb("lc", [P, KV, NCH * NBLK])
        cm, cs = (ph.sb(n, [P, KV * NCH]) for n in ("cm", "cs"))
        pc = ph.sb("pc", [P, KV, NCH, 2 * NBLK])
        pcT = ph.sb("pcT", [2 * NBLK, KV, TP])
        pS = ph.ps("pS", [P, 2, TP])
        pT = ph.ps("pT", [P, 2, NCH, P])
        pO = ph.ps("pO", [P, TP])
        pC = ph.ps("pC", [P, KV, NCH, NBLK])
        pCT = ph.ps("pCT", [2 * NBLK, KV, TP])

        def sems(*names):
            return [ph.sem(n) for n in names]

        q_ready, zeroed, s_done, lg_ready, mx_ready, e_ready, r_ready, p_ready, p_turned, pt_ready, pv_done, o_ready = sems(
            "q_ready", "zeroed", "s_done", "lg_ready", "mx_ready", "e_ready", "r_ready", "p_ready", "p_turned", "pt_ready",
            "pv_done", "o_ready")
        c_done, c_step, c_exp, c_ready, c_turned, c_kept, rc_step, rowmax, c_sum = sems(
            "c_done", "c_step", "c_exp", "c_ready", "c_turned", "c_kept", "rc_step", "rowmax", "c_sum")
        block = ph.block()
        units = [(kv, br, i) for kv in range(KV) for br in range(2) for i in range(NCH)]
        keys = {0: 4, 1: 8}

        @block.gpsimd
        def _(e):
            e.memset(pc[:], 0.0).then_inc(zeroed, 1)
            with e.Fori(0, G) as g:
                e.wait_ge(pv_done, 4 * g)
                for kv in range(KV):
                    e.tensor_copy(qs[:, kv, :], qT[:, bass.ds(kv * G + g, 1), 0:TP].rearrange("p a n -> p (a n)"))\
                        .then_inc(q_ready, 1)

        @block.tensor
        def _(pe):
            with pe.Fori(0, G) as g:
                def scores(n):
                    kv, br, i = units[n]
                    if n >= 2:
                        pe.wait_ge(lg_ready, NU * g + n - 1)
                    pe.matmul(pS[:, n % 2, 0:(i + 1) * P], qs[:, kv, i * P:(i + 1) * P],
                              kvT[:, keys[br] + kv, 0:(i + 1) * P], start=True, stop=True).then_inc(s_done, 1)

                def turn(n):
                    kv, br, i = units[n]
                    pe.wait_ge(p_ready, NU * g + n + 1)
                    pe.wait_ge(pt_ready, NU * g + max(n - 1, 0))
                    for j in range(i + 1):
                        last = pe.transpose(pT[:, n % 2, j, :], lg[:, n % RING, j * P:(j + 1) * P], ident)
                    last.then_inc(p_turned, 1)

                def values(m):
                    kv, br = m // 2, m % 2
                    if br == 0:
                        pe.wait_ge(c_kept, g + 1)
                        pe.wait_ge(o_ready, KV * g + kv)
                        pe.matmul(pO[:], st["vc_p"][:], pcT[:, kv, :], start=True, stop=False)
                    pe.wait_ge(pt_ready, NU * g + NCH * (m + 1))
                    for j in range(NCH):
                        last = pe.matmul(pO[:, j * P:TP], st["vtok"][:, j, br, kv * P:(kv + 1) * P],
                                         PT[:, m % 2, j, j * P:TP], start=False, stop=(br == 1 and j == NCH - 1))
                    last.then_inc(pv_done, 1)

                pe.wait_ge(q_ready, KV * g + KV)
                for kv in range(KV):
                    at = NB * KV * NBLK + kv * NBLK
                    for i in range(NCH):
                        last = pe.matmul(pC[:, kv, i, :], qs[:, kv, i * P:(i + 1) * P], st["kcT"][:, at:at + NBLK],
                                         start=True, stop=True)
                last.then_inc(c_done, 1)
                scores(0)
                for n in range(NU):
                    if n + 1 < NU:
                        scores(n + 1)
                    if n == 1:
                        pe.wait_ge(c_ready, g + 1)
                        for kv in range(KV):
                            for i in range(NCH):
                                last = pe.transpose(pCT[:, kv, i * P:(i + 1) * P], pc[:, kv, i, :], ident)
                        last.then_inc(c_turned, 1)
                    turn(n)
                    if n and n % NCH == 0:
                        values(n // NCH - 1)
                values(NU // NCH - 1)

        @block.scalar
        def _(a):
            with a.Fori(0, G) as g:
                def exps(n):
                    i = units[n][2]
                    w = (i + 1) * P
                    a.wait_ge(mx_ready, NU * g + n + 1)
                    a.activation(lg[:, n % RING, 0:w], lg[:, n % RING, 0:w], ACT.Exp, bias=nm[:, n % RING:n % RING + 1],
                                 accum_out=sm[:, n % RING:n % RING + 1]).then_inc(e_ready, 1)

                def scale(n):
                    w = (units[n][2] + 1) * P
                    a.wait_ge(r_ready, NU * g + n + 1)
                    a.activation(lg[:, n % RING, 0:w], lg[:, n % RING, 0:w], ACT.Copy, scale=rc[:, n % RING:n % RING + 1])\
                        .then_inc(p_ready, 1)

                a.wait_ge(c_step, 3 * g + 2)
                a.activation(lc[:], lc[:], ACT.Exp).then_inc(c_exp, 1)
                exps(0)
                for n in range(NU):
                    if n + 1 < NU:
                        exps(n + 1)
                    scale(n)
                    if n == 2:
                        a.wait_ge(c_turned, g + 1)
                        a.activation(pcT[:], pCT[:], ACT.Copy).then_inc(c_kept, 1)
                    if n in (NU // 2 + 1, NU - 1):
                        kv = 0 if n < NU - 1 else 1
                        a.wait_ge(pv_done, 4 * g + 2 * kv + 2)
                        a.activation(obT[:, bass.ds(kv * G + g, 1), 0:TP].rearrange("p a n -> p (a n)"), pO[:], ACT.Copy)\
                            .then_inc(o_ready, 1)

        @block.vector
        def _(v):
            v.wait_ge(zeroed, 1)
            with v.Fori(0, G) as g:
                def logits(n):
                    kv, br, i = units[n]
                    b = st["bias"][:, bass.ds(kv * G + g, 1), :].rearrange("p a n -> p (a n)")
                    row = lg[:, n % RING]
                    v.wait_ge(s_done, NU * g + n + 1)
                    v.wait_ge(p_turned, NU * g + max(n - RING + 1, 0))
                    lo = max(i - 1, 0) * P
                    if i >= 2:
                        v.tensor_scalar(row[:, 0:lo], pS[:, n % 2, 0:lo], SCALE, b[:, 0:1], ALU.mult, ALU.add)
                    v.scalar_tensor_tensor(row[:, lo:(i + 1) * P], pS[:, n % 2, lo:(i + 1) * P], SCALE,
                                           b[:, (P if i == 0 else 0):2 * P], ALU.mult, ALU.add).then_inc(lg_ready, 1)
                    v.wait_ge(lg_ready, NU * g + n + 1)
                    v.tensor_reduce(nm[:, n % RING:n % RING + 1], row[:, 0:(i + 1) * P], AX.X, ALU.max, negate=True)\
                        .then_inc(mx_ready, 1)

                def factor(n):
                    kv, br, i = units[n]
                    v.wait_ge(e_ready, NU * g + n + 1)
                    v.reciprocal(rc[:, n % RING:n % RING + 1], sm[:, n % RING:n % RING + 1]).then_inc(rc_step, 1)
                    v.wait_ge(rc_step, NU * g + n + 1)
                    v.tensor_tensor(rc[:, n % RING:n % RING + 1], rc[:, n % RING:n % RING + 1],
                                    st["gates"][:, i, bass.ds((br + 1) * H + kv * G + g, 1)], ALU.mult).then_inc(r_ready, 1)

                def keep(n):
                    kv, br, i = units[n]
                    m = n // NCH
                    v.wait_ge(p_turned, NU * g + n + 1)
                    v.wait_ge(pv_done, 4 * g + max(m - 1, 0))
                    v.tensor_copy(PT[:, m % 2, 0:i + 1, i * P:(i + 1) * P], pT[:, n % 2, 0:i + 1, :]).then_inc(pt_ready, 1)

                v.wait_ge(c_done, g + 1)
                bc = st["bias_c"][:].rearrange("p (k g) m -> p k g m", k=KV)[:, :, bass.ds(g, 1), :].rearrange("p k a m -> p k (a m)")
                v.scalar_tensor_tensor(lc[:], pC[:].rearrange("p k i n -> p k (i n)"), SCALE, bc, ALU.mult, ALU.add).then_inc(c_step, 1)
                v.wait_ge(c_step, 3 * g + 1)
                l8 = lc[:].rearrange("p k (i n) -> p (k i) n", n=NBLK)
                v.tensor_reduce(cm[:], l8, AX.X, ALU.max).then_inc(rowmax, 1)
                v.wait_ge(rowmax, g + 1)
                v.tensor_tensor(l8, l8, over(cm[:], NBLK), ALU.subtract).then_inc(c_step, 1)
                logits(0)
                v.wait_ge(c_exp, g + 1)
                v.tensor_reduce(cs[:], l8, AX.X, ALU.add).then_inc(c_sum, 1)
                v.wait_ge(c_sum, 3 * g + 1)
                v.reciprocal(cs[:], cs[:]).then_inc(c_sum, 1)
                v.wait_ge(c_sum, 3 * g + 2)
                gc = st["gates"][:, 0:NCH, 0:H].rearrange("p i (k g) -> p k i g", k=KV)[:, :, :, bass.ds(g, 1)].rearrange(
                    "p k i a -> p k (i a)")
                v.tensor_tensor(cs[:].rearrange("p (k i) -> p k i", k=KV), cs[:].rearrange("p (k i) -> p k i", k=KV), gc,
                                ALU.mult).then_inc(c_sum, 1)
                v.wait_ge(c_sum, 3 * g + 3)
                first = cs[:].rearrange("p (k i) -> p k i", k=KV)[:, :, 0]
                v.tensor_scalar(first, first, consts[:, K_RV:K_RV + 1], None, ALU.mult).then_inc(c_step, 1)
                v.wait_ge(c_step, 3 * g + 3)
                for kv in range(KV):
                    last = v.tensor_tensor(pc[:, kv, :, kv * NBLK:(kv + 1) * NBLK], l8[:, kv * NCH:(kv + 1) * NCH, :],
                                           over(cs[:, kv * NCH:(kv + 1) * NCH], NBLK), ALU.mult)
                last.then_inc(c_ready, 1)
                for n in range(NU):
                    if n + 1 < NU:
                        logits(n + 1)
                    factor(n)
                    if n:
                        keep(n - 1)
                keep(NU - 1)


def request_delta(nc, io, st):
    consts, qkv = st["consts"], st["qkv_s"]
    ones = consts[:, K_ONE:K_ONE + P]
    with Phase(nc, "rd") as ph:
        S = ph.sb("S", [P, NR, P])
        sq, rt, qk = (ph.sb(n, [P, 2, NR]) for n in ("sq", "rt", "qk"))
        ab8 = ph.sb("ab8", [NB, 2, NR])
        ab = ph.sb("ab", [P, 2, NR])
        prod, t1, vnew, bv, o, kq = (ph.sb(n, [P, NR]) for n in ("prod", "t1", "vnew", "bv", "o", "kq"))
        krow, vrow = (ph.sb(n, [NR, P]) for n in ("krow", "vrow"))
        spread = ph.sb("spread", [NR, 2, 4, P])
        p1 = ph.ps("p1", [P, 512])
        p2 = ph.ps("p2", [P, 512])
        p3 = ph.ps("p3", [P, NR, 2])
        p4 = ph.ps("p4", [P, 512])
        pu = ph.ps("pu", [P, 2, 4, P])
        state_in, step, root, mm, spread_ready, outer, updated, stored = (ph.sem(n) for n in (
            "state_in", "step", "root", "mm", "spread_ready", "outer", "updated", "stored"))
        block = ph.block()

        @block.sync
        def _(sp):
            for b in range(NB):
                sp.dma_start(S[:, b * H:(b + 1) * H], io["state_delta"][0, b].rearrange("h k v -> k h v"))\
                    .then_inc(state_in, 16)
            for n in range(2):
                sp.wait_ge(updated, 32 * (n + 1))
                sp.dma_start(io["s_delta"][0, n * 4:(n + 1) * 4].rearrange("b h k v -> k (b h) v"),
                             S[:, n * 32:(n + 1) * 32]).then_inc(stored, 16)
            sp.wait_ge(stored, 32)

        @block.tensor
        def _(pe):
            pe.wait_ge(step, 1)
            pe.matmul(p1[:, 0:P], ones, sq[:].rearrange("p a r -> p (a r)"), start=True, stop=True).then_inc(mm, 1)
            pe.wait_ge(step, 3)
            pe.matmul(p2[:, 0:P], consts[0:NB, K_ONE:K_ONE + P], ab8[:].rearrange("p a r -> p (a r)"),
                      start=True, stop=True).then_inc(mm, 1)
            pe.wait_ge(step, 8)
            pe.matmul(p1[:, 0:NR], ones, prod[:], start=True, stop=True).then_inc(mm, 1)
            pe.wait_ge(state_in, 16 * NB)
            for r in range(NR):
                last = pe.matmul(p3[:, r, :], S[:, r, :], qk[:, :, r], start=True, stop=True)
            last.then_inc(mm, 1)
            pe.wait_ge(step, 13)
            pe.transpose(p4[0:NR, 0:P], qk[:, 1, :], consts[:, K_ID:K_ID + P])
            pe.transpose(p4[0:NR, P:2 * P], bv[:], consts[:, K_ID:K_ID + P]).then_inc(mm, 1)
            pe.wait_ge(step, 17)
            pe.matmul(p1[:, 0:NR], ones, prod[:], start=True, stop=True).then_inc(mm, 1)
            with pe.Fori(0, 8) as j:
                for s in range(2):
                    pe.wait_ge(spread_ready, 2 * j + s + 1)
                    pe.wait_ge(updated, 8 * j)
                    pe.matmul(pu[:, s].rearrange("p a n -> p (a n)"), krow[:], spread[:, s].rearrange("p a n -> p (a n)"),
                              start=True, stop=True).then_inc(outer, 1)

        @block.scalar
        def _(a):
            a.wait_ge(step, 4)
            a.activation(rt[:], rt[:], ACT.Sqrt).then_inc(root, 1)
            a.wait_ge(step, 18)
            a.activation(rt[:, 0, :], rt[:, 0, :], ACT.Sqrt).then_inc(root, 1)

        @block.vector
        def _(v):
            def did(ins, n):
                ins.then_inc(step, 1)
                v.wait_ge(step, n)

            did(v.tensor_tensor(sq[:], qkv[:, 0:2].rearrange("p a b h -> p a (b h)"),
                                qkv[:, 0:2].rearrange("p a b h -> p a (b h)"), ALU.mult), 1)
            e8 = consts[0:NB, K_E8:K_E8 + NR].rearrange("p (b h) -> p b h", h=H)
            did(v.tensor_tensor(ab8[:, 0].rearrange("p (b h) -> p b h", h=H), e8, each(st["es"][0:NB, :], NB), ALU.mult), 2)
            did(v.tensor_tensor(ab8[:, 1].rearrange("p (b h) -> p b h", h=H), e8, each(st["beta"][0:NB, NCH, :], NB), ALU.mult), 3)
            v.wait_ge(mm, 1)
            did(v.tensor_scalar(rt[:].rearrange("p a r -> p (a r)"), p1[:, 0:P], EPS, None, ALU.add), 4)
            v.wait_ge(root, 1)
            did(v.reciprocal(rt[:], rt[:]), 5)
            did(v.scalar_tensor_tensor(qk[:, 0, :], qkv[:, 0].rearrange("p b h -> p (b h)"), SCALE, rt[:, 0, :], ALU.mult, ALU.mult), 6)
            did(v.tensor_tensor(qk[:, 1, :], qkv[:, 1].rearrange("p b h -> p (b h)"), rt[:, 1, :], ALU.mult), 7)
            did(v.tensor_tensor(prod[:], qk[:, 0, :], qk[:, 1, :], ALU.mult), 8)
            v.wait_ge(mm, 3)
            v.tensor_copy(ab[:].rearrange("p a r -> p (a r)"), p2[:, 0:P])
            did(v.tensor_copy(kq[:], p1[:, 0:NR]), 9)
            v.wait_ge(mm, 4)
            did(v.tensor_tensor(t1[:], p3[:, :, 1], ab[:, 0, :], ALU.mult), 10)
            did(v.tensor_tensor(vnew[:], qkv[:, 2].rearrange("p b h -> p (b h)"), t1[:], ALU.subtract), 11)
            did(v.tensor_tensor(bv[:], vnew[:], ab[:, 1, :], ALU.mult), 12)
            did(v.tensor_tensor(o[:], p3[:, :, 0], ab[:, 0, :], ALU.mult), 13)
            did(v.tensor_tensor(t1[:], kq[:], bv[:], ALU.mult), 14)
            did(v.tensor_tensor(o[:], o[:], t1[:], ALU.add), 15)
            v.wait_ge(mm, 5)
            v.tensor_copy(krow[:], p4[0:NR, 0:P])
            did(v.tensor_copy(vrow[:], p4[0:NR, P:2 * P]), 16)
            did(v.tensor_tensor(prod[:], o[:], o[:], ALU.mult), 17)
            v.wait_ge(mm, 6)
            did(v.tensor_scalar(rt[:, 0, :], p1[:, 0:NR], 1.0 / P, EPS, ALU.mult, ALU.add), 18)
            v.wait_ge(root, 2)
            did(v.reciprocal(rt[:, 0, :], rt[:, 0, :]), 19)
            did(v.tensor_tensor(o[:], o[:], rt[:, 0, :], ALU.mult), 20)
            did(v.tensor_tensor(st["oaT"][:, :, TP:T], o[:].rearrange("p (b h) -> p h b", h=H),
                                st["z_s"][:].rearrange("p b h -> p h b"), ALU.mult), 21)

            with v.Fori(0, 8) as j:
                for s in range(2):
                    v.wait_ge(outer, 2 * j)
                    v.tensor_tensor(spread[:, s], over(consts[0:NR, bass.ds(8 * j + 4 * s, 4)], P), each(vrow[:], 4),
                                    ALU.mult).then_inc(spread_ready, 1)
                for s in range(2):
                    v.wait_ge(outer, 2 * j + s + 1)
                    for n in range(4):
                        r = 8 * j + 4 * s + n
                        row = S[:, bass.ds(r, 1), :].rearrange("p a n -> p (a n)")
                        v.scalar_tensor_tensor(row, row, ab[:, 0, bass.ds(r, 1)], pu[:, s, n, :], ALU.mult, ALU.add)\
                            .then_inc(updated, 1)


def request_attention(nc, io, st):
    consts, qT = st["consts"], st["qT"]
    ident = consts[:, K_ID:K_ID + P]
    with Phase(nc, "ra") as ph:
        table = ph.sb("table", [1, NB * NPAGE], I32)
        spare = st["ring"][:].rearrange("p a k m -> p (a k m)")
        K = spare[:, 0:2048].rearrange("p (s n m) -> p s n m", s=2, n=NPAGE)
        KT = spare[:, 2048:4096].rearrange("p (s k m) -> p s k m", s=2, k=KV)
        V = ph.sb("V", [P, 2, NB, NPAGE, KV * P])
        qc = ph.sb("qc", [P, NR])
        qrow = ph.sb("qrow", [NR, P])
        new = ph.sb("new", [NR, 4, P])
        tmp = ph.sb("tmp", [NR, 4, P])
        snew = ph.sb("snew", [NR, 2])
        gr = ph.sb("gr", [NR, 3])
        gm = ph.sb("gm", [NR, 3, H])
        ST = ph.sb("ST", [P, NPAGE, NR])
        lg = ph.sb("lg", [NR, 2, TP + 1])
        lc = ph.sb("lc", [NR, P])
        mx, sm = (ph.sb(n, [NR, 3]) for n in ("mx", "sm"))
        PT = ph.sb("PT", [P, 2, NPAGE, NR])
        PcT = ph.sb("PcT", [P, NR])
        dg = ph.sb("dg", [NR, 2, NR])
        pK = ph.ps("pK", [P, 2, KV, TP])
        pS = ph.ps("pS", [P, NPAGE, NR])
        pA = ph.ps("pA", [P, 512])
        pB = ph.ps("pB", [NR, 512])
        pO = ph.ps("pO", [P, 512])
        table_in, q_ready, mm, step, turned, kept, scored, e_done, v_in = (ph.sem(n) for n in (
            "table_in", "q_ready", "mm", "step", "turned", "kept", "scored", "e_done", "v_in"))
        k_in = [ph.sem(f"k_in{i}") for i in range(2)]
        block = ph.block()

        def kv_load(eng, dst, br, b, c, sem):
            if br == 0:
                for n in range(NPAGE):
                    page = eng.value_load(table[0:1, bass.ds(b * NPAGE + n, 1)], min_val=0, max_val=39)
                    eng.dma_start(dst[:, n, :], io["cache_sel_kv"][0, bass.ds(page, 1), :, c].rearrange(
                        "a t k d -> t (a k d)")).then_inc(sem, 16)
            else:
                for n in range(NPAGE):
                    eng.dma_start(dst[:, n, :], io["cache_win_kv"][0, bass.ds(b, 1), n * P:(n + 1) * P, c].rearrange(
                        "a t k d -> t (a k d)")).then_inc(sem, 16)

        @block.sync
        def _(sp):
            sp.dma_start(table[:], io["page_table"].rearrange("b n -> (b n)").unsqueeze(0)).then_inc(table_in, 16)
            sp.wait_ge(table_in, 16)
            for br in range(2):
                with sp.Fori(0, NB // 2) as r:
                    for s in range(2):
                        sp.wait_ge(turned, NB * br + 2 * r)
                        kv_load(sp, K[:, s], br, 2 * r + s, 0, k_in[s])

        @block.scalar
        def _(a):
            a.wait_ge(table_in, 16)
            for br in range(2):
                with a.Fori(0, NB) as b:
                    kv_load(a, V[:, br, bass.ds(b, 1)].rearrange("p a n m -> p (a n) m"), br, b, 1, v_in)
            for x, at, n in ((lc[:], 2, 10), (lg[:, 0, :], 0, 17), (lg[:, 1, :], 1, 26)):
                a.wait_ge(step, n)
                a.activation(x, x, ACT.Exp, bias=mx[:, at:at + 1], accum_out=sm[:, at:at + 1]).then_inc(e_done, 1)

        @block.tensor
        def _(pe):
            e8 = consts[0:NB, K_E8:K_E8 + NR]
            pe.matmul(pB[:, 0:3 * H], e8, st["gates"][0:NB, NCH, :], start=True, stop=True).then_inc(mm, 1)
            pe.wait_ge(q_ready, 1)
            pe.wait_ge(step, 1)
            pe.transpose(pA[0:NR, 0:P], qc[:], ident).then_inc(mm, 1)
            pe.matmul(pK[0:NR, 0, 0, :], e8, st["rows_s"][:, 512:1024], start=True, stop=True)
            pe.matmul(pK[0:NR, 0, 1, :], e8, st["rows_s"][:, 1024:1536], start=True, stop=True).then_inc(mm, 1)
            pe.matmul(pB[:, 0:P], qc[:], st["kcT"][:, 0:P], start=True, stop=True).then_inc(mm, 1)
            pe.wait_ge(step, 11)
            pe.wait_ge(step, 12)
            pe.transpose(pA[:, 0:NR], lc[:], consts[0:NR, K_ID:K_ID + NR]).then_inc(mm, 1)
            pe.wait_ge(step, 13)
            for br in range(2):
                with pe.Fori(0, NB // 2) as r:
                    for s in range(2):
                        b = 2 * r + s
                        pe.wait_ge(k_in[s], 64 * (NB // 2 * br + r) + 64)
                        pe.wait_ge(kept, NB * br + 2 * r)
                        for k in range(KV):
                            for n in range(NPAGE):
                                last = pe.transpose(pK[:, s, k, n * P:(n + 1) * P], K[:, s, n, k * P:(k + 1) * P], ident)
                        last.then_inc(turned, 1)
                    for s in range(2):
                        b = 2 * r + s
                        pe.wait_ge(kept, NB * br + 2 * r + s + 1)
                        for k in range(KV):
                            for n in range(NPAGE):
                                last = pe.matmul(pS[:, n, bass.ds(b * H + k * G, G)], KT[:, s, k, n * P:(n + 1) * P],
                                                 qc[:, bass.ds(b * H + k * G, G)], start=True, stop=True)
                        last.then_inc(scored, 1)
                pe.wait_ge(step, 14 + 9 * br)
                for n in range(NPAGE):
                    last = pe.transpose(pB[:, n * P:(n + 1) * P], ST[:, n, :], ident)
                last.then_inc(mm, 1)
                pe.wait_ge(step, 20 + 9 * br)
                for n in range(NPAGE):
                    last = pe.transpose(pA[:, n * NR:(n + 1) * NR], lg[:, br, n * P:(n + 1) * P], consts[0:NR, K_ID:K_ID + NR])
                last.then_inc(mm, 1)
            pe.wait_ge(step, 31)
            pe.wait_ge(v_in, 16 * 2 * NB * NPAGE)
            pe.matmul(pO[:, 0:NR], st["vc_s"][:], PcT[:], start=True, stop=False)
            for br in range(2):
                pe.matmul(pO[:, 0:NR], new[:, 2 * br + 1, :], dg[:, br, :], start=False, stop=False)
            for br in range(2):
                for b in range(NB):
                    for k in range(KV):
                        at = b * H + k * G
                        for n in range(NPAGE):
                            last = pe.matmul(pO[:, at:at + G], V[:, br, b, n, k * P:(k + 1) * P], PT[:, br, n, at:at + G],
                                             start=False, stop=(br == 1 and b == NB - 1 and k == KV - 1 and n == NPAGE - 1))
            last.then_inc(mm, 1)

        @block.vector
        def _(v):
            def did(ins, n):
                ins.then_inc(step, 1)
                v.wait_ge(step, n)

            kvm = consts[0:NR, K_KVM:K_KVM + KV]
            v.tensor_copy(qc[:].rearrange("p (b h) -> p b h", h=H), qT[:, :, TP:T].rearrange("p h b -> p b h")).then_inc(q_ready, 1)
            v.wait_ge(mm, 1)
            did(v.tensor_tensor(gm[:], pB[:, 0:3 * H].rearrange("p (a h) -> p a h", h=H),
                                each(consts[0:NR, K_HM:K_HM + H], 3), ALU.mult), 1)
            did(v.tensor_reduce(gr[:], gm[:], AX.X, ALU.add), 2)
            v.wait_ge(mm, 2)
            did(v.tensor_copy(qrow[:], pA[0:NR, 0:P]), 3)
            v.wait_ge(mm, 3)
            own = pK[0:NR, 0].rearrange("p a (c k d) -> p (a c) k d", c=2, k=KV)
            did(v.tensor_scalar(tmp[:], own[:, :, 0, :], kvm[:, 0:1], None, ALU.mult), 4)
            did(v.scalar_tensor_tensor(new[:], own[:, :, 1, :], kvm[:, 1:2], tmp[:], ALU.mult, ALU.add), 5)
            did(v.tensor_tensor(tmp[:, 0:2, :], new[:].rearrange("p (a c) d -> p a c d", c=2)[:, :, 0, :], each(qrow[:], 2), ALU.mult), 6)
            did(v.tensor_reduce(snew[:], tmp[:, 0:2, :], AX.X, ALU.add), 7)
            v.wait_ge(mm, 4)
            did(v.scalar_tensor_tensor(lc[:], pB[:, 0:P], SCALE, st["bias_cs"][:], ALU.mult, ALU.add), 8)
            did(v.tensor_scalar(snew[:], snew[:], SCALE, st["bias_s"][:, TP:TP + 1], ALU.mult, ALU.add), 9)
            did(v.tensor_reduce(mx[:, 2:3], lc[:], AX.X, ALU.max, negate=True), 10)
            v.wait_ge(e_done, 1)
            did(v.reciprocal(sm[:, 2:3], sm[:, 2:3]), 11)
            did(v.tensor_scalar(lc[:], lc[:], sm[:, 2:3], gr[:, 0:1], ALU.mult, ALU.mult), 12)
            v.wait_ge(mm, 5)
            did(v.tensor_copy(PcT[:], pA[:, 0:NR]), 13)
            n = 13
            for br in range(2):
                with v.Fori(0, NB // 2) as r:
                    for s in range(2):
                        b = 2 * r + s
                        v.wait_ge(turned, NB * br + b + 1)
                        v.wait_ge(scored, NB * br + 2 * r)
                        v.tensor_copy(KT[:, s], pK[:, s]).then_inc(kept, 1)
                v.wait_ge(scored, NB * (br + 1))
                n += 1
                did(v.tensor_copy(ST[:], pS[:]), n)
                v.wait_ge(mm, 6 + 2 * br)
                v.tensor_copy(lg[:, br, TP:TP + 1], snew[:, br:br + 1])
                n += 1
                did(v.scalar_tensor_tensor(lg[:, br, 0:TP], pB[:, 0:TP], SCALE, st["bias_s"][:, 0:TP], ALU.mult, ALU.add), n)
                n += 1
                did(v.memset(lg[:, 1, 0:1], MASKED) if br else v.tensor_copy(tmp[:, 0, 0:1], snew[:, 0:1]), n)
                n += 1
                did(v.tensor_reduce(mx[:, br:br + 1], lg[:, br, :], AX.X, ALU.max, negate=True), n)
                v.wait_ge(e_done, 2 + br)
                n += 1
                did(v.reciprocal(sm[:, br:br + 1], sm[:, br:br + 1]), n)
                n += 1
                did(v.tensor_tensor(sm[:, br:br + 1], sm[:, br:br + 1], gr[:, br + 1:br + 2], ALU.mult), n)
                n += 1
                did(v.tensor_scalar(lg[:, br, :], lg[:, br, :], sm[:, br:br + 1], None, ALU.mult), n)
                n += 1
                did(v.tensor_scalar(dg[:, br, :], consts[0:NR, K_ID:K_ID + NR], lg[:, br, TP:TP + 1], None, ALU.mult), n)
                v.wait_ge(mm, 7 + 2 * br)
                n += 1
                did(v.tensor_copy(PT[:, br], pA[:, 0:NPAGE * NR].rearrange("p (n r) -> p n r", r=NR)), n)
            assert n == 31
            v.wait_ge(mm, 10)
            v.tensor_copy(st["obT"][:, :, TP:T], pO[:, 0:NR].rearrange("p (b h) -> p h b", h=H)).then_inc(step, 1)


def merge(nc, io, st):
    ring, mod, xT = st["ring"], st["mod"], st["xT"]
    with Phase(nc, "mg") as ph:
        sg = ph.sb("sg", [P, 2 * KD, T])
        mixed = ph.sb("mixed", [P, KD, T])
        tmp = ph.sb("tmp", [P, 2, T])
        flat = "p a n -> p (a n)"

        def tile_of(x, m):
            return split_halves(x[:, bass.ds(m, 1), :].rearrange(flat))

        def gate_act(a, t, b, done, free, view):
            for j in range(2):
                a.wait_ge(done[j], 2 * t + b + 1)
                a.activation(tile_of(sg, 4 * t + 2 * b + j), view(j), ACT.Sigmoid).then_inc(free[j], 1)

        def oa_dve(v, t, b, done, free, view):
            for j in range(2):
                m = 4 * t + 2 * b + j
                v.wait_ge(done[j], 2 * t + b + 1)
                v.tensor_tensor(tile_of(mixed, m), view(j), tile_of(sg, m), ALU.mult).then_inc(free[j], 1)

        def ob_dve(v, t, b, done, free, view):
            for j in range(2):
                m = 4 * t + 2 * b + j
                v.wait_ge(done[j], 2 * t + b + 1)
                v.tensor_tensor(split_halves(tmp[:, j, :]), view(j), tile_of(sg, m + KD), ALU.mult).then_inc(free[j], 1)
                v.wait_ge(free[j], 2 * t + b + 1)
                v.tensor_tensor(tile_of(mixed, m), tile_of(mixed, m), split_halves(tmp[:, j, :]), ALU.add)

        def out_act(a, t, b, done, free, view):
            for j in range(2):
                a.wait_ge(done[j], 2 * t + b + 1)
                a.activation(tile_of(st["hT"], 4 * t + 2 * b + j), view(j), ACT.Copy).then_inc(free[j], 1)

        gemm(nc, "gg", ring, columns(io["w_in"], C_M), st["hT"], 4, act=gate_act)
        gemm(nc, "goa", ring, columns(io["w_oa"], 0), st["oaT"], 2, dve=oa_dve)
        gemm(nc, "gob", ring, columns(io["w_ob"], 0), st["obT"], 2, dve=ob_dve)
        gemm(nc, "gout", ring, columns(io["w_out"], 0), mixed, 2, act=out_act)

    def add_to_x(v):
        for k in range(KD):
            v.tensor_tensor(xT[:, k, :], xT[:, k, :], st["hT"][:, k, :], ALU.add)

    rms_modulate(nc, "n2", st["hT"], st["hT"], mod[:, 2 * KD:3 * KD, :], None, st["consts"], extra=add_to_x)
    rms_modulate(nc, "n3", xT, st["hT"], mod[:, 4 * KD:5 * KD, :], mod[:, 3 * KD:4 * KD, :], st["consts"])


def feed_forward(nc, io, st):
    ring, mod, xT, hT = st["ring"], st["mod"], st["xT"], st["hT"]
    with Phase(nc, "ff") as ph:
        act_T = ph.sb("act_T", [P, KF, T])
        sil = ph.sb("sil", [P, T])
        sil_ready = ph.sem("sil_ready")

        def src(slot, t, b):
            return [(slot[:, 0:KD, j * P:(j + 1) * P],
                     io["w_gu"][:, bass.ds((2 * t + b) * P + j * FF, P)].rearrange("(k p) m -> p k m", p=P)) for j in range(2)]

        def gate_act(a, t, b, done, free, view):
            a.wait_ge(done[0], 2 * t + b + 1)
            a.wait_ge(free[1], 2 * t + b)
            a.activation(split_halves(sil[:]), view(0), ACT.Silu).then_inc(free[0], 1)

        def up_dve(v, t, b, done, free, view):
            v.wait_ge(done[1], 2 * t + b + 1)
            v.wait_ge(free[0], 2 * t + b + 1)
            v.tensor_tensor(split_halves(act_T[:, bass.ds(2 * t + b, 1), :].rearrange("p a n -> p (a n)")), view(1),
                            split_halves(sil[:]), ALU.mult).then_inc(free[1], 1)

        gemm(nc, "gu", ring, src, hT, KF // 2, act=gate_act, dve=up_dve, per=2)
        with Phase(nc, "dw") as pd:
            KH = KF // 2
            ps = pd.ps("ps", [P, 2, 2, 512])
            loaded = [pd.sem(f"loaded{b}") for b in range(2)]
            used, done, free = pd.sem("used"), pd.sem("done"), pd.sem("free")
            block = pd.block()

            def load(sp, t, b):
                sp.dma_start(ring[:, b], io["w_down"][b * KH * P:(b + 1) * KH * P, bass.ds(t * 256, 256)].rearrange(
                    "(k p) m -> p k m", p=P)).then_inc(loaded[b], 16)

            @block.sync
            def _(sp):
                for b in range(2):
                    load(sp, 0, b)
                with sp.Fori(1, 4) as t:
                    for b in range(2):
                        sp.wait_ge(used, 2 * t + b - 1)
                        load(sp, t, b)

            @block.tensor
            def _(pe):
                with pe.Fori(0, 4) as t:
                    for b in range(2):
                        pe.wait_ge(loaded[b], 16 * t + 16)
                        pe.wait_ge(free, 2 * t)
                        for j in range(2):
                            for k in range(KH):
                                for c in range(2):
                                    last = pe.matmul(ps[:, j, c, 0:HALF], ring[:, b, k, j * P:(j + 1) * P],
                                                     act_T[:, b * KH + k, c * HALF:(c + 1) * HALF],
                                                     start=(b == 0 and k == 0), stop=(b == 1 and k == KH - 1))
                            if b and j == 0:
                                last.then_inc(done, 1)
                        last.then_inc(used, 1)

            @block.scalar
            def _(a):
                with a.Fori(0, 4) as t:
                    for j in range(2):
                        if j:
                            a.wait_ge(used, 2 * t + 2)
                        else:
                            a.wait_ge(done, t + 1)
                        a.activation(split_halves(hT[:, bass.ds(2 * t + j, 1), :].rearrange("p a n -> p (a n)")),
                                     ps[:, j, :, 0:HALF], ACT.Copy).then_inc(free, 1)

    def add_to_x(v):
        for k in range(KD):
            v.tensor_tensor(xT[:, k, :], xT[:, k, :], hT[:, k, :], ALU.add)

    rms_modulate(nc, "n4", hT, hT, mod[:, 5 * KD:6 * KD, :], None, st["consts"], extra=add_to_x)
    with Phase(nc, "y") as ph:
        rows = ph.sb("rows", [P, NCH + 1, D])
        ps = ph.ps("ps", [P, 3, 1024])
        turned, copied, stored = ph.sem("turned"), ph.sem("copied"), ph.sem("stored")
        block = ph.block()
        sizes = [P] * NCH + [NB]

        @block.tensor
        def _(pe):
            for i, n in enumerate(sizes):
                if i >= 3:
                    pe.wait_ge(copied, i - 2)
                for k in range(KD):
                    last = pe.transpose(ps[0:n, i % 3, k * P:(k + 1) * P], xT[:, k, i * P:i * P + n],
                                        st["consts"][:, K_ID:K_ID + P])
                last.then_inc(turned, 1)

        @block.vector
        def _(v):
            for i, n in enumerate(sizes):
                v.wait_ge(turned, i + 1)
                v.tensor_copy(rows[0:n, i, :], ps[0:n, i % 3, :]).then_inc(copied, 1)

        @block.sync
        def _(sp):
            for i in range(NCH):
                sp.wait_ge(copied, i + 1)
                sp.dma_start(io["y_prompt"][0, i * P:(i + 1) * P, :], rows[:, i, :]).then_inc(stored, 16)
            sp.wait_ge(copied, NCH + 1)
            sp.dma_start(io["y_sample"].rearrange("b t d -> (b t) d"), rows[0:NB, NCH, :]).then_inc(stored, 16)
            sp.wait_ge(stored, 16 * (NCH + 1))


def build(nc, io):
    with Phase(nc, "all") as ph:
        st = {
            "consts": ph.sb("consts", [P, K_COLS]), "ring": ph.sb("ring", [P, 2, 11, 256]),
            "xT": ph.sb("xT", [P, KD, T]), "hT": ph.sb("hT", [P, KD, T]), "cT": ph.sb("cT", [P, KD, NMOD]),
            "par": ph.sb("par", [P, 81]), "taps": ph.sb("taps", [P, CONV_W * CONV_T]),
            "stT": ph.sb("stT", [P, CONV_T, 24]), "mod": ph.sb("mod", [P, 6 * KD, NMOD]),
            "scal": ph.sb("scal", [P, 2 * H]), "g": ph.sb("g", [P, NCH + 1, H]), "beta": ph.sb("beta", [P, NCH + 1, H]),
            "gates": ph.sb("gates", [P, NCH + 1, 3 * H]), "egc": ph.sb("egc", [P, NCH, H]),
            "egl": ph.sb("egl", [P, NCH, H]), "eall": ph.sb("eall", [P, NCH, H]), "es": ph.sb("es", [P, H]),
            "tails": ph.sb("tails", [P, CONV_T, 11]), "qkv_s": ph.sb("qkv_s", [P, 3, NB, H]), "z_s": ph.sb("z_s", [P, NB, H]),
            "oaT": ph.sb("oaT", [P, H, T]),
        }
        mod = st["mod"]
        prepare(nc, io, st)
        modulation(nc, io, st)
        rms_modulate(nc, "n1", st["xT"], st["hT"], mod[:, KD:2 * KD, :], mod[:, 0:KD, :], st["consts"])
        token_scalars(nc, io, st)
        deltanet(nc, io, st)
        request_delta(nc, io, st)
        with Phase(nc, "nsa") as pn:
            st.update({
                "qT": pn.sb("qT", [P, H, T]), "rows_s": pn.sb("rows_s", [NB, 12 * P]), "obT": pn.sb("obT", [P, H, T]),
                "bias_s": pn.sb("bias_s", [NR, TP + 2]), "bias_cs": pn.sb("bias_cs", [NR, P]),
                "kcT": pn.sb("kcT", [P, ROWS]), "vc_s": pn.sb("vc_s", [P, P]),
            })
            with Phase(nc, "nsp") as pp:
                st.update({
                    "kvT": pp.sb("kvT", [P, 12, T]), "vtok": pp.sb("vtok", [P, NCH, 2, KV * P]),
                    "bias": pp.sb("bias", [P, H, 2 * P]), "bias_c": pp.sb("bias_c", [P, H, NCH * NBLK]),
                    "vc_p": pp.sb("vc_p", [16, P]),
                })
                sparse_projections(nc, io, st)
                compress(nc, io, st)
                prompt_attention(nc, io, st)
            request_attention(nc, io, st)
            merge(nc, io, st)
        feed_forward(nc, io, st)


_INS = ["x_prompt", "x_sample", "cache_cmp_kv", "cache_sel_kv", "cache_win_kv", "state_delta", "state_conv",
        "page_table", "c_prompt", "c_sample", "w_ada", "b_ada", "norm_g", "w_in", "conv_w", "a_log", "dt_bias",
        "onorm_g", "w_oa", "w_ob", "w_out", "cmp_pe", "cmp_w1", "cmp_w2", "rel_bias", "w_gu", "w_down"]
_OUTS = [("y_prompt", (1, TP, D)), ("y_sample", (NB, 1, D)), ("p_cmp", (1, 1, TP, 2, KV, P)),
         ("p_sel", (1, 1, TP, 2, KV, P)), ("p_win", (1, 1, TP, 2, KV, P)), ("p_delta", (1, 1, H, P, P)),
         ("p_conv", (1, 1, 3, 3 * D)), ("s_cmp", (1, NB, 1, 2, KV, P)), ("s_sel", (1, NB, 1, 2, KV, P)),
         ("s_win", (1, NB, TP, 2, KV, P)), ("s_delta", (1, NB, H, P, P)), ("s_conv", (1, NB, 3, 3 * D))]


def _tables():
    import numpy as np

    c = np.zeros((P, K_COLS), np.float32)
    r, q = np.arange(P)[:, None], np.arange(P)[None, :]
    c[:, K_ID:K_ID + P] = r == q
    c[:, K_LE:K_LE + P] = r <= q
    c[:, K_GT:K_GT + P] = r > q
    c[:, K_LT:K_LT + P] = r < q

    def pairs(s):
        return (r // (2 * s) == q // (2 * s)) & (r // s % 2 == 0) & (q // s % 2 == 1)

    c[:, K_NEG1:K_NEG1 + P] = -1.0 * pairs(1)
    for i, s in enumerate(LEVELS):
        c[:, K_LEV + i * P:K_LEV + (i + 1) * P] = pairs(s)
    c[:, K_ONE:K_ONE + P] = 1.0
    rows = np.arange(NR)
    c[0:NB, K_E8:K_E8 + NR] = np.arange(NB)[:, None] == rows[None, :] // H
    c[0:NR, K_HM:K_HM + H] = rows[:, None] % H == np.arange(H)[None, :]
    c[0:NR, K_KVM:K_KVM + KV] = rows[:, None] % H // G == np.arange(KV)[None, :]
    keys = np.arange(P)
    same = (keys[None, :] // 16 == rows[:, None] // H) & (keys[None, :] % 16 // 8 == rows[:, None] % H // G)
    c[0:NR, K_X:K_X + P] = np.where(same, 0.0, MASKED)
    c[:, K_RV] = np.arange(P) >= BLK - 1

    c[:, K_MH] = -0.5
    c[:, K_J:K_J + P] = r == P - 1 - q
    def bucket(dist):
        n = np.maximum(dist, 0)
        big = 16 + (np.log(np.maximum(n, 1).astype(np.float32) / np.float32(16))
                    / np.float32(np.log(8.0)) * np.float32(16)).astype(np.int32)
        return np.where(n < 16, n, np.minimum(big, 31))

    o = np.zeros((NBK, B_COLS), np.float32)

    def put(at, dist):
        dist = dist.reshape(-1)
        row = np.where(dist >= 0, bucket(dist), NBK - 1)
        o[row, at + np.arange(dist.size)] = 1.0

    put(B_R, 255 - np.arange(B_S))
    put(B_S, TP - np.arange(TP + 1))
    i, n, t = np.meshgrid(np.arange(NCH), np.arange(NBLK), np.arange(P), indexing="ij")
    put(B_CP, i * P + t - (n * BLK + BLK - 1))
    put(B_CS, TP - (keys % 8 * BLK + BLK - 1))
    return c, o


def kernel(**inputs):
    import numpy as _np
    import concourse.bacc as _bacc
    from concourse import mybir as _mybir
    from concourse.bass_utils import run_bass_kernel_spmd as _run

    nc = _bacc.Bacc("TRN2", target_bir_lowering=False, num_devices=1)
    arrays, io = {}, {}
    squeeze = {"w_ada", "w_in", "w_oa", "w_ob", "w_out", "w_gu", "w_down"}
    for name in _INS:
        a = _np.ascontiguousarray(inputs[name])
        if name in squeeze:
            a = a[0]
        arrays[f"in_{name}"] = a
        io[name] = nc.dram_tensor(f"in_{name}", a.shape, _mybir.dt.from_np(a.dtype), kind="ExternalInput").ap()
    for name, a in zip(("consts", "buckets"), _tables()):
        arrays[f"in_{name}"] = a
        io[name] = nc.dram_tensor(f"in_{name}", a.shape, _mybir.dt.float32, kind="ExternalInput").ap()
    for name, shape in _OUTS:
        io[name] = nc.dram_tensor(f"out_{name}", shape, _mybir.dt.float32, kind="ExternalOutput").ap()
    build(nc, io)
    r = _run(nc, [arrays], core_ids=[0])
    return tuple(r.results[0][f"out_{name}"] for name, _ in _OUTS)
```

```python
from collections import deque
from contextlib import ExitStack

import concourse.bass as bass
from concourse import mybir

F32 = mybir.dt.float32
I32 = mybir.dt.int32
F32R = mybir.dt.float32r
ALU = mybir.AluOpType
ACT = mybir.ActivationFunctionType
AX = mybir.AxisListType

P = 128
D = 1024
KD = D // P
TP = 512
NB = 8
T = TP + NB
HALF = T // 2
NCH = TP // P
H = 8
KV = 2
G = H // KV
NR = NB * H
CONV_W = 4
CONV_T = 24
BLK = 64
NBLK = TP // BLK
PAGE = 128
NPAGE = 4
FF = 2816
KF = FF // P
EPS = 1e-6
SCALE = P ** -0.5
MASKED = -1e30
NMOD = 1 + NB
ROWS = NB * KV * NBLK + KV * NBLK
LEVELS = (2, 4, 8, 16, 32, 64)

C_Z = 3072
C_B = 4096
C_Q = C_B + 2 * H
C_KV = C_Q + H * P
C_G = C_KV + 6 * KV * P
C_M = C_G + 3 * H

K_ID, K_LE, K_GT, K_LT, K_NEG1 = 0, P, 2 * P, 3 * P, 4 * P
K_LEV = 5 * P
K_ONE = K_LEV + len(LEVELS) * P
K_E8 = K_ONE + P
K_HM = K_E8 + NR
K_KVM = K_HM + H
K_X = K_KVM + KV
K_RV = K_X + P
K_MH = K_RV + 1
K_J = K_MH + 1
K_COLS = K_J + P
B_R, B_S = 0, 384
B_CP = B_S + TP + 2
B_CS = B_CP + NCH * NBLK * P
B_COLS = B_CS + P
NBK = 33
BITES = {"scaled": 64, "turned": 4, "kk": 8, "hop": 4}
ADA_SLOTS = 4
SEMAPHORES = 157
START = 1


def split_halves(ap):
    return ap.rearrange("p (a n) -> p a n", a=2)


def tile_of(x, m):
    return split_halves(x[:, bass.ds(m, 1), :].rearrange("p a n -> p (a n)"))


def over(ap, n):
    if len(ap.shape) == 2:
        ap = ap.unsqueeze(2)
    return ap.broadcast_to([ap.shape[0], ap.shape[1], n])


def each(ap, n):
    return ap.unsqueeze(1).broadcast_to([ap.shape[0], n, ap.shape[1]])


class Phase:

    pool = None

    def __init__(self, nc, name):
        self.nc, self.name, self.ctx, self.sems = nc, name, ExitStack(), []

    def __enter__(self):
        return self

    def __exit__(self, *e):
        done = self.ctx.__exit__(*e)
        for s in self.sems:
            self.nc.sync.sem_clear(s)
            self.nc.sync.sem_inc(s, START)
            self.pool.idle.append(s)
        return done

    def sb(self, name, shape, dt=F32):
        return self.ctx.enter_context(self.nc.sbuf_tensor(f"{self.name}_{name}", shape, dt))

    def ps(self, name, shape, dt=F32):
        return self.ctx.enter_context(self.nc.psum_tensor(f"{self.name}_{name}", shape, dt))

    def sem(self, name):
        self.sems.append(self.pool.idle.popleft())
        return self.sems[-1]

    def block(self):
        return self.ctx.enter_context(self.nc.Block())


class Semaphores:

    def __init__(self, nc, ctx):
        self.idle = deque(ctx.enter_context(nc.semaphore(f"signal{n}")) for n in range(SEMAPHORES))
        for s in self.idle:
            nc.sync.sem_inc(s, START)
        nc.all_engine_barrier()


def columns(w, base):
    def src(slot, t, b):
        c = base + t * 512 + b * 256
        return [(slot[:, 0:KD, :], w[:, bass.ds(c, 256)].rearrange("(k p) m -> p k m", p=P))]
    return src


class Job:

    def __init__(self, load, iters, pair, source=None, act=None, dve=None, K=KD, halves=False,
                 source_steps=0):
        self.source_steps = source_steps
        self.load, self.iters, self.pair, self.source = load, iters, pair, source
        self.act, self.dve, self.K, self.halves = act, dve, K, halves


def first_loads(sp, st, name, load):
    for b in range(2):
        for dst, s in load(st["ring"][:, b], 0, b):
            sp.dma_start(dst, s).then_inc(st["w_loaded"][name][b], 16)


class Chain:

    def __init__(self, nc, name, ring, jobs, per=1, K=KD, loaded=None, then_load=None):
        self.jobs, self.ring, self.per = jobs, ring, per
        with Phase(nc, name) as ph:
            self.wh, self.wl = (ph.sb(n, [P, 2, K, P], F32R) for n in ("wh", "wl"))
            self.ps = ph.ps("ps", [P, 2, 2, 512])
            self.ahead = loaded is not None
            self.loaded = loaded or [ph.sem(f"loaded{b}") for b in range(2)]
            self.high, self.low, self.done = (ph.sem(n) for n in ("high", "low", "done"))
            self.free = [ph.sem(f"free{j}") for j in range(2)]
            self.x_high, self.x_low = ph.sem("x_high"), ph.sem("x_low")
            self.extra = [ph.sem(f"extra{n}") for n in range(2)]
            unit, x, freed = 0, 0, 0
            for job in jobs:
                if job.source is not None:
                    x += KD
                job.unit, job.x, job.freed = unit, x, freed
                unit += 4 * job.iters
                freed += job.iters * (1 if job.halves else 2)
            block = ph.block()
            chain = self

            @block.sync
            def _(sp):
                chain.run_loads(sp)
                if then_load:
                    then_load(sp)

            @block.tensor
            def _(pe):
                chain.run_products(pe)

            @block.scalar
            def _(act):
                chain.run_high(act)

            @block.vector
            def _(v):
                chain.run_low(v)

    def view(self, j):
        return self.ps[:, j, :, 0:HALF]

    def run_loads(self, sp):
        for job in self.jobs:
            def load(t, b, wait):
                if wait:
                    sp.wait_ge(self.low, job.unit + 4 * t + 2 * b - 2 + START)
                for dst, s in job.load(self.ring[:, b], t, b):
                    sp.dma_start(dst, s).then_inc(self.loaded[b], 16)

            for b in range(2):
                if job.unit or not self.ahead:
                    load(0, b, job.unit > 0)
            with sp.Fori(1, job.iters) as t:
                for b in range(2):
                    load(t, b, True)

    def run_products(self, pe):
        for job in self.jobs:
            xh, xl = job.pair
            if job.x:
                pe.wait_ge(self.x_low, job.x + START)
            with pe.Fori(0, job.iters) as t:
                for i in range(4):
                    b, j = i // 2, i % 2
                    pe.wait_ge(self.low, job.unit + 4 * t + i + 1 + START)
                    if not (job.halves and b):
                        pe.wait_ge(self.free[j], (job.freed + (t if job.halves else 2 * t + b)) + START)
                    k0 = b * job.K if job.halves else 0
                    for k in range(job.K):
                        for w, x in ((self.wh, xh), (self.wh, xl), (self.wl, xh)):
                            for c in range(2):
                                last = pe.matmul(
                                    self.ps[:, j, c, 0:HALF], w[:, j, k, :], x[:, k0 + k, c * HALF:(c + 1) * HALF],
                                    start=(k0 + k == 0 and w is self.wh and x is xh),
                                    stop=(k == job.K - 1 and w is self.wl and not (job.halves and b == 0)))
                    last.then_inc(self.done, 1)

    def splits_before(self, job):
        i = self.jobs.index(job)
        own = job.source is not None and (i == 0 or job.source_steps)
        after = self.jobs[i + 1:i + 2]
        return ([job] if own else []) + [j for j in after if j.source is not None and not j.source_steps]

    def steps(self, eng, job, ahead, empty):
        last_job = job is self.jobs[-1]
        with eng.Fori(0, job.iters - 1 if last_job else job.iters) as t:
            for i in range(4):
                ahead(job, t, i + 1)
                if empty:
                    empty(eng, self, job, t, i)
        if last_job:
            t = job.iters - 1
            for i in range(4):
                if i < 3:
                    ahead(job, t, i + 1)
                if empty:
                    empty(eng, self, job, t, i)

    def run_high(self, act):
        def ahead(job, t, i):
            n, b, j = job.unit + 4 * t + i, i // 2 % 2, i % 2
            if j == 0:
                act.wait_ge(self.loaded[b], (job.unit // 4 + t + i // 4 + 1) * 16 * self.per + START)
            act.wait_ge(self.done, n - 1 + START)
            act.activation(self.wh[:, j, 0:job.K], self.ring[:, b, 0:job.K, j * P:(j + 1) * P], ACT.Copy).then_inc(self.high, 1)

        def split(job):
            if job.source_steps:
                act.wait_ge(self.extra[1], job.source_steps + START)
            for k in range(KD):
                act.activation(job.pair[0][:, k], job.source[:, k], ACT.Copy).then_inc(self.x_high, 1)

        for job in self.jobs:
            for other in self.splits_before(job):
                split(other)
            if job is self.jobs[0]:
                act.wait_ge(self.loaded[0], 16 * self.per + START)
                act.activation(self.wh[:, 0, 0:job.K], self.ring[:, 0, 0:job.K, 0:P], ACT.Copy).then_inc(self.high, 1)
            self.steps(act, job, ahead, job.act)

    def run_low(self, v):
        def low(job, t, i):
            n, b, j = job.unit + 4 * t + i, i // 2 % 2, i % 2
            v.wait_ge(self.high, n + 1 + START)
            v.tensor_tensor(self.wl[:, j, 0:job.K], self.ring[:, b, 0:job.K, j * P:(j + 1) * P],
                            self.wh[:, j, 0:job.K].bitcast(F32), ALU.subtract).then_inc(self.low, 1)

        def split(job):
            for k in range(KD):
                v.wait_ge(self.x_high, job.x - KD + k + 1 + START)
                v.tensor_tensor(job.pair[1][:, k], job.source[:, k], job.pair[0][:, k].bitcast(F32), ALU.subtract)\
                    .then_inc(self.x_low, 1)

        for job in self.jobs:
            for other in self.splits_before(job):
                split(other)
            if job is self.jobs[0]:
                low(job, 0, 0)
            self.steps(v, job, low, job.dve)


def rms_modulate(nc, name, src, dst, s, sh, consts, onto=None, pair=None, sync=None):
    with Phase(nc, name) as ph:
        high = ph.sem("high")
        sq = ph.sb("sq", [P, KD, T])
        rbc = ph.sb("rbc", [P, T])
        total = ph.sb("total", [P, T])
        ps = ph.ps("ps", [P, 2, 512])
        squared, added, summed, rooted, normed, scaled, shifted, part = (
            ph.sem(n) for n in ("squared", "added", "summed", "rooted", "normed", "scaled", "shifted", "part"))
        tail_ready = ph.sem("tail_ready")
        block = ph.block()

        if sync:
            @block.sync
            def _(sp):
                sync(sp)

        @block.scalar
        def _(act):
            for k in range(KD):
                act.activation(sq[:, k, :], src[:, k, :], ACT.Square).then_inc(squared, 1)
            act.wait_ge(part, 1 + START)
            act.activation(rbc[:], rbc[:], ACT.Sqrt).then_inc(rooted, 1)
            if sh is not None:
                for k in range(KD):
                    act.wait_ge(scaled, k + 1 + START)
                    act.activation(dst[:, k, 0:TP], dst[:, k, 0:TP], ACT.Identity, bias=sh[:, k, 0:1]).then_inc(shifted, 1)
            if pair:
                act.wait_ge(tail_ready, 2 + START)
                for k in range(KD):
                    act.wait_ge(shifted, k + 1 + START)
                    act.activation(pair[0][:, k], dst[:, k], ACT.Copy).then_inc(high, 1)

        @block.tensor
        def _(pe):
            pe.wait_ge(added, KD - 1 + START)
            for c in range(2):
                last = pe.matmul(ps[:, c, 0:HALF], consts[:, K_ONE:K_ONE + P], total[:, c * HALF:(c + 1) * HALF],
                                 start=True, stop=True)
            last.then_inc(summed, 1)

        @block.vector
        def _(v):
            for k in range(1, KD):
                v.wait_ge(squared, k + 1 + START)
                if k > 1:
                    v.wait_ge(added, k - 1 + START)
                v.tensor_tensor(total[:], sq[:, 0, :] if k == 1 else total[:], sq[:, k, :], ALU.add).then_inc(added, 1)
            v.wait_ge(summed, 1 + START)
            v.tensor_scalar(split_halves(rbc[:]), ps[:, :, 0:HALF], 1.0 / D, EPS, ALU.mult, ALU.add).then_inc(part, 1)
            v.wait_ge(rooted, 1 + START)
            v.reciprocal(rbc[:], rbc[:]).then_inc(part, 1)
            v.wait_ge(part, 2 + START)
            tail = sq[:, :, 0:NB]
            v.tensor_tensor(tail, src[:, :, TP:T], each(rbc[:, TP:T], KD), ALU.mult).then_inc(normed, 1)
            v.wait_ge(normed, 1 + START)
            v.tensor_tensor(dst[:, :, TP:T], tail, s[:, :, 1:NMOD], ALU.mult).then_inc(tail_ready, 1)
            if sh is not None:
                v.wait_ge(tail_ready, 1 + START)
                v.tensor_tensor(dst[:, :, TP:T], dst[:, :, TP:T], sh[:, :, 1:NMOD], ALU.add).then_inc(tail_ready, 1)
            for k in range(KD):
                v.scalar_tensor_tensor(dst[:, k, 0:TP], src[:, k, 0:TP], s[:, k, 0:1], rbc[:, 0:TP], ALU.mult, ALU.mult)\
                    .then_inc(scaled, 1)
            if pair:
                for k in range(KD):
                    v.wait_ge(high, k + 1 + START)
                    v.tensor_tensor(pair[1][:, k], dst[:, k], pair[0][:, k].bitcast(F32), ALU.subtract)
            if onto is not None:
                v.wait_ge(tail_ready, 1 + START)
                for k in range(3, KD):
                    v.wait_ge(scaled, k + 1 + START)
                    v.tensor_tensor(onto[:, k, :], onto[:, k, :], dst[:, k, :], ALU.add)

        if onto is not None:
            @block.gpsimd
            def _(p):
                p.wait_ge(tail_ready, 1 + START)
                for k in range(3):
                    p.wait_ge(scaled, k + 1 + START)
                    p.tensor_tensor(onto[:, k, :], onto[:, k, :], dst[:, k, :], ALU.add)



def prepare(nc, io, st):
    consts, xT, cT, par, taps = st["consts"], st["hT"], st["cT"], st["par"], st["taps"]
    with Phase(nc, "prep") as ph:
        par_rows = ph.sb("par_rows", [81, P])
        tap_rows = ph.sb("tap_rows", [CONV_W * CONV_T, P])
        x_rows = ph.sb("x_rows", [P, NCH, D])
        s_rows = ph.sb("s_rows", [NB, D])
        c_rows = ph.sb("c_rows", [NMOD, D])
        st_rows = ph.sb("st_rows", [NB * 3, CONV_T * P])
        ps = ph.ps("ps", [P, 8, 512])
        const_in, rows_in, c_in, x_in, conv_in, c_silu, turned, copied = (
            ph.sem(n) for n in ("const_in", "rows_in", "c_in", "x_in", "conv_in", "c_silu", "turned", "copied"))
        block = ph.block()
        ident = consts[:, K_ID:K_ID + P]

        @block.sync
        def _(sp):
            sp.dma_start(consts[:], io["consts"]).then_inc(const_in, 16)
            sp.dma_start(c_rows[0:1, :], io["c_prompt"]).then_inc(c_in, 16)
            sp.dma_start(c_rows[1:NMOD, :], io["c_sample"]).then_inc(c_in, 16)
            sp.dma_start(par_rows[0:48, :], io["b_ada"].rearrange("a (m p) -> (a m) p", p=P)).then_inc(rows_in, 16)
            sp.dma_start(par_rows[48:80, :], io["norm_g"].rearrange("a i (m p) -> (a i m) p", p=P)).then_inc(rows_in, 16)
            sp.dma_start(par_rows[80:81, :], io["onorm_g"]).then_inc(rows_in, 16)
            sp.dma_start(tap_rows[:], io["conv_w"].rearrange("a i (m p) -> (a i m) p", p=P)).then_inc(rows_in, 16)
            for i in range(NCH):
                sp.dma_start(x_rows[:, i, :], io["x_prompt"][0, i * P:(i + 1) * P, :]).then_inc(x_in, 16)
            sp.dma_start(s_rows[:], io["x_sample"].rearrange("b t d -> (b t) d")).then_inc(x_in, 16)
            sp.dma_start(st_rows[:], io["state_conv"].rearrange("a b j n -> (a b j) n")).then_inc(conv_in, 16)
            sp.dma_start(st["scal"][:, 0:H], io["a_log"].broadcast_to([P, H])).then_inc(rows_in, 16)
            sp.dma_start(st["scal"][:, H:2 * H], io["dt_bias"].broadcast_to([P, H])).then_inc(rows_in, 16)
            for b in range(ADA_SLOTS):
                load_ada(sp, io, st, 0, b)

        @block.scalar
        def _(act):
            act.wait_ge(c_in, 32 + START)
            act.activation(c_rows[:], c_rows[:], ACT.Silu).then_inc(c_silu, 1)

        @block.tensor
        def _(pe):
            pe.wait_ge(const_in, 16 + START)
            pe.wait_ge(c_silu, 1 + START)
            for k in range(KD):
                last = pe.transpose(ps[:, 0, k * NMOD:(k + 1) * NMOD], c_rows[:, k * P:(k + 1) * P],
                                    consts[0:NMOD, K_ID:K_ID + NMOD])
            last.then_inc(turned, 1)
            pe.wait_ge(rows_in, 96 + START)
            pe.transpose(ps[:, 1, 0:81], par_rows[:], consts[0:81, K_ID:K_ID + 81])
            pe.transpose(ps[:, 1, 128:224], tap_rows[:], consts[0:96, K_ID:K_ID + 96]).then_inc(turned, 1)
            pe.wait_ge(x_in, 80 + START)
            for k in range(KD):
                if k >= 6:
                    pe.wait_ge(copied, k - 3 + START)
                for i in range(NCH):
                    last = pe.transpose(ps[:, 2 + k % 6, i * P:(i + 1) * P], x_rows[:, i, k * P:(k + 1) * P], ident)
                last.then_inc(turned, 1)
            pe.wait_ge(copied, 2 + START)
            for k in range(KD):
                last = pe.transpose(ps[:, 0, k * NB:(k + 1) * NB], s_rows[:, k * P:(k + 1) * P],
                                    consts[0:NB, K_ID:K_ID + NB])
            last.then_inc(turned, 1)
            pe.wait_ge(conv_in, 16 + START)
            pe.wait_ge(copied, 9 + START)
            for c in range(CONV_T):
                bank, at = (1, c * 24) if c < 12 else (2, (c - 12) * 24)
                last = pe.transpose(ps[:, bank, at:at + 24], st_rows[:, c * P:(c + 1) * P],
                                    consts[0:24, K_ID:K_ID + 24])
            last.then_inc(turned, 1)

        @block.vector
        def _(v):
            v.wait_ge(turned, 1 + START)
            v.tensor_copy(cT[:], ps[:, 0, 0:KD * NMOD].rearrange("p (k n) -> p k n", n=NMOD)).then_inc(copied, 1)
            v.wait_ge(turned, 2 + START)
            v.tensor_copy(par[:], ps[:, 1, 0:81])
            v.tensor_copy(taps[:], ps[:, 1, 128:224]).then_inc(copied, 1)
            for k in range(KD):
                v.wait_ge(turned, 3 + k + START)
                v.tensor_copy(xT[:, k, 0:TP], ps[:, 2 + k % 6, :]).then_inc(copied, 1)
            v.wait_ge(turned, 3 + KD + START)
            v.tensor_copy(xT[:, :, TP:T], ps[:, 0, 0:KD * NB].rearrange("p (k n) -> p k n", n=NB)).then_inc(copied, 1)
            v.wait_ge(turned, 4 + KD + START)
            for g in range(2):
                v.tensor_copy(st["stT"][:, g * 12:(g + 1) * 12], ps[:, 1 + g, 0:288].rearrange(
                    "p (c n) -> p c n", n=24)).then_inc(copied, 1)


def load_ada(sp, io, st, t, b):
    sp.dma_start(st["ada_ring"][:, b], io["w_ada"][:, bass.ds((t * ADA_SLOTS + b) * 256, 256)].rearrange(
        "(k p) m -> p k m", p=P)).then_inc(st["ada_loaded"][b], 16)


def modulation(nc, io, st):
    mod, par, ring = st["mod"], st["par"], st["ada_ring"]
    rounds = 6 * KD // (2 * ADA_SLOTS)
    with Phase(nc, "ada") as ph:
        rows = ph.sb("rows", [NMOD, ADA_SLOTS, 256])
        ps = ph.ps("ps", [NMOD, ADA_SLOTS, 512])
        pt = ph.ps("pt", [P, ADA_SLOTS, 512])
        done, kept, turned, added = ([ph.sem(f"{n}{b}") for b in range(ADA_SLOTS)] for n in ("done", "kept", "turned", "added"))
        block = ph.block()

        @block.sync
        def _(sp):
            with sp.Fori(1, rounds) as t:
                for b in range(ADA_SLOTS):
                    sp.wait_ge(done[b], t + START)
                    load_ada(sp, io, st, t, b)

        @block.tensor
        def _(pe):
            def turn(t, b):
                pe.wait_ge(kept[b], t + 1 + START)
                pe.wait_ge(added[b], t + START)
                for j in range(2):
                    last = pe.matmul(pt[:, b, j * NMOD:(j + 1) * NMOD], rows[:, b, j * P:(j + 1) * P],
                                     st["consts"][0:NMOD, K_ID:K_ID + NMOD], start=True, stop=True)
                last.then_inc(turned[b], 1)

            with pe.Fori(0, rounds) as t:
                for b in range(ADA_SLOTS):
                    pe.wait_ge(st["ada_loaded"][b], 16 * t + 16 + START)
                    pe.wait_ge(kept[b], t + START)
                    for k in range(KD):
                        last = pe.matmul(ps[:, b, 0:256], st["cT"][:, k, :], ring[:, b, k, :], start=(k == 0), stop=(k == KD - 1))
                    last.then_inc(done[b], 1)
                    if b:
                        turn(t, b - 1)
                turn(t, ADA_SLOTS - 1)

        @block.scalar
        def _(act):
            with act.Fori(0, rounds) as t:
                for b in range(ADA_SLOTS):
                    act.wait_ge(done[b], t + 1 + START)
                    act.wait_ge(turned[b], t + START)
                    act.activation(rows[:, b, :], ps[:, b, 0:256], ACT.Copy).then_inc(kept[b], 1)

        @block.vector
        def _(v):
            with v.Fori(0, rounds) as t:
                for b in range(ADA_SLOTS):
                    m = (t * ADA_SLOTS + b) * 2
                    v.wait_ge(turned[b], t + 1 + START)
                    v.tensor_tensor(mod[:, bass.ds(m, 2), :], pt[:, b, 0:2 * NMOD].rearrange("p (j n) -> p j n", n=NMOD),
                                    over(par[:, bass.ds(m, 2)], NMOD), ALU.add).then_inc(added[b], 1)

    with Phase(nc, "fac") as ph:
        step = ph.sem("step")
        block = ph.block()

        @block.vector
        def _(v):
            for n, (row, norm) in enumerate(((1, 0), (4, 2), (2, 1), (5, 3))):
                m = mod[:, row * KD:(row + 1) * KD, :]
                if row in (1, 4):
                    v.tensor_scalar(m, m, 1.0, None, ALU.add).then_inc(step, 1)
                    v.wait_ge(step, n + 1 + START)
                v.tensor_tensor(m, m, over(par[:, 48 + norm * KD:48 + (norm + 1) * KD], NMOD), ALU.mult)


def token_scalars(nc, io, st):
    hT, consts, scal = st["hT"], st["consts"], st["scal"]
    with Phase(nc, "tok") as ph:
        w = ph.sb("w", [P, KD, 40])
        raw = ph.sb("raw", [P, NCH + 1, 40])
        sp_a = ph.sb("sp_a", [P, NCH + 1, H])
        sp_b = ph.sb("sp_b", [P, NCH + 1, H])
        ea = ph.sb("ea", [P, H])
        ps = ph.ps("ps", [P, NCH + 1, 40])
        pc = ph.ps("pc", [P, 3, NCH, H])
        w_in, projected, step, a_step, summed = (ph.sem(n) for n in ("w_in", "projected", "step", "a_step", "summed"))
        block = ph.block()
        sizes = [P] * NCH + [NB]

        @block.sync
        def _(sp):
            wv = io["w_in"].rearrange("(k p) m -> p k m", p=P)
            sp.dma_start(w[:, :, 0:16], wv[:, :, C_B:C_B + 16]).then_inc(w_in, 16)
            sp.dma_start(w[:, :, 16:40], wv[:, :, C_G:C_G + 24]).then_inc(w_in, 16)
            first_loads(sp, st, "dn", heads_columns(io))

        @block.tensor
        def _(pe):
            pe.wait_ge(w_in, 32 + START)
            for i, n in enumerate(sizes):
                for k in range(KD):
                    last = pe.matmul(ps[0:n, i, :], hT[:, k, i * P:i * P + n], w[:, k, :],
                                     start=(k == 0), stop=(k == KD - 1))
            last.then_inc(projected, 1)
            pe.wait_ge(step, 7 + START)
            for c in range(NCH):
                for n, m in enumerate((K_LE, K_GT, K_ONE)):
                    last = pe.matmul(pc[:, n, c, :], consts[:, m:m + P], st["g"][:, c, :], start=True, stop=True)
            last.then_inc(summed, 1)

        @block.vector
        def _(v):
            v.memset(raw[:], 0.0).then_inc(step, 1)
            v.wait_ge(step, 1 + START)
            v.wait_ge(projected, 1 + START)
            v.tensor_copy(raw[:, 0:NCH, :], ps[:, 0:NCH, :])
            v.tensor_copy(raw[0:NB, NCH, :], ps[0:NB, NCH, :]).then_inc(step, 1)
            v.wait_ge(step, 2 + START)
            v.tensor_tensor(sp_a[:], raw[:, :, H:2 * H], each(scal[:, H:2 * H], NCH + 1), ALU.add).then_inc(step, 1)
            v.wait_ge(a_step, 5 + START)
            v.wait_ge(step, 3 + START)
            v.tensor_scalar(sp_a[:], sp_a[:], 0.0, None, ALU.max).then_inc(step, 1)
            v.wait_ge(step, 4 + START)
            v.tensor_tensor(sp_a[:], sp_a[:], sp_b[:], ALU.add).then_inc(step, 1)
            v.tensor_scalar(ea[:], ea[:], -1.0, None, ALU.mult).then_inc(step, 1)
            v.wait_ge(step, 6 + START)
            v.tensor_tensor(st["g"][:], sp_a[:], each(ea[:], NCH + 1), ALU.mult).then_inc(step, 1)

        @block.scalar
        def _(a):
            a.wait_ge(step, 3 + START)
            a.activation(sp_b[:], sp_a[:], ACT.Abs).then_inc(a_step, 1)
            a.wait_ge(a_step, 1 + START)
            a.activation(sp_b[:], sp_b[:], ACT.Exp, scale=-1.0).then_inc(a_step, 1)
            a.activation(ea[:], scal[:, 0:H], ACT.Exp).then_inc(a_step, 1)
            a.wait_ge(a_step, 2 + START)
            a.activation(sp_b[:], sp_b[:], ACT.Ln, bias=1.0).then_inc(a_step, 1)
            a.activation(st["beta"][:], raw[:, :, 0:H], ACT.Sigmoid)
            a.activation(st["gates"][:], raw[:, :, 16:40], ACT.Sigmoid).then_inc(a_step, 1)
            a.wait_ge(summed, 1 + START)
            a.activation(st["egc"][:], pc[:, 0], ACT.Exp)
            a.activation(st["egl"][:], pc[:, 1], ACT.Exp)
            a.activation(st["eall"][:], pc[:, 2], ACT.Exp)
            a.activation(st["es"][:], st["g"][:, NCH, :], ACT.Exp)


def heads_columns(io):
    def load(slot, g, b):
        return [(slot[:, :, j * P:(j + 1) * P],
                 io["w_in"][:, bass.ds(g * P + (2 * b + j) * 1024, P)].rearrange("(k p) m -> p k m", p=P)) for j in range(2)]
    return load


def deltanet(nc, io, st):
    hT, consts, ring, taps, par = st["hT"], st["consts"], st["ring"], st["taps"], st["par"]
    oaT = st["oaT"]
    ident = consts[:, K_ID:K_ID + P]
    NL = len(LEVELS)
    with Phase(nc, "dn") as ph:
        xin = [ph.sb(f"xin{j}", [P, 3 + T]) for j in range(3)]
        cv = [ph.sb(f"cv{j}", [P, T]) for j in range(3)]
        zs = ph.sb("zs", [P, T])
        kn, kb, kbg, kp, qn, qg, vb = (ph.sb(n, [P, NCH, P]) for n in ("kn", "kb", "kbg", "kp", "qn", "qg", "vb"))
        knT, kbT, qnT, qgT = (ph.sb(n, [P, NCH, P]) for n in ("knT", "kbT", "qnT", "qgT"))
        gm, e, em, es, LT, QKT, mk = (ph.sb(n, [P, NCH, P]) for n in ("gm", "e", "em", "es", "LT", "QKT", "mk"))
        Lm = [ph.sb(f"Lm{i}", [P, NCH, P]) for i in range(2)]
        M, MT, nwT, sq, sk = (ph.sb(n, [P, NCH, P]) for n in ("M", "MT", "nwT", "sq", "sk"))
        X = ph.sb("X", [P, NCH, BLK])
        on = ph.sb("on", [P, NCH, P])
        vn = ph.sb("vn", [P, P])
        S = ph.sb("S", [P, P])
        S_out = ph.sb("S_out", [P, H, P])
        ss = ph.sb("ss", [P, 3, NCH])
        fac = ph.sb("fac", [P, 6, NCH])
        pair = [ph.sb(n, [P, KD, T], F32R) for n in ("xh", "xl")]
        wh, wl = (ph.sb(n, [P, 2, KD, P], F32R) for n in ("wh", "wl"))
        pg = ph.ps("pg", [P, 2, 2, 512])
        A, B, C, Dp = (ph.ps(n, [P, NCH, P]) for n in "ABCD")

        def sems(*names):
            return [ph.sem(n) for n in names]

        loaded = st["w_loaded"]["dn"]
        done = sems("done_q", "done_k", "done_v", "done_z")
        free = sems("free_q", "free_k", "free_v", "free_z")
        conv, silu, z_ready, z_kept = sems("conv", "silu", "z_ready", "z_kept")
        high, low, x_high, x_low = sems("high", "low", "x_high", "x_low")
        tails_kept = sems("tails_kept_q", "tails_kept_k", "tails_kept_v")
        samples_kept = sems("samples_kept_q", "samples_kept_k", "samples_kept_v")
        tok_q, tok_k, tok_v, sq_ready, ss_ready, factors, scaled = sems(
            "tok_q", "tok_k", "tok_v", "sq_ready", "ss_ready", "factors", "scaled")
        turned, ch_ready = sems("turned", "ch_ready")
        gm_ready, dt_done, e_ready, em_ready, es_ready = sems("gm_ready", "dt_done", "e_ready", "em_ready", "es_ready")
        kk_done, qk_done, LT_ready, QKT_ready, m1_ready, MT0_ready, M0_turned, M_ready = sems(
            "kk_done", "qk_done", "LT_ready", "QKT_ready", "m1_ready", "MT0_ready", "M0_turned", "M_ready")
        Lm_ready, X_done, X_ready, Y_done, M_turned, MT_ready = sems(
            "Lm_ready", "X_done", "X_ready", "Y_done", "M_turned", "MT_ready")
        w_done, w_ready, v_done, v_ready, s_done, S_ready, o_done, o_sq, o_sum, o_ready, o_turned, out_ready = sems(
            "w_done", "w_ready", "v_done", "v_ready", "s_done", "S_ready", "o_done", "o_sq", "o_sum", "o_ready",
            "o_turned", "out_ready")
        padded, stored, eps_added = sems("padded", "stored", "eps_added")
        mh = consts[:, K_MH:K_MH + 1].unsqueeze(1)
        block = ph.block()

        @block.sync
        def _(sp):
            with sp.Fori(1, H) as g:
                for b in range(2):
                    sp.wait_ge(low, 4 * g + 2 * b - 2 + START)
                    for dst, s in heads_columns(io)(ring[:, b], g, b):
                        sp.dma_start(dst, s).then_inc(loaded[b], 16)
            sp.wait_ge(S_ready, H * NCH + START)
            sp.dma_start(io["p_delta"].rearrange("a b h k v -> k (a b h) v"), S_out[:]).then_inc(stored, 16)
            sp.wait_ge(stored, 16 + START)

        @block.tensor
        def _(pe):
            per_unit = 6 * KD

            def products(g, first, count):
                for i in range(first, first + count):
                    n, k, term, c = i // per_unit, i % per_unit // 6, i % 6 // 2, i % 2
                    j = n % 2
                    if i % per_unit == 0:
                        pe.wait_ge(low, 4 * g + n + 1 + START)
                        pe.wait_ge(free[(n + 2) % 4], (g if n < 2 else g + 1) + START)
                    w, x = ((wh, pair[0]), (wh, pair[1]), (wl, pair[0]))[term]
                    last = pe.matmul(pg[:, j, c, 0:HALF], w[:, j, k, :], x[:, k, c * HALF:(c + 1) * HALF],
                                     start=(k == 0 and term == 0), stop=(k == KD - 1 and term == 2))
                    if (i + 1) % per_unit == 0:
                        last.then_inc(done[n], 1)

            def rule(h, more):
                h1 = h + 1
                taken = [0]

                def fill(count):
                    if more:
                        products(h1, taken[0], count)
                        taken[0] += count

                pe.wait_ge(out_ready, h + START)
                for n, (bank, sem) in enumerate(((A, tok_q), (B, tok_k), (C, tok_v))):
                    pe.wait_ge(silu, 3 * h + n + 1 + START)
                    for c in range(NCH):
                        last = pe.transpose(bank[:, c, :], cv[n][:, c * P:(c + 1) * P], ident)
                    last.then_inc(sem, 1)
                pe.wait_ge(gm_ready, h1 + START)
                for c in range(NCH):
                    last = pe.matmul(Dp[:, c, :], consts[:, K_GT:K_GT + P], gm[:, c, :], start=True, stop=True)
                last.then_inc(dt_done, 1)
                fill(BITES["scaled"])
                pe.wait_ge(e_ready, h1 + START)
                pe.wait_ge(scaled, 7 * h + 7 + START)
                for bank, src in ((Dp, kn), (B, kb), (A, qn), (C, qg)):
                    for c in range(NCH):
                        last = pe.transpose(bank[:, c, :], src[:, c, :], ident)
                    last.then_inc(turned, 1)
                fill(BITES["turned"])
                pe.wait_ge(ch_ready, 4 * h + 4 + START)
                for bank, rhs, sem in ((A, kbT, kk_done), (B, qnT, qk_done)):
                    for c in range(NCH):
                        last = pe.matmul(bank[:, c, :], knT[:, c, :], rhs[:, c, :], start=True, stop=True)
                    last.then_inc(sem, 1)
                fill(BITES["kk"])
                pe.wait_ge(MT0_ready, h1 + START)
                for c in range(NCH):
                    last = pe.transpose(C[:, c, :], MT[:, c, :], ident)
                last.then_inc(M0_turned, 1)
                fill(BITES["hop"])
                for i, s in enumerate(LEVELS):
                    pe.wait_ge(Lm_ready, NL * h + i + 1 + START)
                    pe.wait_ge(M_ready, (NL + 1) * h + i + 1 + START)
                    for c in range(NCH):
                        even = M[:, c, :].rearrange("p (n two s) -> p n two s", two=2, s=s)[:, :, 0, :]
                        last = pe.matmul(Dp[:, c, 0:BLK], Lm[i % 2][:, c, :], even, start=True, stop=True)
                    last.then_inc(X_done, 1)
                    fill(BITES["hop"])
                    pe.wait_ge(X_ready, NL * h + i + 1 + START)
                    if i:
                        pe.wait_ge(MT_ready, NL * h + i + START)
                    for c in range(NCH):
                        last = pe.matmul(A[:, c, 0:BLK], MT[:, c, :], X[:, c, :], start=True, stop=True)
                    last.then_inc(Y_done, 1)
                    fill(BITES["hop"])
                    pe.wait_ge(M_ready, (NL + 1) * h + i + 2 + START)
                    for c in range(NCH):
                        last = pe.transpose(C[:, c, :], M[:, c, :], ident)
                    last.then_inc(M_turned, 1)
                pe.wait_ge(MT_ready, NL * h + NL + START)
                pe.wait_ge(QKT_ready, h1 + START)
                for c in range(NCH):
                    last = pe.matmul(B[:, c, :], kbg[:, c, :], MT[:, c, :], start=True, stop=True)
                last.then_inc(w_done, 1)
                fill(BITES["hop"])
                pe.wait_ge(w_ready, h1 + START)
                for c in range(NCH):
                    last = pe.matmul(Dp[:, c, :], MT[:, c, :], vb[:, c, :], start=True, stop=(c == 0))
                    if c:
                        pe.wait_ge(S_ready, NCH * h + c + START)
                        last = pe.matmul(Dp[:, c, :], nwT[:, c, :], S[:], start=False, stop=True)
                    last.then_inc(v_done, 1)
                    if c:
                        pe.matmul(A[:, c, :], qgT[:, c, :], S[:], start=True, stop=False)
                    fill(BITES["hop"])
                    pe.wait_ge(v_ready, NCH * h + c + 1 + START)
                    pe.matmul(C[:, c, :], kp[:, c, :], vn[:], start=True, stop=True).then_inc(s_done, 1)
                    last = pe.matmul(A[:, c, :], QKT[:, c, :], vn[:], start=(c == 0), stop=True)
                    last.then_inc(o_done, 1)
                    fill(BITES["hop"])
                fill(4 * per_unit - taken[0] - BITES["turned"])
                pe.wait_ge(o_ready, h1 + START)
                for c in range(NCH):
                    last = pe.transpose(B[:, c, :], on[:, c, :], ident)
                last.then_inc(o_turned, 1)
                fill(BITES["turned"])

            pe.wait_ge(x_low, KD + START)
            products(0, 0, 4 * per_unit)
            with pe.Fori(0, H - 1) as h:
                rule(h, True)
            rule(H - 1, False)

        @block.scalar
        def _(a):
            def split_high(g, n):
                b, j = n // 2, n % 2
                if j == 0:
                    a.wait_ge(loaded[b], 32 * g + 32 + START)
                a.wait_ge(done[(n + 2) % 4], (g if n < 2 else g + 1) + START)
                a.activation(wh[:, j], ring[:, b, :, j * P:(j + 1) * P], ACT.Copy).then_inc(high, 1)

            def take(g, n):
                a.wait_ge(done[n], g + 1 + START)
                a.wait_ge(tails_kept[n], g + START)
                a.activation(split_halves(xin[n][:, 3:3 + T]), pg[:, n % 2, :, 0:HALF], ACT.Copy).then_inc(free[n], 1)

            def pass_silu(g, n):
                a.wait_ge(conv, 3 * CONV_W * g + CONV_W * (n + 1) + START)
                a.activation(cv[n][:], cv[n][:], ACT.Silu).then_inc(silu, 1)

            def rule(h, more):
                h1 = h + 1
                a.wait_ge(done[3], h1 + START)
                a.wait_ge(out_ready, h + START)
                a.wait_ge(z_kept, h + START)
                a.activation(split_halves(zs[:]), pg[:, 1, :, 0:HALF], ACT.Silu).then_inc(free[3], 1)
                if more:
                    split_high(h1, 0)
                a.wait_ge(tok_q, h1 + START)
                a.wait_ge(ss_ready, 3 * h + START)
                a.activation(sq[:], A[:], ACT.Square).then_inc(sq_ready, 1)
                a.wait_ge(tok_k, h1 + START)
                a.activation(sk[:], B[:], ACT.Square).then_inc(sq_ready, 1)
                if more:
                    split_high(h1, 1)
                a.wait_ge(dt_done, h1 + START)
                a.wait_ge(em_ready, h + START)
                a.wait_ge(es_ready, h + START)
                a.activation(e[:], Dp[:], ACT.Exp).then_inc(e_ready, 1)
                for n, (bank, dst) in enumerate(((Dp, knT), (B, kbT), (A, qnT), (C, qgT))):
                    a.wait_ge(turned, 4 * h + n + 1 + START)
                    a.activation(dst[:], bank[:], ACT.Copy).then_inc(ch_ready, 1)
                if more:
                    take(h1, 0)
                    split_high(h1, 2)
                for i in range(NL):
                    a.wait_ge(X_done, NL * h + i + 1 + START)
                    a.activation(X[:], Dp[:, :, 0:BLK], ACT.Copy).then_inc(X_ready, 1)
                    a.wait_ge(M_turned, NL * h + i + 1 + START)
                    a.activation(MT[:], C[:], ACT.Copy).then_inc(MT_ready, 1)
                    if more and i == 2:
                        take(h1, 1)
                        pass_silu(h1, 0)
                    if more and i == 3:
                        split_high(h1, 3)
                a.wait_ge(w_done, h1 + START)
                a.activation(nwT[:], B[:], ACT.Copy).then_inc(w_ready, 1)
                if more:
                    pass_silu(h1, 1)
                    take(h1, 2)
                a.wait_ge(o_done, NCH * h1 + START)
                a.activation(sq[:], A[:], ACT.Square).then_inc(o_sq, 1)
                if more:
                    pass_silu(h1, 2)

            for k in range(KD):
                a.activation(pair[0][:, k], hT[:, k], ACT.Copy).then_inc(x_high, 1)
            split_high(0, 0)
            split_high(0, 1)
            take(0, 0)
            split_high(0, 2)
            take(0, 1)
            split_high(0, 3)
            pass_silu(0, 0)
            take(0, 2)
            pass_silu(0, 1)
            pass_silu(0, 2)
            with a.Fori(0, H - 1) as h:
                rule(h, True)
            rule(H - 1, False)

        @block.gpsimd
        def _(p):
            def keep_tails(g, n):
                p.wait_ge(free[n], g + 1 + START)
                p.tensor_copy(st["tails"][:, bass.ds(g + H * n, 1), :],
                              xin[n][:, TP:3 + T].unsqueeze(1)).then_inc(tails_kept[n], 1)

            def keep_samples(g, n):
                p.wait_ge(silu, 3 * g + n + 1 + START)
                p.tensor_copy(st["qkv_s"][:, n, :, bass.ds(g, 1)], cv[n][:, TP:T].unsqueeze(2)).then_inc(samples_kept[n], 1)

            def rule(h, more):
                h1 = h + 1
                p.wait_ge(dt_done, h + START)
                p.tensor_tensor(gm[:], each(consts[:, K_LE:K_LE + P], NCH), over(st["g"][:, 0:NCH, bass.ds(h, 1)], P),
                                ALU.mult).then_inc(gm_ready, 1)
                p.wait_ge(eps_added, h1 + START)
                p.tensor_tensor(ss[:, 0:2, :], ss[:, 0:2, :], mh.broadcast_to([P, 2, NCH]), ALU.pow).then_inc(factors, 1)
                p.wait_ge(e_ready, h1 + START)
                p.wait_ge(LT_ready, h + START)
                p.tensor_tensor(es[:], e[:], each(consts[:, K_LT:K_LT + P], NCH), ALU.mult).then_inc(es_ready, 1)
                p.wait_ge(QKT_ready, h + START)
                p.tensor_tensor(em[:], e[:], each(consts[:, K_LE:K_LE + P], NCH), ALU.mult).then_inc(em_ready, 1)
                p.wait_ge(LT_ready, h1 + START)
                p.tensor_tensor(mk[:], LT[:], each(consts[:, K_NEG1:K_NEG1 + P], NCH), ALU.mult).then_inc(m1_ready, 1)
                for i in range(NL):
                    if i >= 2:
                        p.wait_ge(X_done, NL * h + i - 1 + START)
                    p.tensor_tensor(Lm[i % 2][:], LT[:], each(consts[:, K_LEV + i * P:K_LEV + (i + 1) * P], NCH),
                                    ALU.mult).then_inc(Lm_ready, 1)
                    if i == 3:
                        p.wait_ge(z_ready, h1 + START)
                        p.tensor_copy(st["z_s"][:, :, bass.ds(h, 1)], zs[:, TP:T].unsqueeze(2)).then_inc(z_kept, 1)
                if more:
                    keep_tails(h1, 0)
                    keep_tails(h1, 1)
                    keep_samples(h1, 0)
                p.wait_ge(o_sum, 2 * h + 1 + START)
                p.tensor_tensor(ss[:, 2, :], ss[:, 2, :], mh[:, 0, :].broadcast_to([P, NCH]), ALU.pow).then_inc(o_sum, 1)
                if more:
                    keep_samples(h1, 1)
                    keep_tails(h1, 2)
                    keep_samples(h1, 2)

            for n in range(3):
                p.memset(xin[n][:, 0:3], 0.0).then_inc(padded, 1)
            for n in range(3):
                keep_tails(0, n)
                keep_samples(0, n)
            with p.Fori(0, H - 1) as h:
                rule(h, True)
            rule(H - 1, False)

        @block.vector
        def _(v):
            def split_low(g, n):
                b, j = n // 2, n % 2
                v.wait_ge(high, 4 * g + n + 1 + START)
                v.tensor_tensor(wl[:, j], ring[:, b, :, j * P:(j + 1) * P], wh[:, j].bitcast(F32), ALU.subtract).then_inc(low, 1)

            def convolve(g, n, i):
                tap = taps[:, bass.ds(g + CONV_T * i + H * n, 1)]
                state = st["stT"][:, bass.ds(g + H * n, 1), :].rearrange("p a (b j) -> p (a b) j", j=3)
                if i == 0:
                    v.wait_ge(free[n], g + 1 + START)
                    v.wait_ge((tok_q, tok_k, tok_v)[n], g + START)
                    v.wait_ge(samples_kept[n], g + START)
                    v.tensor_scalar(cv[n][:, 0:TP], xin[n][:, 0:TP], tap, None, ALU.mult)
                    ins = v.tensor_scalar(cv[n][:, TP:T], state[:, :, 0], tap, None, ALU.mult)
                else:
                    v.wait_ge(conv, 3 * CONV_W * g + CONV_W * n + i + START)
                    v.scalar_tensor_tensor(cv[n][:, 0:TP], xin[n][:, i:i + TP], tap, cv[n][:, 0:TP],
                                           ALU.mult, ALU.add)
                    new = state[:, :, i] if i < 3 else xin[n][:, 3 + TP:3 + T]
                    ins = v.scalar_tensor_tensor(cv[n][:, TP:T], new, tap, cv[n][:, TP:T], ALU.mult, ALU.add)
                ins.then_inc(conv, 1)

            def rule(h, more):
                h1 = h + 1
                if more:
                    split_low(h1, 0)
                v.wait_ge(sq_ready, 2 * h + 1 + START)
                v.tensor_reduce(ss[:, 0, :], sq[:], AX.X, ALU.add).then_inc(ss_ready, 1)
                v.wait_ge(sq_ready, 2 * h + 2 + START)
                v.tensor_reduce(ss[:, 1, :], sk[:], AX.X, ALU.add).then_inc(ss_ready, 1)
                v.wait_ge(ss_ready, 3 * h + 2 + START)
                v.tensor_scalar(ss[:, 0:2, :], ss[:, 0:2, :], EPS, None, ALU.add).then_inc(eps_added, 1)
                if more:
                    split_low(h1, 1)
                egc, egl, beta = (st[n][:, 0:NCH, bass.ds(h, 1)].rearrange("p c a -> p (c a)") for n in ("egc", "egl", "beta"))
                v.wait_ge(tok_v, h1 + START)
                v.tensor_tensor(vb[:], C[:], over(beta, P), ALU.mult).then_inc(scaled, 1)
                v.wait_ge(factors, 4 * h + 1 + START)
                v.tensor_scalar(fac[:, 0, :], ss[:, 0, :], SCALE, None, ALU.mult)
                v.scalar_tensor_tensor(fac[:, 1, :], ss[:, 0, :], SCALE, egc, ALU.mult, ALU.mult)
                v.tensor_tensor(fac[:, 3, :], ss[:, 1, :], beta, ALU.mult).then_inc(factors, 1)
                v.tensor_tensor(fac[:, 5, :], ss[:, 1, :], egl, ALU.mult).then_inc(factors, 1)
                v.wait_ge(factors, 4 * h + 2 + START)
                v.scalar_tensor_tensor(fac[:, 4, :], fac[:, 3, :], -1.0, egc, ALU.mult, ALU.mult).then_inc(factors, 1)
                v.wait_ge(factors, 4 * h + 4 + START)
                for dst, bank, f in ((qn, A, fac[:, 0, :]), (qg, A, fac[:, 1, :]), (kn, B, ss[:, 1, :]), (kb, B, fac[:, 3, :]),
                                     (kbg, B, fac[:, 4, :]), (kp, B, fac[:, 5, :])):
                    v.tensor_tensor(dst[:], bank[:], over(f, P), ALU.mult).then_inc(scaled, 1)
                v.wait_ge(kk_done, h1 + START)
                v.wait_ge(es_ready, h1 + START)
                v.tensor_tensor(LT[:], A[:], es[:], ALU.mult).then_inc(LT_ready, 1)
                v.wait_ge(qk_done, h1 + START)
                v.wait_ge(em_ready, h1 + START)
                v.tensor_tensor(QKT[:], B[:], em[:], ALU.mult).then_inc(QKT_ready, 1)
                v.wait_ge(m1_ready, h1 + START)
                v.tensor_tensor(MT[:], mk[:], each(ident, NCH), ALU.add).then_inc(MT0_ready, 1)
                v.wait_ge(M0_turned, h1 + START)
                v.tensor_copy(M[:], C[:]).then_inc(M_ready, 1)
                if more:
                    split_low(h1, 2)
                for i, s in enumerate(LEVELS):
                    v.wait_ge(Y_done, NL * h + i + 1 + START)
                    v.wait_ge(M_ready, (NL + 1) * h + i + 1 + START)
                    even = M[:].rearrange("p c (n two s) -> p (c n) two s", two=2, s=s)[:, :, 0, :]
                    y = A[:, :, 0:BLK]
                    v.tensor_tensor(even.rearrange("p (c n) s -> p c n s", c=NCH), even.rearrange("p (c n) s -> p c n s", c=NCH),
                                    y.rearrange("p c (n s) -> p c n s", s=s), ALU.subtract).then_inc(M_ready, 1)
                    if more and i in (0, 1):
                        convolve(h1, 0, 2 * i)
                        convolve(h1, 0, 2 * i + 1)
                    if i == 2:
                        v.wait_ge(free[3], h1 + START)
                        v.tensor_scalar(zs[:], zs[:], par[:, 80:81], None, ALU.mult).then_inc(z_ready, 1)
                    if more and i in (3, 4):
                        convolve(h1, 1, 2 * i - 6)
                        convolve(h1, 1, 2 * i - 5)
                    if more and i == 5:
                        split_low(h1, 3)
                for c in range(NCH):
                    v.wait_ge(v_done, NCH * h + c + 1 + START)
                    v.wait_ge(o_done, NCH * h + c + START)
                    v.tensor_copy(vn[:], Dp[:, c, :]).then_inc(v_ready, 1)
                    v.wait_ge(s_done, NCH * h + c + 1 + START)
                    to = S_out[:, bass.ds(h, 1), :].rearrange("p a n -> p (a n)") if c == NCH - 1 else S[:]
                    if c == 0:
                        v.tensor_copy(to, C[:, c, :]).then_inc(S_ready, 1)
                    else:
                        v.wait_ge(S_ready, NCH * h + c + START)
                        v.scalar_tensor_tensor(to, S[:], st["eall"][:, c, bass.ds(h, 1)], C[:, c, :],
                                               ALU.mult, ALU.add).then_inc(S_ready, 1)
                    if more and c:
                        convolve(h1, 2, c - 1)
                if more:
                    convolve(h1, 2, 3)
                v.wait_ge(o_sq, h1 + START)
                v.tensor_reduce(ss[:, 2, :], sq[:], AX.X, ALU.add).then_inc(ss_ready, 1)
                v.wait_ge(ss_ready, 3 * h + 3 + START)
                v.tensor_scalar(ss[:, 2, :], ss[:, 2, :], 1.0 / P, EPS, ALU.mult, ALU.add).then_inc(o_sum, 1)
                v.wait_ge(o_sum, 2 * h + 2 + START)
                v.tensor_tensor(on[:], A[:], over(ss[:, 2, :], P), ALU.mult).then_inc(o_ready, 1)
                v.wait_ge(o_turned, h1 + START)
                v.wait_ge(z_ready, h1 + START)
                v.tensor_tensor(oaT[:, bass.ds(h, 1), 0:TP].rearrange("p a n -> p (a n)"),
                                B[:].rearrange("p c n -> p (c n)"), zs[:, 0:TP], ALU.mult).then_inc(out_ready, 1)

            for k in range(KD):
                v.wait_ge(x_high, k + 1 + START)
                v.tensor_tensor(pair[1][:, k], hT[:, k], pair[0][:, k].bitcast(F32), ALU.subtract).then_inc(x_low, 1)
            v.wait_ge(padded, 3 + START)
            split_low(0, 0)
            split_low(0, 1)
            split_low(0, 2)
            for i in range(CONV_W):
                convolve(0, 0, i)
            split_low(0, 3)
            for n in range(1, 3):
                for i in range(CONV_W):
                    convolve(0, n, i)
            with v.Fori(0, H - 1) as h:
                rule(h, True)
            rule(H - 1, False)


def sparse_projections(nc, io, st):
    consts, ring = st["consts"], st["ring"]
    ident = consts[:, K_ID:K_ID + P]

    def copy_act(a, c, job, t, i):
        if i % 2 == 0:
            a.wait_ge(c.done, job.unit + 4 * t + i + 1 + START)
            a.activation(tile_of(job.out, 4 * t + i), c.view(0), ACT.Copy).then_inc(c.free[0], 1)

    def copy_dve(v, c, job, t, i):
        if i % 2:
            v.wait_ge(c.done, job.unit + 4 * t + i + 1 + START)
            v.tensor_copy(tile_of(job.out, 4 * t + i), c.view(1)).then_inc(c.free[1], 1)

    with Phase(nc, "gp") as ph:
        pair = [ph.sb(n, [P, KD, T], F32R) for n in ("xh", "xl")]
        jobs = [Job(columns(io["w_in"], C_Q), 2, pair, source=st["hT"], act=copy_act, dve=copy_dve),
                Job(columns(io["w_in"], C_KV), 3, pair, act=copy_act, dve=copy_dve)]
        jobs[0].out, jobs[1].out = st["qT"], st["kvT"]
        Chain(nc, "gqkv", ring, jobs, loaded=st["w_loaded"]["gqkv"])

    with Phase(nc, "kvr") as ph:
        rows = ph.sb("rows", [P, NCH, 12 * P])
        tail_rows = ph.sb("tail_rows", [11, CONV_T * P])
        slanted = ring[:].rearrange("p a k m -> p (a k m)")[:, 0:H * 2 * P]
        oh = ph.sb("oh", [NBK, B_COLS])
        rel = ph.sb("rel", [NBK, H])
        rel64 = ph.sb("rel64", [NBK, NB, H])
        vec = st["bias"][0:H, 0:2, :].rearrange("p a n -> p (a n)")[:, 0:B_S]
        vec_dram = nc.dram_tensor("bias_by_distance", [H, B_S], F32, kind="Internal")
        pt = ph.ps("pt", [P, 2, 4, 512])
        turned, emptied, tab_in, rel_in, masked, stored, vec_ready, vec_out, bias_in, biased, repeated, kept = (ph.sem(n) for n in (
            "turned", "emptied", "tab_in", "rel_in", "masked", "stored", "vec_ready", "vec_out", "bias_in", "biased",
            "repeated", "kept"))
        block = ph.block()
        NSTEP = 8

        @block.sync
        def _(sp):
            sp.dma_start(oh[:, 0:B_COLS], io["buckets"]).then_inc(tab_in, 16)
            sp.dma_start(rel[0:32, :], io["rel_bias"]).then_inc(rel_in, 16)
            sp.dma_start(io["s_conv"][0, :, 0:2, :], io["state_conv"][0, :, 1:3, :]).then_inc(stored, 16)
            for i in range(NCH):
                sp.wait_ge(emptied, i + 1 + START)
                for n, name in enumerate(("p_cmp", "p_sel", "p_win")):
                    sp.dma_start(io[name][0, 0, i * P:(i + 1) * P].rearrange("t c k d -> t (c k d)"),
                                 rows[:, i, n * 512:(n + 1) * 512]).then_inc(stored, 16)
            sp.wait_ge(emptied, 5 + START)
            for n, (name, at) in enumerate((("s_cmp", 0), ("s_sel", 0), ("s_win", TP - 1))):
                sp.dma_start(io[name][0, :, at].rearrange("b c k d -> b (c k d)"),
                             st["rows_s"][:, n * 512:(n + 1) * 512]).then_inc(stored, 16)
            sp.wait_ge(emptied, 7 + START)
            sp.dma_start(io["p_conv"].rearrange("a b j n -> (a b j) n"), tail_rows[0:3, :]).then_inc(stored, 16)
            sp.dma_start(io["s_conv"][0, :, 2, :], tail_rows[3:11, :]).then_inc(stored, 16)
            sp.wait_ge(vec_ready, 1 + START)
            sp.dma_start(vec_dram.ap(), vec).then_inc(vec_out, 16)
            sp.wait_ge(vec_out, 16 + START)
            sp.dma_start(slanted.rearrange("p (h k) -> p h k", h=H),
                         bass.AP(vec_dram, 0, [[1, P], [B_S, H], [1, 2 * P]])).then_inc(bias_in, 16)
            sp.wait_ge(stored, 16 * 18 + START)

        @block.scalar
        def _(a):
            a.dma_start(io["s_win"][0, :, 0:TP - 1], io["cache_win_kv"][0, :, 1:TP]).then_inc(kept, 16)
            a.wait_ge(kept, 16 + START)

        @block.tensor
        def _(pe):
            for s in range(7):
                bank = pt[:, s % 2].rearrange("p a n -> p (a n)")
                if s >= 2:
                    pe.wait_ge(emptied, s - 1 + START)
                if s < NCH:
                    for m in range(12):
                        last = pe.transpose(bank[:, m * P:(m + 1) * P], st["kvT"][:, m, s * P:(s + 1) * P], ident)
                elif s == NCH:
                    for m in range(12):
                        last = pe.transpose(bank[0:NB, m * P:(m + 1) * P], st["kvT"][:, m, TP:T], ident)
                else:
                    for m in range(12):
                        last = pe.transpose(bank[0:11, m * P:(m + 1) * P], st["tails"][:, (s - 5) * 12 + m, :], ident)
                last.then_inc(turned, 1)
            pe.wait_ge(tab_in, 16 + START)
            pe.wait_ge(rel_in, 16 + START)
            pe.wait_ge(masked, 1 + START)
            pe.wait_ge(repeated, 1 + START)
            pe.wait_ge(emptied, 6 + START)
            bank = pt[:, 1]
            pe.matmul(bank[0:H, 0, 0:B_S], rel[:], oh[:, B_R:B_R + B_S], start=True, stop=True)
            r64 = rel64[:].rearrange("p b h -> p (b h)")
            pe.matmul(bank[0:NR, 1, :], r64, oh[:, B_S:B_S + TP], start=True, stop=True)
            pe.matmul(bank[0:NR, 2, 0:2], r64, oh[:, B_S + TP:B_S + TP + 2], start=True, stop=True)
            pe.matmul(bank[0:NR, 2, 128:256], r64, oh[:, B_CS:B_CS + P], start=True, stop=True)
            for m in range(NCH * NBLK):
                last = pe.matmul(bank[:, 3, m * H:(m + 1) * H], oh[:, B_CP + m * P:B_CP + (m + 1) * P], rel[:],
                                 start=True, stop=True)
            last.then_inc(turned, 1)
            pe.wait_ge(bias_in, 16 + START)
            pe.wait_ge(emptied, 7 + START)
            for n in range(4):
                last = pe.matmul(pt[:, 0, n, :], consts[:, K_J:K_J + P], slanted[:, n * 512:(n + 1) * 512], start=True, stop=True)
            last.then_inc(turned, 1)

        @block.vector
        def _(v):
            v.memset(rel[32:33, :], MASKED).then_inc(masked, 1)
            for s in range(7):
                bank = pt[:, s % 2].rearrange("p a n -> p (a n)")
                v.wait_ge(turned, s + 1 + START)
                if s < NCH:
                    v.tensor_copy(rows[:, s, :], bank[:, 0:12 * P]).then_inc(emptied, 1)
                    v.wait_ge(emptied, s + 1 + START)
                    for n in range(2):
                        v.tensor_copy(st["vtok"][:, s, n, :], rows[:, s, 768 + 512 * n:1024 + 512 * n])
                elif s == NCH:
                    v.tensor_copy(st["rows_s"][:], bank[0:NB, 0:12 * P]).then_inc(emptied, 1)
                else:
                    v.tensor_copy(tail_rows[:, (s - 5) * 12 * P:(s - 4) * 12 * P], bank[0:11, 0:12 * P]).then_inc(emptied, 1)
            v.wait_ge(rel_in, 16 + START)
            v.wait_ge(masked, 1 + START)
            v.tensor_copy(rel64[:], each(rel[:], NB)).then_inc(repeated, 1)
            v.wait_ge(turned, 8 + START)
            bank = pt[:, 1]
            v.tensor_copy(vec, bank[0:H, 0, 0:B_S]).then_inc(vec_ready, 1)
            v.tensor_copy(st["bias_s"][:, 0:TP], bank[0:NR, 1, :])
            v.tensor_copy(st["bias_s"][:, TP:TP + 1], bank[0:NR, 2, 0:1])
            v.tensor_tensor(st["bias_cs"][:], bank[0:NR, 2, 128:256], consts[0:NR, K_X:K_X + P], ALU.add)
            v.tensor_copy(st["bias_c"][:], bank[:, 3, 0:256].rearrange("p (m h) -> p h m", h=H)).then_inc(biased, 1)
            v.wait_ge(turned, 9 + START)
            v.tensor_copy(st["bias"][:].rearrange("p h k -> p (h k)"), pt[:, 0].rearrange("p a n -> p (a n)")).then_inc(biased, 1)


def compress(nc, io, st):
    consts, kvT = st["consts"], st["kvT"]
    ident = consts[:, K_ID:K_ID + P]
    LC = 8
    with Phase(nc, "cmp") as ph:
        table = ph.sb("table", [1, NB * NPAGE], I32)
        spare = st["obT"][:].rearrange("p h t -> p (h t)")
        low_slots = spare[:, 0:2048].rearrange("p (s n m) -> p s n m", s=2, n=NPAGE)
        pages = [low_slots[:, 0], low_slots[:, 1], st["ring"][:, 0, KD // 2:KD, :], st["ring"][:, 1, KD // 2:KD, :]]
        w2 = spare[:, 2048:2304].rearrange("p (c m) -> p c m", c=2)
        pe_rows = spare[0:BLK, 2304:2560].rearrange("p (c m) -> p c m", c=2)
        cT = ph.sb("cT", [P, BLK, ROWS + 1])
        w1 = st["ring"][:, :, 0:LC // 2, :].rearrange("p s k (m f) -> p s (k m) f", f=P)
        hidden = ph.sb("hidden", [P, ROWS])
        pe_term = ph.sb("pe_term", [P, 1])
        ptr = ph.ps("ptr", [P, 2, 2, 512])
        pm = ph.ps("pm", [P, 512])
        pk = ph.ps("pk", [P, 512])
        pp = ph.ps("pp", [P, 512])
        table_in, small_in, turned, spread, pe_turned, pe_ready, mixed, term, hid, outp, outc = (ph.sem(n) for n in (
            "table_in", "small_in", "turned", "spread", "pe_turned", "pe_ready", "mixed", "term", "hid", "outp", "outc"))
        page_in = [ph.sem(f"page_in{i}") for i in range(4)]
        w_in = [ph.sem(f"w_in{i}") for i in range(2)]
        used = ph.sem("used")
        block = ph.block()

        def load_pages(eng, c, r, slots):
            for s in slots:
                if 2 * c + r:
                    eng.wait_ge(turned, NB * c + 4 * r + s - 3 + START)
                for n in range(NPAGE):
                    at = (4 * r + s) * NPAGE + n
                    page = eng.value_load(table[0:1, at:at + 1], min_val=0, max_val=39)
                    eng.dma_start(pages[s][:, n, :], io["cache_cmp_kv"][0, bass.ds(page, 1), :, c].rearrange(
                        "a t k d -> t (a k d)")).then_inc(page_in[s], 16)

        @block.sync
        def _(sp):
            sp.dma_start(table[:], io["page_table"].rearrange("b n -> (b n)").unsqueeze(0)).then_inc(table_in, 16)
            sp.dma_start(w2, io["cmp_w2"][0].rearrange("c f d -> f c d")).then_inc(small_in, 16)
            sp.dma_start(pe_rows, io["cmp_pe"][0]).then_inc(small_in, 16)
            sp.wait_ge(table_in, 16 + START)
            for c in range(2):
                for r in range(NB // 4):
                    load_pages(sp, c, r, (0, 1))

        @block.scalar
        def _(a):
            def load(c, i):
                n = c * 8 + i
                if n >= 2:
                    a.wait_ge(used, n - 1 + START)
                a.dma_start(w1[:, n % 2], io["cmp_w1"][0, c, i * LC:(i + 1) * LC].rearrange("l d f -> d l f"))\
                    .then_inc(w_in[n % 2], 16)

            for c in range(2):
                if c:
                    load_pages(a, 1, 0, (2, 3))
                load(c, 0)
                load(c, 1)
                if c == 0:
                    a.wait_ge(table_in, 16 + START)
                    load_pages(a, 0, 0, (2, 3))
                load_pages(a, c, 1, (2, 3))
                for i in range(2, 8):
                    load(c, i)
                a.wait_ge(term, c + 1 + START)
                a.activation(hidden[:], pm[:, 0:ROWS], ACT.Silu, bias=pe_term[:]).then_inc(hid, 1)

        @block.tensor
        def _(pe):
            pe.wait_ge(small_in, 32 + START)
            for c in range(2):
                pe.transpose(pp[:, 64 * c:64 * c + 64], pe_rows[:, c, :], consts[0:BLK, K_ID:K_ID + BLK]).then_inc(pe_turned, 1)
            for c in range(2):
                with pe.Fori(0, NB // 4) as r:
                    for s in range(4):
                        pe.wait_ge(page_in[s], 64 * (NB // 4 * c + r) + 64 + START)
                        pe.wait_ge(spread, (NB * c + 4 * r + s // 2 * 2 if s < 2 else NB * c + 4 * r + s - 1) + START)
                        for k in range(KV):
                            for n in range(NPAGE):
                                last = pe.transpose(ptr[:, s % 2, k, n * P:(n + 1) * P], pages[s][:, n, k * P:(k + 1) * P], ident)
                        last.then_inc(turned, 1)
                pe.wait_ge(spread, NB * (c + 1) + START)
                pe.wait_ge(pe_ready, c + 1 + START)
                for i in range(8):
                    n = c * 8 + i
                    pe.wait_ge(w_in[n % 2], 16 * (n // 2) + 16 + START)
                    for j in range(LC):
                        l = i * LC + j
                        last = pe.matmul(pm[:, 0:ROWS + 1], w1[:, n % 2, j, :], cT[:, l, :], start=(l == 0), stop=(l == BLK - 1))
                    last.then_inc(used, 1)
                last = None
                pe.wait_ge(hid, c + 1 + START)
                if c == 0:
                    pe.matmul(pk[:, 0:ROWS], w2[:, 0, :], hidden[:], start=True, stop=True).then_inc(outp, 1)
                else:
                    pe.wait_ge(outc, 1 + START)
                    pe.matmul(pk[:, 0:P], hidden[:, 0:P], w2[:, 1, :], start=True, stop=True)
                    pe.matmul(pk[0:16, P:2 * P], hidden[:, P:ROWS], w2[:, 1, :], start=True, stop=True).then_inc(outp, 1)

        @block.vector
        def _(v):
            for c in range(2):
                if c:
                    v.wait_ge(used, 8 + START)
                v.wait_ge(pe_turned, 2 + START)
                v.tensor_copy(cT[:, :, ROWS:ROWS + 1], pp[:, 64 * c:64 * c + 64].unsqueeze(2))
                for k in range(KV):
                    at = NB * KV * NBLK + k * NBLK
                    last = v.tensor_copy(cT[:, :, at:at + NBLK], kvT[:, 2 * c + k, 0:TP].rearrange("p (n l) -> p l n", l=BLK))
                last.then_inc(pe_ready, 1)
                with v.Fori(0, NB // 2) as r:
                    for s in range(2):
                        v.wait_ge(turned, NB * c + 2 * r + s + 1 + START)
                        for k in range(KV):
                            ins = v.tensor_copy(cT[:, :, bass.ds((2 * r + s) * 16 + k * NBLK, NBLK)],
                                                ptr[:, s, k, :].rearrange("p (n l) -> p l n", l=BLK))
                        ins.then_inc(spread, 1)
                v.wait_ge(used, 8 * (c + 1) + START)
                if c:
                    v.wait_ge(hid, 1 + START)
                v.tensor_copy(pe_term[:], pm[:, ROWS:ROWS + 1]).then_inc(term, 1)
                v.wait_ge(outp, c + 1 + START)
                if c == 0:
                    v.tensor_copy(st["kcT"][:], pk[:, 0:ROWS]).then_inc(outc, 1)
                else:
                    v.tensor_copy(st["vc_s"][:], pk[:, 0:P])
                    v.tensor_copy(st["vc_p"][:], pk[0:16, P:2 * P]).then_inc(outc, 1)


def prompt_attention(nc, io, st):
    consts, qT, kvT, obT = st["consts"], st["qT"], st["kvT"], st["obT"]
    ident = consts[:, K_ID:K_ID + P]
    NU = KV * 2 * NCH
    RING = 4
    with Phase(nc, "att") as ph:
        qs = ph.sb("qs", [P, KV, TP])
        lg = ph.sb("lg", [P, RING, TP])
        PT = ph.sb("PT", [P, 2, NCH, TP])
        nm, sm, rc = (ph.sb(n, [P, RING]) for n in ("nm", "sm", "rc"))
        lc = ph.sb("lc", [P, KV, NCH * NBLK])
        cm, cs = (ph.sb(n, [P, KV * NCH]) for n in ("cm", "cs"))
        pc = ph.sb("pc", [P, KV, NCH, 2 * NBLK])
        pcT = ph.sb("pcT", [2 * NBLK, KV, TP])
        pS = ph.ps("pS", [P, 2, TP])
        pT = ph.ps("pT", [P, 2, NCH, P])
        pO = ph.ps("pO", [P, TP])
        pC = ph.ps("pC", [P, KV, NCH, NBLK])
        pCT = ph.ps("pCT", [2 * NBLK, KV, TP])

        def sems(*names):
            return [ph.sem(n) for n in names]

        q_ready, zeroed, s_done, lg_ready, mx_ready, e_ready, r_ready, p_ready, p_turned, pt_ready, pv_done, o_ready = sems(
            "q_ready", "zeroed", "s_done", "lg_ready", "mx_ready", "e_ready", "r_ready", "p_ready", "p_turned", "pt_ready",
            "pv_done", "o_ready")
        c_done, c_step, c_exp, c_ready, c_turned, c_kept, rc_step, rowmax, c_sum = sems(
            "c_done", "c_step", "c_exp", "c_ready", "c_turned", "c_kept", "rc_step", "rowmax", "c_sum")
        block = ph.block()
        units = [(kv, br, i) for kv in range(KV) for br in range(2) for i in range(NCH)]
        keys = {0: 4, 1: 8}

        @block.gpsimd
        def _(e):
            e.memset(pc[:], 0.0).then_inc(zeroed, 1)
            with e.Fori(0, G) as g:
                e.wait_ge(pv_done, 4 * g + START)
                for kv in range(KV):
                    e.tensor_copy(qs[:, kv, :], qT[:, bass.ds(kv * G + g, 1), 0:TP].rearrange("p a n -> p (a n)"))\
                        .then_inc(q_ready, 1)

        @block.tensor
        def _(pe):
            with pe.Fori(0, G) as g:
                def scores(n):
                    kv, br, i = units[n]
                    if n >= 2:
                        pe.wait_ge(lg_ready, NU * g + n - 1 + START)
                    pe.matmul(pS[:, n % 2, 0:(i + 1) * P], qs[:, kv, i * P:(i + 1) * P],
                              kvT[:, keys[br] + kv, 0:(i + 1) * P], start=True, stop=True).then_inc(s_done, 1)

                def turn(n):
                    kv, br, i = units[n]
                    pe.wait_ge(p_ready, NU * g + n + 1 + START)
                    pe.wait_ge(pt_ready, NU * g + max(n - 1, 0) + START)
                    for j in range(i + 1):
                        last = pe.transpose(pT[:, n % 2, j, :], lg[:, n % RING, j * P:(j + 1) * P], ident)
                    last.then_inc(p_turned, 1)

                def values(m):
                    kv, br = m // 2, m % 2
                    if br == 0:
                        pe.wait_ge(c_kept, g + 1 + START)
                        pe.wait_ge(o_ready, KV * g + kv + START)
                        pe.matmul(pO[:], st["vc_p"][:], pcT[:, kv, :], start=True, stop=False)
                    pe.wait_ge(pt_ready, NU * g + NCH * (m + 1) + START)
                    for j in range(NCH):
                        last = pe.matmul(pO[:, j * P:TP], st["vtok"][:, j, br, kv * P:(kv + 1) * P],
                                         PT[:, m % 2, j, j * P:TP], start=False, stop=(br == 1 and j == NCH - 1))
                    last.then_inc(pv_done, 1)

                pe.wait_ge(q_ready, KV * g + KV + START)
                for kv in range(KV):
                    at = NB * KV * NBLK + kv * NBLK
                    for i in range(NCH):
                        last = pe.matmul(pC[:, kv, i, :], qs[:, kv, i * P:(i + 1) * P], st["kcT"][:, at:at + NBLK],
                                         start=True, stop=True)
                last.then_inc(c_done, 1)
                scores(0)
                scores(1)
                for n in range(NU):
                    if n + 2 < NU:
                        scores(n + 2)
                    if n == 1:
                        pe.wait_ge(c_ready, g + 1 + START)
                        for kv in range(KV):
                            for i in range(NCH):
                                last = pe.transpose(pCT[:, kv, i * P:(i + 1) * P], pc[:, kv, i, :], ident)
                        last.then_inc(c_turned, 1)
                    turn(n)
                    if n and n % NCH == 0:
                        values(n // NCH - 1)
                values(NU // NCH - 1)

        @block.scalar
        def _(a):
            with a.Fori(0, G) as g:
                def exps(n):
                    i = units[n][2]
                    w = (i + 1) * P
                    a.wait_ge(mx_ready, NU * g + n + 1 + START)
                    a.activation(lg[:, n % RING, 0:w], lg[:, n % RING, 0:w], ACT.Exp, bias=nm[:, n % RING:n % RING + 1],
                                 accum_out=sm[:, n % RING:n % RING + 1]).then_inc(e_ready, 1)

                def scale(n):
                    w = (units[n][2] + 1) * P
                    a.wait_ge(r_ready, NU * g + n + 1 + START)
                    a.activation(lg[:, n % RING, 0:w], lg[:, n % RING, 0:w], ACT.Copy, scale=rc[:, n % RING:n % RING + 1])\
                        .then_inc(p_ready, 1)

                a.wait_ge(c_step, 3 * g + 2 + START)
                a.activation(lc[:], lc[:], ACT.Exp).then_inc(c_exp, 1)
                exps(0)
                for n in range(NU):
                    if n + 1 < NU:
                        exps(n + 1)
                    scale(n)
                    if n == 2:
                        a.wait_ge(c_turned, g + 1 + START)
                        a.activation(pcT[:], pCT[:], ACT.Copy).then_inc(c_kept, 1)
                    if n in (NU // 2 + 1, NU - 1):
                        kv = 0 if n < NU - 1 else 1
                        a.wait_ge(pv_done, 4 * g + 2 * kv + 2 + START)
                        a.activation(obT[:, bass.ds(kv * G + g, 1), 0:TP].rearrange("p a n -> p (a n)"), pO[:], ACT.Copy)\
                            .then_inc(o_ready, 1)

        @block.vector
        def _(v):
            v.wait_ge(zeroed, 1 + START)
            with v.Fori(0, G) as g:
                def logits(n):
                    kv, br, i = units[n]
                    b = st["bias"][:, bass.ds(kv * G + g, 1), :].rearrange("p a n -> p (a n)")
                    row = lg[:, n % RING]
                    v.wait_ge(s_done, NU * g + n + 1 + START)
                    v.wait_ge(p_turned, NU * g + max(n - RING + 1, 0) + START)
                    lo = max(i - 1, 0) * P
                    if i >= 2:
                        v.tensor_scalar(row[:, 0:lo], pS[:, n % 2, 0:lo], SCALE, b[:, 0:1], ALU.mult, ALU.add)
                    v.scalar_tensor_tensor(row[:, lo:(i + 1) * P], pS[:, n % 2, lo:(i + 1) * P], SCALE,
                                           b[:, (P if i == 0 else 0):2 * P], ALU.mult, ALU.add).then_inc(lg_ready, 1)
                    v.wait_ge(lg_ready, NU * g + n + 1 + START)
                    v.tensor_reduce(nm[:, n % RING:n % RING + 1], row[:, 0:(i + 1) * P], AX.X, ALU.max, negate=True)\
                        .then_inc(mx_ready, 1)

                def factor(n):
                    kv, br, i = units[n]
                    v.wait_ge(e_ready, NU * g + n + 1 + START)
                    v.reciprocal(rc[:, n % RING:n % RING + 1], sm[:, n % RING:n % RING + 1]).then_inc(rc_step, 1)
                    v.wait_ge(rc_step, NU * g + n + 1 + START)
                    v.tensor_tensor(rc[:, n % RING:n % RING + 1], rc[:, n % RING:n % RING + 1],
                                    st["gates"][:, i, bass.ds((br + 1) * H + kv * G + g, 1)], ALU.mult).then_inc(r_ready, 1)

                def keep(n):
                    kv, br, i = units[n]
                    m = n // NCH
                    v.wait_ge(p_turned, NU * g + n + 1 + START)
                    v.wait_ge(pv_done, 4 * g + max(m - 1, 0) + START)
                    v.tensor_copy(PT[:, m % 2, 0:i + 1, i * P:(i + 1) * P], pT[:, n % 2, 0:i + 1, :]).then_inc(pt_ready, 1)

                v.wait_ge(c_done, g + 1 + START)
                bc = st["bias_c"][:].rearrange("p (k g) m -> p k g m", k=KV)[:, :, bass.ds(g, 1), :].rearrange("p k a m -> p k (a m)")
                v.scalar_tensor_tensor(lc[:], pC[:].rearrange("p k i n -> p k (i n)"), SCALE, bc, ALU.mult, ALU.add).then_inc(c_step, 1)
                v.wait_ge(c_step, 3 * g + 1 + START)
                l8 = lc[:].rearrange("p k (i n) -> p (k i) n", n=NBLK)
                v.tensor_reduce(cm[:], l8, AX.X, ALU.max).then_inc(rowmax, 1)
                v.wait_ge(rowmax, g + 1 + START)
                v.tensor_tensor(l8, l8, over(cm[:], NBLK), ALU.subtract).then_inc(c_step, 1)
                logits(0)
                logits(1)
                v.wait_ge(c_exp, g + 1 + START)
                v.tensor_reduce(cs[:], l8, AX.X, ALU.add).then_inc(c_sum, 1)
                v.wait_ge(c_sum, 3 * g + 1 + START)
                v.reciprocal(cs[:], cs[:]).then_inc(c_sum, 1)
                v.wait_ge(c_sum, 3 * g + 2 + START)
                gc = st["gates"][:, 0:NCH, 0:H].rearrange("p i (k g) -> p k i g", k=KV)[:, :, :, bass.ds(g, 1)].rearrange(
                    "p k i a -> p k (i a)")
                v.tensor_tensor(cs[:].rearrange("p (k i) -> p k i", k=KV), cs[:].rearrange("p (k i) -> p k i", k=KV), gc,
                                ALU.mult).then_inc(c_sum, 1)
                v.wait_ge(c_sum, 3 * g + 3 + START)
                first = cs[:].rearrange("p (k i) -> p k i", k=KV)[:, :, 0]
                v.tensor_scalar(first, first, consts[:, K_RV:K_RV + 1], None, ALU.mult).then_inc(c_step, 1)
                v.wait_ge(c_step, 3 * g + 3 + START)
                for kv in range(KV):
                    last = v.tensor_tensor(pc[:, kv, :, kv * NBLK:(kv + 1) * NBLK], l8[:, kv * NCH:(kv + 1) * NCH, :],
                                           over(cs[:, kv * NCH:(kv + 1) * NCH], NBLK), ALU.mult)
                last.then_inc(c_ready, 1)
                for n in range(NU):
                    factor(n)
                    if n + 2 < NU:
                        logits(n + 2)
                    if n:
                        keep(n - 1)
                keep(NU - 1)


def request_delta(nc, io, st):
    consts, qkv = st["consts"], st["qkv_s"]
    ones = consts[:, K_ONE:K_ONE + P]
    with Phase(nc, "rd") as ph:
        S = ph.sb("S", [P, NR, P])
        sq, rt, qk = (ph.sb(n, [P, 2, NR]) for n in ("sq", "rt", "qk"))
        ab8 = ph.sb("ab8", [NB, 2, NR])
        ab = ph.sb("ab", [P, 2, NR])
        prod, t1, vnew, bv, o, kq = (ph.sb(n, [P, NR]) for n in ("prod", "t1", "vnew", "bv", "o", "kq"))
        krow, vrow = (ph.sb(n, [NR, P]) for n in ("krow", "vrow"))
        spread = ph.sb("spread", [NR, 2, 4, P])
        p1 = ph.ps("p1", [P, 512])
        p2 = ph.ps("p2", [P, 512])
        p3 = ph.ps("p3", [P, NR, 2])
        p4 = ph.ps("p4", [P, 512])
        pu = ph.ps("pu", [P, 2, 4, P])
        state_in, step, root, mm, stored = (ph.sem(n) for n in ("state_in", "step", "root", "mm", "stored"))
        spread_ready, outer, updated = ([ph.sem(f"{n}{s}") for s in range(2)] for n in ("spread_ready", "outer", "updated"))
        block = ph.block()

        @block.sync
        def _(sp):
            for b in range(NB):
                sp.dma_start(S[:, b * H:(b + 1) * H], io["state_delta"][0, b].rearrange("h k v -> k h v"))\
                    .then_inc(state_in, 16)
            first_loads(sp, st, "gqkv", columns(io["w_in"], C_Q))
            for n in range(2):
                for s in range(2):
                    sp.wait_ge(updated[s], 16 * (n + 1) + START)
                sp.dma_start(io["s_delta"][0, n * 4:(n + 1) * 4].rearrange("b h k v -> k (b h) v"),
                             S[:, n * 32:(n + 1) * 32]).then_inc(stored, 16)
            sp.wait_ge(stored, 32 + START)

        @block.tensor
        def _(pe):
            pe.wait_ge(step, 1 + START)
            pe.matmul(p1[:, 0:P], ones, sq[:].rearrange("p a r -> p (a r)"), start=True, stop=True).then_inc(mm, 1)
            pe.wait_ge(step, 3 + START)
            pe.matmul(p2[:, 0:P], consts[0:NB, K_ONE:K_ONE + P], ab8[:].rearrange("p a r -> p (a r)"),
                      start=True, stop=True).then_inc(mm, 1)
            pe.wait_ge(step, 8 + START)
            pe.matmul(p1[:, 0:NR], ones, prod[:], start=True, stop=True).then_inc(mm, 1)
            pe.wait_ge(state_in, 16 * NB + START)
            for r in range(NR):
                last = pe.matmul(p3[:, r, :], S[:, r, :], qk[:, :, r], start=True, stop=True)
            last.then_inc(mm, 1)
            pe.wait_ge(step, 13 + START)
            pe.transpose(p4[0:NR, 0:P], qk[:, 1, :], consts[:, K_ID:K_ID + P])
            pe.transpose(p4[0:NR, P:2 * P], bv[:], consts[:, K_ID:K_ID + P]).then_inc(mm, 1)
            pe.wait_ge(step, 17 + START)
            pe.matmul(p1[:, 0:NR], ones, prod[:], start=True, stop=True).then_inc(mm, 1)
            with pe.Fori(0, 8) as j:
                for s in range(2):
                    pe.wait_ge(spread_ready[s], j + 1 + START)
                    pe.wait_ge(updated[s], 4 * j + START)
                    pe.matmul(pu[:, s].rearrange("p a n -> p (a n)"), krow[:], spread[:, s].rearrange("p a n -> p (a n)"),
                              start=True, stop=True).then_inc(outer[s], 1)

        @block.scalar
        def _(a):
            a.wait_ge(step, 4 + START)
            a.activation(rt[:], rt[:], ACT.Sqrt).then_inc(root, 1)
            a.wait_ge(step, 18 + START)
            a.activation(rt[:, 0, :], rt[:, 0, :], ACT.Sqrt).then_inc(root, 1)

        @block.vector
        def _(v):
            def did(ins, n):
                ins.then_inc(step, 1)
                v.wait_ge(step, n + START)

            did(v.tensor_tensor(sq[:], qkv[:, 0:2].rearrange("p a b h -> p a (b h)"),
                                qkv[:, 0:2].rearrange("p a b h -> p a (b h)"), ALU.mult), 1)
            e8 = consts[0:NB, K_E8:K_E8 + NR].rearrange("p (b h) -> p b h", h=H)
            did(v.tensor_tensor(ab8[:, 0].rearrange("p (b h) -> p b h", h=H), e8, each(st["es"][0:NB, :], NB), ALU.mult), 2)
            did(v.tensor_tensor(ab8[:, 1].rearrange("p (b h) -> p b h", h=H), e8, each(st["beta"][0:NB, NCH, :], NB), ALU.mult), 3)
            v.wait_ge(mm, 1 + START)
            did(v.tensor_scalar(rt[:].rearrange("p a r -> p (a r)"), p1[:, 0:P], EPS, None, ALU.add), 4)
            v.wait_ge(root, 1 + START)
            did(v.reciprocal(rt[:], rt[:]), 5)
            did(v.scalar_tensor_tensor(qk[:, 0, :], qkv[:, 0].rearrange("p b h -> p (b h)"), SCALE, rt[:, 0, :], ALU.mult, ALU.mult), 6)
            did(v.tensor_tensor(qk[:, 1, :], qkv[:, 1].rearrange("p b h -> p (b h)"), rt[:, 1, :], ALU.mult), 7)
            did(v.tensor_tensor(prod[:], qk[:, 0, :], qk[:, 1, :], ALU.mult), 8)
            v.wait_ge(mm, 3 + START)
            v.tensor_copy(ab[:].rearrange("p a r -> p (a r)"), p2[:, 0:P])
            did(v.tensor_copy(kq[:], p1[:, 0:NR]), 9)
            v.wait_ge(mm, 4 + START)
            did(v.tensor_tensor(t1[:], p3[:, :, 1], ab[:, 0, :], ALU.mult), 10)
            did(v.tensor_tensor(vnew[:], qkv[:, 2].rearrange("p b h -> p (b h)"), t1[:], ALU.subtract), 11)
            did(v.tensor_tensor(bv[:], vnew[:], ab[:, 1, :], ALU.mult), 12)
            did(v.tensor_tensor(o[:], p3[:, :, 0], ab[:, 0, :], ALU.mult), 13)
            did(v.tensor_tensor(t1[:], kq[:], bv[:], ALU.mult), 14)
            did(v.tensor_tensor(o[:], o[:], t1[:], ALU.add), 15)
            v.wait_ge(mm, 5 + START)
            v.tensor_copy(krow[:], p4[0:NR, 0:P])
            did(v.tensor_copy(vrow[:], p4[0:NR, P:2 * P]), 16)
            did(v.tensor_tensor(prod[:], o[:], o[:], ALU.mult), 17)
            v.wait_ge(mm, 6 + START)
            did(v.tensor_scalar(rt[:, 0, :], p1[:, 0:NR], 1.0 / P, EPS, ALU.mult, ALU.add), 18)
            v.wait_ge(root, 2 + START)
            did(v.reciprocal(rt[:, 0, :], rt[:, 0, :]), 19)
            did(v.tensor_tensor(o[:], o[:], rt[:, 0, :], ALU.mult), 20)
            did(v.tensor_tensor(st["oaT"][:, :, TP:T], o[:].rearrange("p (b h) -> p h b", h=H),
                                st["z_s"][:].rearrange("p b h -> p h b"), ALU.mult), 21)

            with v.Fori(0, 8) as j:
                for s in range(2):
                    v.wait_ge(outer[s], j + 1 + START)
                    for n in range(4):
                        r = 8 * j + 4 * s + n
                        row = S[:, bass.ds(r, 1), :].rearrange("p a n -> p (a n)")
                        v.scalar_tensor_tensor(row, row, ab[:, 0, bass.ds(r, 1)], pu[:, s, n, :], ALU.mult, ALU.add)\
                            .then_inc(updated[s], 1)

        @block.gpsimd
        def _(p):
            p.wait_ge(step, 16 + START)
            with p.Fori(0, 8) as j:
                for s in range(2):
                    p.wait_ge(outer[s], j + START)
                    p.tensor_tensor(spread[:, s], over(consts[0:NR, bass.ds(8 * j + 4 * s, 4)], P), each(vrow[:], 4),
                                    ALU.mult).then_inc(spread_ready[s], 1)


def request_attention(nc, io, st):
    consts, qT = st["consts"], st["qT"]
    ident = consts[:, K_ID:K_ID + P]
    with Phase(nc, "ra") as ph:
        table = ph.sb("table", [1, NB * NPAGE], I32)
        K = ph.sb("K", [P, 4, NPAGE, KV * P])
        KT = ph.sb("KT", [P, 2, KV, TP])
        V = ph.sb("V", [P, 2, NB, NPAGE, KV * P])
        qc = ph.sb("qc", [P, NR])
        qrow = ph.sb("qrow", [NR, P])
        new = ph.sb("new", [NR, 4, P])
        tmp = ph.sb("tmp", [NR, 4, P])
        snew = ph.sb("snew", [NR, 2])
        gr = ph.sb("gr", [NR, 3])
        gm = ph.sb("gm", [NR, 3, H])
        ST = ph.sb("ST", [P, NPAGE, NR])
        lg = ph.sb("lg", [NR, 2, TP + 1])
        lc = ph.sb("lc", [NR, P])
        mx, sm = (ph.sb(n, [NR, 3]) for n in ("mx", "sm"))
        PT = ph.sb("PT", [P, 2, NPAGE, NR])
        PcT = ph.sb("PcT", [P, NR])
        dg = ph.sb("dg", [NR, 2, NR])
        pK = ph.ps("pK", [P, 2, KV, TP])
        pS = ph.ps("pS", [P, NPAGE, NR])
        pA = ph.ps("pA", [P, 512])
        pB = ph.ps("pB", [NR, 512])
        pO = ph.ps("pO", [P, 512])
        rows_o = K[0:G, 0:2].rearrange("p i n (r d) -> p i (n r) d", d=P)
        pR = pK[0:G].rearrange("p i k t -> p (i k t)").rearrange("p (i b k d) -> p i b k d", i=2, b=4, k=KV)
        rows_done, rows_kept = ph.sem("rows_done"), ph.sem("rows_kept")
        table_in, q_ready, mm, step, turned, kept, scored, e_done, v_in = (ph.sem(n) for n in (
            "table_in", "q_ready", "mm", "step", "turned", "kept", "scored", "e_done", "v_in"))
        k_in = [ph.sem(f"k_in{i}") for i in range(4)]
        block = ph.block()

        def kv_load(eng, dst, br, b, c, sem):
            if br == 0:
                for n in range(NPAGE):
                    page = eng.value_load(table[0:1, bass.ds(b * NPAGE + n, 1)], min_val=0, max_val=39)
                    eng.dma_start(dst[:, n, :], io["cache_sel_kv"][0, bass.ds(page, 1), :, c].rearrange(
                        "a t k d -> t (a k d)")).then_inc(sem, 16)
            else:
                eng.dma_start(dst, io["cache_win_kv"][0, bass.ds(b, 1), :, c].rearrange(
                    "a (n t) k d -> t (a n) (k d)", n=NPAGE)).then_inc(sem, 16)

        @block.sync
        def _(sp):
            sp.dma_start(table[:], io["page_table"].rearrange("b n -> (b n)").unsqueeze(0)).then_inc(table_in, 16)
            sp.wait_ge(table_in, 16 + START)
            for br in range(2):
                with sp.Fori(0, NB // 4) as r:
                    for s in range(4):
                        if br == 0:
                            sp.wait_ge(turned, 4 * r + START)
                        else:
                            sp.wait_ge(turned, NB + 4 * r + s - 3 + START)
                        kv_load(sp, K[:, s], br, 4 * r + s, 0, k_in[s])
            first_loads(sp, st, "mix", columns(io["w_in"], C_M))

        @block.scalar
        def _(a):
            a.wait_ge(table_in, 16 + START)
            def weigh(x, at, n):
                a.wait_ge(step, n + START)
                a.activation(x, x, ACT.Exp, bias=mx[:, at:at + 1], accum_out=sm[:, at:at + 1]).then_inc(e_done, 1)

            weigh(lc[:], 2, 10)
            for br in range(2):
                with a.Fori(0, NB) as b:
                    a.wait_ge(turned, NB * br + b + START)
                    kv_load(a, V[:, br, bass.ds(b, 1)].rearrange("p a n m -> p (a n) m"), br, b, 1, v_in)
                weigh(lg[:, br, :], br, 17 + 9 * br)

        @block.tensor
        def _(pe):
            e8 = consts[0:NB, K_E8:K_E8 + NR]
            pe.matmul(pB[:, 0:3 * H], e8, st["gates"][0:NB, NCH, :], start=True, stop=True).then_inc(mm, 1)
            pe.wait_ge(q_ready, 1 + START)
            pe.wait_ge(step, 1 + START)
            pe.transpose(pA[0:NR, 0:P], qc[:], ident).then_inc(mm, 1)
            pe.matmul(pK[0:NR, 0, 0, :], e8, st["rows_s"][:, 512:1024], start=True, stop=True)
            pe.matmul(pK[0:NR, 0, 1, :], e8, st["rows_s"][:, 1024:1536], start=True, stop=True).then_inc(mm, 1)
            pe.matmul(pB[:, 0:P], qc[:], st["kcT"][:, 0:P], start=True, stop=True).then_inc(mm, 1)
            pe.wait_ge(step, 11 + START)
            pe.wait_ge(step, 12 + START)
            pe.transpose(pA[:, 0:NR], lc[:], consts[0:NR, K_ID:K_ID + NR]).then_inc(mm, 1)
            pe.wait_ge(step, 13 + START)
            for br in range(2):
                with pe.Fori(0, NB // 4) as r:
                    for s in range(5):
                        if s < 4:
                            pe.wait_ge(k_in[s], (64 * r + 64 if br == 0 else 64 * (NB // 4) + 16 * r + 16) + START)
                            pe.wait_ge(kept, NB * br + 4 * r + max(s - 1, 0) + START)
                            for k in range(KV):
                                for n in range(NPAGE):
                                    last = pe.transpose(pK[:, s % 2, k, n * P:(n + 1) * P], K[:, s, n, k * P:(k + 1) * P], ident)
                            last.then_inc(turned, 1)
                        if s:
                            b = 4 * r + s - 1
                            pe.wait_ge(kept, NB * br + b + 1 + START)
                            for k in range(KV):
                                for n in range(NPAGE):
                                    last = pe.matmul(pS[:, n, bass.ds(b * H + k * G, G)], KT[:, (s - 1) % 2, k, n * P:(n + 1) * P],
                                                     qc[:, bass.ds(b * H + k * G, G)], start=True, stop=True)
                            last.then_inc(scored, 1)
                pe.wait_ge(step, 14 + 9 * br + START)
                for n in range(NPAGE):
                    last = pe.transpose(pB[:, n * P:(n + 1) * P], ST[:, n, :], ident)
                last.then_inc(mm, 1)
                pe.wait_ge(step, 20 + 9 * br + START)
                for n in range(NPAGE):
                    last = pe.transpose(pA[:, n * NR:(n + 1) * NR], lg[:, br, n * P:(n + 1) * P], consts[0:NR, K_ID:K_ID + NR])
                last.then_inc(mm, 1)
            pe.wait_ge(step, 31 + START)
            pe.wait_ge(v_in, 16 * NB * (NPAGE + 1) + START)
            pe.matmul(pO[:, 0:NR], st["vc_s"][:], PcT[:], start=True, stop=False)
            for br in range(2):
                pe.matmul(pO[:, 0:NR], new[:, 2 * br + 1, :], dg[:, br, :], start=False, stop=False)
            for b in range(NB):
                for k in range(KV):
                    at = b * H + k * G
                    for br in range(2):
                        for n in range(NPAGE):
                            last = pe.matmul(pR[:, b // 4, b % 4, k], PT[:, br, n, at:at + G], V[:, br, b, n, k * P:(k + 1) * P],
                                             start=(br == 0 and n == 0), stop=(br == 1 and n == NPAGE - 1))
                if b % 4 == 3:
                    last.then_inc(rows_done, 1)
            for i in range(2):
                pe.wait_ge(rows_kept, i + 1 + START)
                for r in range(NB):
                    at = (i * NB + r) * G
                    last = pe.matmul(pO[:, at:at + G], rows_o[:, i, r, :], consts[0:G, K_ID:K_ID + G],
                                     start=False, stop=(i == 1 and r == NB - 1))
            last.then_inc(mm, 1)

        @block.vector
        def _(v):
            def did(ins, n):
                ins.then_inc(step, 1)
                v.wait_ge(step, n + START)

            kvm = consts[0:NR, K_KVM:K_KVM + KV]
            v.tensor_copy(qc[:].rearrange("p (b h) -> p b h", h=H), qT[:, :, TP:T].rearrange("p h b -> p b h")).then_inc(q_ready, 1)
            v.wait_ge(mm, 1 + START)
            did(v.tensor_tensor(gm[:], pB[:, 0:3 * H].rearrange("p (a h) -> p a h", h=H),
                                each(consts[0:NR, K_HM:K_HM + H], 3), ALU.mult), 1)
            did(v.tensor_reduce(gr[:], gm[:], AX.X, ALU.add), 2)
            v.wait_ge(mm, 2 + START)
            did(v.tensor_copy(qrow[:], pA[0:NR, 0:P]), 3)
            v.wait_ge(mm, 3 + START)
            own = pK[0:NR, 0].rearrange("p a (c k d) -> p (a c) k d", c=2, k=KV)
            did(v.tensor_scalar(tmp[:], own[:, :, 0, :], kvm[:, 0:1], None, ALU.mult), 4)
            did(v.scalar_tensor_tensor(new[:], own[:, :, 1, :], kvm[:, 1:2], tmp[:], ALU.mult, ALU.add), 5)
            did(v.tensor_tensor(tmp[:, 0:2, :], new[:].rearrange("p (a c) d -> p a c d", c=2)[:, :, 0, :], each(qrow[:], 2), ALU.mult), 6)
            did(v.tensor_reduce(snew[:], tmp[:, 0:2, :], AX.X, ALU.add), 7)
            v.wait_ge(mm, 4 + START)
            did(v.scalar_tensor_tensor(lc[:], pB[:, 0:P], SCALE, st["bias_cs"][:], ALU.mult, ALU.add), 8)
            did(v.tensor_scalar(snew[:], snew[:], SCALE, st["bias_s"][:, TP:TP + 1], ALU.mult, ALU.add), 9)
            did(v.tensor_reduce(mx[:, 2:3], lc[:], AX.X, ALU.max, negate=True), 10)
            v.wait_ge(e_done, 1 + START)
            did(v.reciprocal(sm[:, 2:3], sm[:, 2:3]), 11)
            did(v.tensor_scalar(lc[:], lc[:], sm[:, 2:3], gr[:, 0:1], ALU.mult, ALU.mult), 12)
            v.wait_ge(mm, 5 + START)
            did(v.tensor_copy(PcT[:], pA[:, 0:NR]), 13)
            n = 13
            for br in range(2):
                with v.Fori(0, NB // 2) as r:
                    for s in range(2):
                        b = 2 * r + s
                        v.wait_ge(turned, NB * br + b + 1 + START)
                        v.wait_ge(scored, (NB * br + b - 1 if s else NB * br + 2 * r) + START)
                        v.tensor_copy(KT[:, s], pK[:, s]).then_inc(kept, 1)
                v.wait_ge(scored, NB * (br + 1) + START)
                n += 1
                did(v.tensor_copy(ST[:], pS[:]), n)
                v.wait_ge(mm, 6 + 2 * br + START)
                v.tensor_copy(lg[:, br, TP:TP + 1], snew[:, br:br + 1])
                n += 1
                did(v.scalar_tensor_tensor(lg[:, br, 0:TP], pB[:, 0:TP], SCALE, st["bias_s"][:, 0:TP], ALU.mult, ALU.add), n)
                n += 1
                did(v.memset(lg[:, 1, 0:1], MASKED) if br else v.tensor_copy(tmp[:, 0, 0:1], snew[:, 0:1]), n)
                n += 1
                did(v.tensor_reduce(mx[:, br:br + 1], lg[:, br, :], AX.X, ALU.max, negate=True), n)
                v.wait_ge(e_done, 2 + br + START)
                n += 1
                did(v.reciprocal(sm[:, br:br + 1], sm[:, br:br + 1]), n)
                n += 1
                did(v.tensor_tensor(sm[:, br:br + 1], sm[:, br:br + 1], gr[:, br + 1:br + 2], ALU.mult), n)
                n += 1
                did(v.tensor_scalar(lg[:, br, :], lg[:, br, :], sm[:, br:br + 1], None, ALU.mult), n)
                n += 1
                did(v.tensor_scalar(dg[:, br, :], consts[0:NR, K_ID:K_ID + NR], lg[:, br, TP:TP + 1], None, ALU.mult), n)
                v.wait_ge(mm, 7 + 2 * br + START)
                n += 1
                did(v.tensor_copy(PT[:, br], pA[:, 0:NPAGE * NR].rearrange("p (n r) -> p n r", r=NR)), n)
            assert n == 31
            for i in range(2):
                v.wait_ge(rows_done, i + 1 + START)
                v.tensor_copy(rows_o[:, i], pR[:, i].rearrange("p b k d -> p (b k) d")).then_inc(rows_kept, 1)
            v.wait_ge(mm, 10 + START)
            v.tensor_copy(st["obT"][:, :, TP:T], pO[:, 0:NR].rearrange("p (b h) -> p h b", h=H)).then_inc(step, 1)


def merge(nc, io, st):
    with Phase(nc, "xr") as px:
        x_rows = st["oaT"][:].rearrange("p h t -> p (h t)")[:, 0:NCH * D].rearrange("p (i d) -> p i d", d=D)
        s_rows = px.sb("s_rows", [NB, D])
        x_in = px.sem("x_in")

        def load_x(sp):
            for i in range(NCH):
                sp.dma_start(x_rows[:, i, :], io["x_prompt"][0, i * P:(i + 1) * P, :]).then_inc(x_in, 16)
            sp.dma_start(s_rows[:], io["x_sample"].rearrange("b t d -> (b t) d")).then_inc(x_in, 16)

        mix(nc, io, st, load_x)
        reload_x(nc, st, x_rows, s_rows, x_in)


def mix(nc, io, st, load_x):
    ring, hT = st["ring"], st["hT"]
    with Phase(nc, "mg") as ph:
        sg = ph.sb("sg", [P, 2 * KD, T])
        pairs = [[ph.sb(f"x{n}{i}", [P, KD, T], F32R) for n in ("h", "l")] for i in range(2)]

        def gate_act(a, c, job, t, i):
            a.wait_ge(c.done, job.unit + 4 * t + i + 1 + START)
            a.activation(tile_of(sg, 4 * t + i), c.view(i % 2), ACT.Sigmoid).then_inc(c.free[i % 2], 1)

        def oa_dve(v, c, job, t, i):
            v.wait_ge(c.done, job.unit + 4 * t + i + 1 + START)
            v.tensor_tensor(tile_of(sg, 4 * t + i), c.view(i % 2), tile_of(sg, 4 * t + i), ALU.mult).then_inc(c.free[i % 2], 1)

        def ob_dve(v, c, job, t, i):
            j, m = i % 2, 4 * t + i
            v.wait_ge(c.done, job.unit + 4 * t + i + 1 + START)
            v.tensor_tensor(tile_of(hT, j), c.view(j), tile_of(sg, m + KD), ALU.mult).then_inc(c.free[j], 1)
            v.wait_ge(c.free[j], job.freed + 2 * t + i // 2 + 1 + START)
            v.tensor_tensor(tile_of(sg, m), tile_of(sg, m), tile_of(hT, j), ALU.add).then_inc(c.extra[1], 1)

        def out_act(a, c, job, t, i):
            a.wait_ge(c.done, job.unit + 4 * t + i + 1 + START)
            a.activation(tile_of(hT, 4 * t + i), c.view(i % 2), ACT.Copy).then_inc(c.free[i % 2], 1)

        Chain(nc, "mix", ring, [
            Job(columns(io["w_in"], C_M), 4, pairs[0], source=hT, act=gate_act),
            Job(columns(io["w_oa"], 0), 2, pairs[1], source=st["oaT"], dve=oa_dve),
            Job(columns(io["w_ob"], 0), 2, pairs[0], source=st["obT"], dve=ob_dve),
            Job(columns(io["w_out"], 0), 2, pairs[1], source=sg, source_steps=KD, act=out_act)],
              loaded=st["w_loaded"]["mix"], then_load=load_x)


def reload_x(nc, st, x_rows, s_rows, x_in):
    xT, ident = st["xT"], st["consts"][:, K_ID:K_ID + P]
    with Phase(nc, "x") as ph:
        ps = ph.ps("ps", [P, 8, 512])
        turned, copied = ph.sem("turned"), ph.sem("copied")
        block = ph.block()

        @block.tensor
        def _(pe):
            pe.wait_ge(x_in, 80 + START)
            for k in range(KD):
                for i in range(NCH):
                    last = pe.transpose(ps[:, k, i * P:(i + 1) * P], x_rows[:, i, k * P:(k + 1) * P], ident)
                last.then_inc(turned, 1)
            pe.wait_ge(copied, 1 + START)
            for k in range(KD):
                last = pe.transpose(ps[:, 0, k * NB:(k + 1) * NB], s_rows[:, k * P:(k + 1) * P],
                                    st["consts"][0:NB, K_ID:K_ID + NB])
            last.then_inc(turned, 1)

        @block.vector
        def _(v):
            for k in range(KD):
                v.wait_ge(turned, k + 1 + START)
                v.tensor_copy(xT[:, k, 0:TP], ps[:, k, :]).then_inc(copied, 1)
            v.wait_ge(turned, KD + 1 + START)
            v.tensor_copy(xT[:, :, TP:T], ps[:, 0, 0:KD * NB].rearrange("p (k n) -> p k n", n=NB))


def feed_forward(nc, io, st):
    ring, mod, xT, hT = st["ring"], st["mod"], st["xT"], st["hT"]

    rms_modulate(nc, "n2", hT, hT, mod[:, 2 * KD:3 * KD, :], None, st["consts"], onto=xT)
    with Phase(nc, "ff") as ph:
        gated = [ph.sb(f"gated_{n}", [P, KF, T], F32R) for n in ("high", "low")]
        with Phase(nc, "fh") as pp:
            pair = [pp.sb(n, [P, KD, T], F32R) for n in ("xh", "xl")]
            def load_gu(slot, t, b):
                return [(slot[:, 0:KD, j * P:(j + 1) * P],
                         io["w_gu"][:, bass.ds((2 * t + b) * P + j * FF, P)].rearrange("(k p) m -> p k m", p=P)) for j in range(2)]

            rms_modulate(nc, "n3", xT, hT, mod[:, 4 * KD:5 * KD, :], mod[:, 3 * KD:4 * KD, :], st["consts"], pair=pair,
                         sync=lambda sp: first_loads(sp, st, "gu", load_gu))
            sil, prod = split_halves(hT[:, 0, :]), split_halves(hT[:, 1, :])

            def gate_act(a, c, job, t, i):
                m = 2 * t + i // 2
                if i % 2 == 0:
                    a.wait_ge(c.done, 4 * t + i + 1 + START)
                    a.activation(sil, c.view(0), ACT.Silu).then_inc(c.free[0], 1)
                else:
                    a.wait_ge(c.free[1], m + 1 + START)
                    a.wait_ge(c.extra[1], m + START)
                    a.activation(tile_of(gated[0], m), prod, ACT.Copy).then_inc(c.extra[0], 1)

            def up_dve(v, c, job, t, i):
                m = 2 * t + i // 2
                if i % 2:
                    v.wait_ge(c.done, 4 * t + i + 1 + START)
                    v.wait_ge(c.free[0], m + 1 + START)
                    v.tensor_tensor(prod, c.view(1), sil, ALU.mult).then_inc(c.free[1], 1)
                    v.wait_ge(c.extra[0], m + 1 + START)
                    v.tensor_tensor(tile_of(gated[1], m), prod, tile_of(gated[0], m).bitcast(F32), ALU.subtract)\
                        .then_inc(c.extra[1], 1)

            Chain(nc, "gu", ring, [Job(load_gu, KF // 2, pair, act=gate_act, dve=up_dve)], per=2,
                  loaded=st["w_loaded"]["gu"])
        with Phase(nc, "fd") as pd:
            KH = KF // 2
            deep = pd.sb("ring", [P, 2, KH, 256])

            def load_down(slot, t, b):
                return [(slot, io["w_down"][b * KH * P:(b + 1) * KH * P, bass.ds(t * 256, 256)].rearrange(
                    "(k p) m -> p k m", p=P))]

            def down_act(a, c, job, t, i):
                if i >= 2:
                    a.wait_ge(c.done, 4 * t + i + 1 + START)
                    a.activation(tile_of(hT, 2 * t + i - 2), c.view(i % 2), ACT.Copy).then_inc(c.free[i % 2], 1)

            Chain(nc, "dw", deep, [Job(load_down, 4, gated, act=down_act, K=KH, halves=True)], K=KH)

    rms_modulate(nc, "n4", hT, hT, mod[:, 5 * KD:6 * KD, :], None, st["consts"], onto=xT)
    with Phase(nc, "y") as ph:
        rows = ph.sb("rows", [P, NCH + 1, D])
        ps = ph.ps("ps", [P, 3, 1024])
        turned, copied, stored = ph.sem("turned"), ph.sem("copied"), ph.sem("stored")
        block = ph.block()
        sizes = [P] * NCH + [NB]

        @block.tensor
        def _(pe):
            for i, n in enumerate(sizes):
                if i >= 3:
                    pe.wait_ge(copied, i - 2 + START)
                for k in range(KD):
                    last = pe.transpose(ps[0:n, i % 3, k * P:(k + 1) * P], xT[:, k, i * P:i * P + n],
                                        st["consts"][:, K_ID:K_ID + P])
                last.then_inc(turned, 1)

        @block.vector
        def _(v):
            for i, n in enumerate(sizes):
                v.wait_ge(turned, i + 1 + START)
                v.tensor_copy(rows[0:n, i, :], ps[0:n, i % 3, :]).then_inc(copied, 1)

        @block.sync
        def _(sp):
            for i in range(NCH):
                sp.wait_ge(copied, i + 1 + START)
                sp.dma_start(io["y_prompt"][0, i * P:(i + 1) * P, :], rows[:, i, :]).then_inc(stored, 16)
            sp.wait_ge(copied, NCH + 1 + START)
            sp.dma_start(io["y_sample"].rearrange("b t d -> (b t) d"), rows[0:NB, NCH, :]).then_inc(stored, 16)
            sp.wait_ge(stored, 16 * (NCH + 1) + START)


def build(nc, io):
    with ExitStack() as life, Phase(nc, "all") as ph:
        Phase.pool = Semaphores(nc, life)
        st = {
            "consts": ph.sb("consts", [P, K_COLS]), "ring": ph.sb("ring", [P, 2, KD, 256]),
            "hT": ph.sb("hT", [P, KD, T]), "cT": ph.sb("cT", [P, KD, NMOD]),
            "par": ph.sb("par", [P, 81]), "taps": ph.sb("taps", [P, CONV_W * CONV_T]),
            "stT": ph.sb("stT", [P, CONV_T, 24]), "mod": ph.sb("mod", [P, 6 * KD, NMOD]),
            "scal": ph.sb("scal", [P, 2 * H]), "g": ph.sb("g", [P, NCH + 1, H]), "beta": ph.sb("beta", [P, NCH + 1, H]),
            "gates": ph.sb("gates", [P, NCH + 1, 3 * H]), "egc": ph.sb("egc", [P, NCH, H]),
            "egl": ph.sb("egl", [P, NCH, H]), "eall": ph.sb("eall", [P, NCH, H]), "es": ph.sb("es", [P, H]),
            "tails": ph.sb("tails", [P, CONV_T, 11]), "qkv_s": ph.sb("qkv_s", [P, 3, NB, H]), "z_s": ph.sb("z_s", [P, NB, H]),
            "obT": ph.sb("obT", [P, H, T]),
        }
        st["w_loaded"] = {n: [ph.sem(f"{n}_loaded{b}") for b in range(2)] for n in ("dn", "gqkv", "mix", "gu")}
        st["xT"] = st["obT"]
        mod = st["mod"]
        with Phase(nc, "early") as pa:
            st["ada_ring"] = pa.sb("ring", [P, ADA_SLOTS, KD, 256])
            st["ada_loaded"] = [pa.sem(f"loaded{b}") for b in range(ADA_SLOTS)]
            prepare(nc, io, st)
            modulation(nc, io, st)
        rms_modulate(nc, "n1", st["hT"], st["hT"], mod[:, KD:2 * KD, :], mod[:, 0:KD, :], st["consts"])
        token_scalars(nc, io, st)
        with Phase(nc, "mixers") as pn:
            st["oaT"] = pn.sb("oaT", [P, H, T])
            deltanet(nc, io, st)
            request_delta(nc, io, st)
            with Phase(nc, "nsa") as ps:
                st.update({
                    "qT": ps.sb("qT", [P, H, T]), "rows_s": ps.sb("rows_s", [NB, 12 * P]),
                    "bias_s": ps.sb("bias_s", [NR, TP + 2]), "bias_cs": ps.sb("bias_cs", [NR, P]),
                    "kcT": ps.sb("kcT", [P, ROWS]), "vc_s": ps.sb("vc_s", [P, P]),
                })
                with Phase(nc, "nsp") as pp:
                    st.update({
                        "kvT": pp.sb("kvT", [P, 12, T]), "vtok": pp.sb("vtok", [P, NCH, 2, KV * P]),
                        "bias": pp.sb("bias", [P, H, 2 * P]), "bias_c": pp.sb("bias_c", [P, H, NCH * NBLK]),
                        "vc_p": pp.sb("vc_p", [16, P]),
                    })
                    sparse_projections(nc, io, st)
                    compress(nc, io, st)
                    prompt_attention(nc, io, st)
                request_attention(nc, io, st)
            merge(nc, io, st)
        feed_forward(nc, io, st)


_INS = ["x_prompt", "x_sample", "cache_cmp_kv", "cache_sel_kv", "cache_win_kv", "state_delta", "state_conv",
        "page_table", "c_prompt", "c_sample", "w_ada", "b_ada", "norm_g", "w_in", "conv_w", "a_log", "dt_bias",
        "onorm_g", "w_oa", "w_ob", "w_out", "cmp_pe", "cmp_w1", "cmp_w2", "rel_bias", "w_gu", "w_down"]
_OUTS = [("y_prompt", (1, TP, D)), ("y_sample", (NB, 1, D)), ("p_cmp", (1, 1, TP, 2, KV, P)),
         ("p_sel", (1, 1, TP, 2, KV, P)), ("p_win", (1, 1, TP, 2, KV, P)), ("p_delta", (1, 1, H, P, P)),
         ("p_conv", (1, 1, 3, 3 * D)), ("s_cmp", (1, NB, 1, 2, KV, P)), ("s_sel", (1, NB, 1, 2, KV, P)),
         ("s_win", (1, NB, TP, 2, KV, P)), ("s_delta", (1, NB, H, P, P)), ("s_conv", (1, NB, 3, 3 * D))]


def _tables():
    import numpy as np

    c = np.zeros((P, K_COLS), np.float32)
    r, q = np.arange(P)[:, None], np.arange(P)[None, :]
    c[:, K_ID:K_ID + P] = r == q
    c[:, K_LE:K_LE + P] = r <= q
    c[:, K_GT:K_GT + P] = r > q
    c[:, K_LT:K_LT + P] = r < q

    def pairs(s):
        return (r // (2 * s) == q // (2 * s)) & (r // s % 2 == 0) & (q // s % 2 == 1)

    c[:, K_NEG1:K_NEG1 + P] = -1.0 * pairs(1)
    for i, s in enumerate(LEVELS):
        c[:, K_LEV + i * P:K_LEV + (i + 1) * P] = pairs(s)
    c[:, K_ONE:K_ONE + P] = 1.0
    rows = np.arange(NR)
    c[0:NB, K_E8:K_E8 + NR] = np.arange(NB)[:, None] == rows[None, :] // H
    c[0:NR, K_HM:K_HM + H] = rows[:, None] % H == np.arange(H)[None, :]
    c[0:NR, K_KVM:K_KVM + KV] = rows[:, None] % H // G == np.arange(KV)[None, :]
    keys = np.arange(P)
    same = (keys[None, :] // 16 == rows[:, None] // H) & (keys[None, :] % 16 // 8 == rows[:, None] % H // G)
    c[0:NR, K_X:K_X + P] = np.where(same, 0.0, MASKED)
    c[:, K_RV] = np.arange(P) >= BLK - 1

    c[:, K_MH] = -0.5
    c[:, K_J:K_J + P] = r == P - 1 - q
    def bucket(dist):
        n = np.maximum(dist, 0)
        big = 16 + (np.log(np.maximum(n, 1).astype(np.float32) / np.float32(16))
                    / np.float32(np.log(8.0)) * np.float32(16)).astype(np.int32)
        return np.where(n < 16, n, np.minimum(big, 31))

    o = np.zeros((NBK, B_COLS), np.float32)

    def put(at, dist):
        dist = dist.reshape(-1)
        row = np.where(dist >= 0, bucket(dist), NBK - 1)
        o[row, at + np.arange(dist.size)] = 1.0

    put(B_R, 255 - np.arange(B_S))
    put(B_S, TP - np.arange(TP + 1))
    i, n, t = np.meshgrid(np.arange(NCH), np.arange(NBLK), np.arange(P), indexing="ij")
    put(B_CP, i * P + t - (n * BLK + BLK - 1))
    put(B_CS, TP - (keys % 8 * BLK + BLK - 1))
    return c, o


def kernel(**inputs):
    import numpy as _np
    import concourse.bacc as _bacc
    from concourse import mybir as _mybir
    from concourse.bass_utils import run_bass_kernel_spmd as _run

    nc = _bacc.Bacc("TRN2", target_bir_lowering=False, num_devices=1)
    arrays, io = {}, {}
    squeeze = {"w_ada", "w_in", "w_oa", "w_ob", "w_out", "w_gu", "w_down"}
    for name in _INS:
        a = _np.ascontiguousarray(inputs[name])
        if name in squeeze:
            a = a[0]
        arrays[f"in_{name}"] = a
        io[name] = nc.dram_tensor(f"in_{name}", a.shape, _mybir.dt.from_np(a.dtype), kind="ExternalInput").ap()
    for name, a in zip(("consts", "buckets"), _tables()):
        arrays[f"in_{name}"] = a
        io[name] = nc.dram_tensor(f"in_{name}", a.shape, _mybir.dt.float32, kind="ExternalInput").ap()
    for name, shape in _OUTS:
        io[name] = nc.dram_tensor(f"out_{name}", shape, _mybir.dt.float32, kind="ExternalOutput").ap()
    build(nc, io)
    r = _run(nc, [arrays], core_ids=[0])
    return tuple(r.results[0][f"out_{name}"] for name, _ in _OUTS)
```
